# Optimizing a Trainium2 kernel written in Bass

```python
import jax, jax.numpy as jnp
from jax import lax
import numpy as np

D_MODEL = 1024
BATCH = 1
SEQ = 512
DEPTH = 2

GRID_W = 64
CTX_LEN = 256
N_MIXERS = 2
N_HEADS = 16
QK_NOPE_DIM = 64
QK_ROPE_DIM = 32
V_HEAD_DIM = 64
Q_LORA_RANK = 512
KV_LORA_RANK = 256
ROPE_THETA = 10000.0
Q_BLOCK = 128
CONV_WIDTH = 31
N_EXPERTS = 64
TOP_K = 6
N_GROUPS = 8
TOPK_GROUPS = 4
EXPERT_DIM = 256
SHARED_DIM = 256
ROUTED_SCALE = 2.5
EXPERT_BLOCK = 128
NORM_EPS = 1e-6

kernel_name = "hybrid_mla_conformer_moe_dit"

def rmsnorm(x, w):
    x32 = x.astype(jnp.float32)
    y = x32 * lax.rsqrt(jnp.mean(x32 * x32, axis=-1, keepdims=True) + NORM_EPS)
    return (y * w.astype(jnp.float32)).astype(x.dtype)

def layernorm(x, w, b):
    x32 = x.astype(jnp.float32)
    mu = jnp.mean(x32, axis=-1, keepdims=True)
    var = jnp.mean(jnp.square(x32 - mu), axis=-1, keepdims=True)
    y = (x32 - mu) * lax.rsqrt(var + NORM_EPS)
    return (y * w.astype(jnp.float32) + b.astype(jnp.float32)).astype(x.dtype)

def modulate(h, shift, scale):
    return h * (1 + scale) + shift

def axial_rope_tables(n_tokens, dtype):
    rows = n_tokens // GRID_W
    row = jnp.repeat(jnp.arange(rows, dtype=jnp.float32), GRID_W)
    col = jnp.tile(jnp.arange(GRID_W, dtype=jnp.float32), rows)
    axis_dim = QK_ROPE_DIM // 2
    inv_freq = ROPE_THETA ** (-jnp.arange(0, axis_dim, 2, dtype=jnp.float32) / axis_dim)
    ang_r = row[:, None] * inv_freq
    ang_c = col[:, None] * inv_freq
    ang = jnp.concatenate([ang_r, ang_r, ang_c, ang_c], axis=-1)
    return jnp.cos(ang).astype(dtype), jnp.sin(ang).astype(dtype)

def _rotate_half(v):
    v1, v2 = jnp.split(v, 2, axis=-1)
    return jnp.concatenate([-v2, v1], axis=-1)

def apply_axial_rope(v, cos, sin):
    half = QK_ROPE_DIM // 2
    rot = jnp.concatenate([_rotate_half(v[..., :half]), _rotate_half(v[..., half:])], axis=-1)
    return v * cos + rot * sin

def mla_queries(h, wq_a, q_norm, wq_b, rope):
    B, L, _ = h.shape
    q = (rmsnorm(h @ wq_a, q_norm) @ wq_b).reshape(B, L, N_HEADS, QK_NOPE_DIM + QK_ROPE_DIM)
    if rope is not None:
        cos, sin = rope
        q_pe = apply_axial_rope(q[..., QK_NOPE_DIM:], cos[:, None, :], sin[:, None, :])
        q = jnp.concatenate([q[..., :QK_NOPE_DIM], q_pe], axis=-1)
    return q

def mla_keys_values(h, wkv_a, kv_norm, wkv_b, rope):
    B, L, _ = h.shape
    kv_a = h @ wkv_a
    c_kv, k_pe = kv_a[..., :KV_LORA_RANK], kv_a[..., KV_LORA_RANK:]
    if rope is not None:
        cos, sin = rope
        k_pe = apply_axial_rope(k_pe, cos, sin)
    kv = (rmsnorm(c_kv, kv_norm) @ wkv_b).reshape(B, L, N_HEADS, QK_NOPE_DIM + V_HEAD_DIM)
    k_nope, v = kv[..., :QK_NOPE_DIM], kv[..., QK_NOPE_DIM:]
    k_pe = jnp.broadcast_to(k_pe[:, :, None, :], (B, L, N_HEADS, QK_ROPE_DIM))
    return jnp.concatenate([k_nope, k_pe], axis=-1), v

def attend(q, k, v):
    scale = (QK_NOPE_DIM + QK_ROPE_DIM) ** -0.5
    s = jnp.einsum('bqhd,bkhd->bhqk', q, k) * scale
    p = jax.nn.softmax(s.astype(jnp.float32), axis=-1).astype(v.dtype)
    return jnp.einsum('bhqk,bkhd->bqhd', p, v)

def blocked_attend(q, k, v):
    B, L, H, dq = q.shape
    nb = L // Q_BLOCK
    qb = q.reshape(B, nb, Q_BLOCK, H, dq).transpose(1, 0, 2, 3, 4)
    ob = lax.map(lambda qq: attend(qq, k, v), qb)
    return ob.transpose(1, 0, 2, 3, 4).reshape(B, L, H * V_HEAD_DIM)

def conv_module(h, pw1_w, pw1_b, dw_w, dw_b, n_w, n_b, pw2_w, pw2_b):
    u = h @ pw1_w + pw1_b
    a, g = jnp.split(u, 2, axis=-1)
    u = a * jax.nn.sigmoid(g)
    pad = CONV_WIDTH // 2
    u = lax.conv_general_dilated(u, dw_w[:, None, :], window_strides=(1,), padding=[(pad, pad)],
                                 dimension_numbers=('NWC', 'WIO', 'NWC'),
                                 feature_group_count=u.shape[-1]) + dw_b
    u = jax.nn.silu(layernorm(u, n_w, n_b))
    return u @ pw2_w + pw2_b

def swiglu(x, w1, w3, w2):
    return (jax.nn.silu(x @ w1) * (x @ w3)) @ w2

def moe_ffn(xs, router_w, router_bias, exp_w1, exp_w3, exp_w2, sh_w1, sh_w3, sh_w2):
    T, D = xs.shape
    scores = jax.nn.sigmoid((xs @ router_w).astype(jnp.float32))
    sel = scores + router_bias.astype(jnp.float32)
    per_group = N_EXPERTS // N_GROUPS
    group_scores = lax.top_k(sel.reshape(T, N_GROUPS, per_group), 2)[0].sum(-1)
    gidx = lax.top_k(group_scores, TOPK_GROUPS)[1]
    gmask = jax.nn.one_hot(gidx, N_GROUPS, dtype=jnp.float32).sum(1) > 0
    emask = jnp.repeat(gmask, per_group, axis=1)
    _, idx = lax.top_k(jnp.where(emask, sel, -jnp.inf), TOP_K)
    w = jnp.take_along_axis(scores, idx, axis=1)
    w = (w / jnp.sum(w, axis=-1, keepdims=True) * ROUTED_SCALE).astype(xs.dtype)

    TK = T * TOP_K
    flat_e = idx.reshape(-1)
    flat_tok = jnp.broadcast_to(jnp.arange(T, dtype=jnp.int32)[:, None], (T, TOP_K)).reshape(-1)
    flat_w = w.reshape(-1)
    order = jnp.argsort(flat_e, stable=True)
    sorted_e = flat_e[order]
    counts = jnp.zeros((N_EXPERTS,), jnp.int32).at[flat_e].add(1)
    padded = (counts + EXPERT_BLOCK - 1) // EXPERT_BLOCK * EXPERT_BLOCK
    pad_end = jnp.cumsum(padded)
    pad_start = pad_end - padded
    sort_start = jnp.cumsum(counts) - counts
    rank = jnp.arange(TK, dtype=jnp.int32) - sort_start[sorted_e]
    dest = pad_start[sorted_e] + rank
    n_blocks = (TK + EXPERT_BLOCK - 1) // EXPERT_BLOCK + N_EXPERTS
    P = n_blocks * EXPERT_BLOCK
    slot_tok = jnp.full((P,), T, jnp.int32).at[dest].set(flat_tok[order])
    slot_w = jnp.zeros((P,), xs.dtype).at[dest].set(flat_w[order])
    blk_e = jnp.minimum(jnp.searchsorted(pad_end, jnp.arange(n_blocks, dtype=jnp.int32) * EXPERT_BLOCK,
                                         side='right'), N_EXPERTS - 1)
    xs_pad = jnp.concatenate([xs, jnp.zeros((1, D), xs.dtype)], axis=0)
    xg = xs_pad[slot_tok].reshape(n_blocks, EXPERT_BLOCK, D)

    def expert_block(args):
        xb, e = args
        return swiglu(xb, exp_w1[e], exp_w3[e], exp_w2[e])

    yg = lax.map(expert_block, (xg, blk_e)).reshape(P, D) * slot_w[:, None]
    routed = jax.ops.segment_sum(yg, slot_tok, num_segments=T + 1)[:T]
    return routed + swiglu(xs, sh_w1, sh_w3, sh_w2)

def setup_inputs(seed: int = 0) -> dict:
    key = jax.random.key(seed)
    ks = iter(jax.random.split(key, 40))
    f32 = jnp.float32
    D = D_MODEL
    n_mla = (DEPTH + N_MIXERS - 1) // N_MIXERS
    n_conv = DEPTH // N_MIXERS

    def nrm(shape, scale):
        return jax.random.normal(next(ks), shape, f32) * scale

    def gain(shape):
        return 1.0 + nrm(shape, 0.1)

    return {
        "x": nrm((BATCH, SEQ, D), 1.0),
        "c": nrm((BATCH, D), 1.0),
        "ctx": nrm((BATCH, CTX_LEN, D), 1.0),
        "c_ctx": nrm((D,), 1.0),
        "mod_w": nrm((DEPTH, D, 6 * D), 0.5 * D ** -0.5),
        "mod_b": nrm((DEPTH, 6 * D), 0.02),
        "norm_mix_w": gain((DEPTH, D)),
        "norm_ffn_w": gain((DEPTH, D)),
        "mla_wq_a": nrm((n_mla, D, Q_LORA_RANK), D ** -0.5),
        "mla_q_norm": gain((n_mla, Q_LORA_RANK)),
        "mla_wq_b": nrm((n_mla, Q_LORA_RANK, N_HEADS * (QK_NOPE_DIM + QK_ROPE_DIM)), Q_LORA_RANK ** -0.5),
        "mla_wkv_a": nrm((n_mla, D, KV_LORA_RANK + QK_ROPE_DIM), D ** -0.5),
        "mla_kv_norm": gain((n_mla, KV_LORA_RANK)),
        "mla_wkv_b": nrm((n_mla, KV_LORA_RANK, N_HEADS * (QK_NOPE_DIM + V_HEAD_DIM)), KV_LORA_RANK ** -0.5),
        "mla_wo": nrm((n_mla, N_HEADS * V_HEAD_DIM, D), (N_HEADS * V_HEAD_DIM) ** -0.5),
        "conv_pw1_w": nrm((n_conv, D, 2 * D), D ** -0.5),
        "conv_pw1_b": nrm((n_conv, 2 * D), 0.02),
        "conv_dw_w": nrm((n_conv, CONV_WIDTH, D), CONV_WIDTH ** -0.5),
        "conv_dw_b": nrm((n_conv, D), 0.02),
        "conv_norm_w": gain((n_conv, D)),
        "conv_norm_b": nrm((n_conv, D), 0.02),
        "conv_pw2_w": nrm((n_conv, D, D), D ** -0.5),
        "conv_pw2_b": nrm((n_conv, D), 0.02),
        "router_w": nrm((DEPTH, D, N_EXPERTS), D ** -0.5),
        "router_bias": nrm((DEPTH, N_EXPERTS), 0.01),
        "exp_w1": nrm((DEPTH, N_EXPERTS, D, EXPERT_DIM), D ** -0.5),
        "exp_w3": nrm((DEPTH, N_EXPERTS, D, EXPERT_DIM), D ** -0.5),
        "exp_w2": nrm((DEPTH, N_EXPERTS, EXPERT_DIM, D), EXPERT_DIM ** -0.5),
        "shared_w1": nrm((DEPTH, D, SHARED_DIM), D ** -0.5),
        "shared_w3": nrm((DEPTH, D, SHARED_DIM), D ** -0.5),
        "shared_w2": nrm((DEPTH, SHARED_DIM, D), SHARED_DIM ** -0.5),
        "final_norm_w": gain((D,)),
    }

def reference(x, c, ctx, c_ctx, mod_w, mod_b, norm_mix_w, norm_ffn_w,
              mla_wq_a, mla_q_norm, mla_wq_b, mla_wkv_a, mla_kv_norm, mla_wkv_b, mla_wo,
              conv_pw1_w, conv_pw1_b, conv_dw_w, conv_dw_b, conv_norm_w, conv_norm_b,
              conv_pw2_w, conv_pw2_b,
              router_w, router_bias, exp_w1, exp_w3, exp_w2, shared_w1, shared_w3, shared_w2,
              final_norm_w):
    B, L, D = x.shape
    C = ctx.shape[1]
    rope = axial_rope_tables(L, x.dtype)
    xs, cs = x, ctx
    for i in range(DEPTH):
        last = i == DEPTH - 1
        j = i // N_MIXERS
        is_mla = i % N_MIXERS == 0
        mx = jax.nn.silu(c) @ mod_w[i] + mod_b[i]
        sh1x, sc1x, g1x, sh2x, sc2x, g2x = [t[:, None, :] for t in jnp.split(mx, 6, axis=-1)]
        hx = modulate(rmsnorm(xs, norm_mix_w[i]), sh1x, sc1x)
        need_ctx = is_mla or not last
        if need_ctx:
            mc = jax.nn.silu(c_ctx) @ mod_w[i] + mod_b[i]
            sh1c, sc1c, g1c, sh2c, sc2c, g2c = jnp.split(mc, 6, axis=-1)
            hc = modulate(rmsnorm(cs, norm_mix_w[i]), sh1c, sc1c)

        if is_mla:
            k_c, v_c = mla_keys_values(hc, mla_wkv_a[j], mla_kv_norm[j], mla_wkv_b[j], None)
            k_x, v_x = mla_keys_values(hx, mla_wkv_a[j], mla_kv_norm[j], mla_wkv_b[j], rope)
            q_x = mla_queries(hx, mla_wq_a[j], mla_q_norm[j], mla_wq_b[j], rope)
            keys = jnp.concatenate([k_c, k_x], axis=1)
            vals = jnp.concatenate([v_c, v_x], axis=1)
            out_x = blocked_attend(q_x, keys, vals) @ mla_wo[j]
            if not last:
                q_c = mla_queries(hc, mla_wq_a[j], mla_q_norm[j], mla_wq_b[j], None)
                out_c = attend(q_c, k_c, v_c).reshape(B, C, N_HEADS * V_HEAD_DIM) @ mla_wo[j]
        else:
            conv_args = (conv_pw1_w[j], conv_pw1_b[j], conv_dw_w[j], conv_dw_b[j],
                         conv_norm_w[j], conv_norm_b[j], conv_pw2_w[j], conv_pw2_b[j])
            out_x = conv_module(hx, *conv_args)
            if not last:
                out_c = conv_module(hc, *conv_args)
        xs = xs + g1x * out_x

        moe_args = (router_w[i], router_bias[i], exp_w1[i], exp_w3[i], exp_w2[i],
                    shared_w1[i], shared_w3[i], shared_w2[i])
        h2x = modulate(rmsnorm(xs, norm_ffn_w[i]), sh2x, sc2x)
        if last:
            xs = xs + g2x * moe_ffn(h2x.reshape(B * L, D), *moe_args).reshape(B, L, D)
        else:
            cs = cs + g1c * out_c
            h2c = modulate(rmsnorm(cs, norm_ffn_w[i]), sh2c, sc2c)
            tokens = jnp.concatenate([h2x.reshape(B * L, D), h2c.reshape(B * C, D)], axis=0)
            y = moe_ffn(tokens, *moe_args)
            xs = xs + g2x * y[:B * L].reshape(B, L, D)
            cs = cs + g2c * y[B * L:].reshape(B, C, D)
    return rmsnorm(xs, final_norm_w)


_drawn_inputs = setup_inputs


def setup_inputs(seed=0):
    import zlib

    import numpy as np

    out = dict(_drawn_inputs(seed))
    spreads = {}
    factors = {'conv_pw1_b': 4.622, 'conv_dw_b': 3.816, 'conv_norm_b': 4.478, 'conv_pw2_b': 3.299}
    for name, (base, spread) in spreads.items():
        noise = np.random.default_rng([zlib.crc32(name.encode()), seed]).standard_normal(out[name].shape)
        drawn = base * np.exp(spread * noise) if base else spread * noise
        out[name] = __import__('jax').numpy.asarray(drawn.astype(out[name].dtype))
    for name, factor in factors.items():
        out[name] = (out[name] * factor).astype(out[name].dtype)
    return out
```

```python
import concourse.bass as bass
from concourse import mybir
import numpy as np
from contextlib import ExitStack

D = 1024
T = 512
C = 256
H = 16
NOPE, ROPE, VD = 64, 32, 64
QL, KVL = 512, 256
E = 64
K = 6
G = 8
TOPG = 4
F = 256
TAPS = 31
PAD = TAPS // 2
DC = D // 128
TT = T // 128
KEYS = C + T
EPS = 1e-6
SM_SCALE = float(NOPE + ROPE) ** -0.5
ROUTED = 2.5
CAP = T
BLOCKS = CAP // 128
XMAX = T * K // 128
ROWS = 128 * (E + XMAX)
NONE = 1 << 20
PE_TAPS = 6

VEC = {}
_at = 0
for _n, _w in (("c", 2 * DC), ("modb", 96), ("nmix", 2 * DC), ("nffn", 2 * DC), ("qn", QL // 128),
               ("kvn", KVL // 128), ("pw1b", 2 * DC), ("dwb", DC), ("lnw", DC), ("lnb", DC), ("pw2b", DC),
               ("fin", DC), ("dww", DC * TAPS)):
    VEC[_n] = (_at, _at + _w)
    _at += _w
NVEC = _at
CST = {}
_at = 0
for _n, _w in (("ident", 128), ("sel", 2), ("iota", E), ("before", G * G), ("upper", 128), ("upto", E),
               ("tok", TT), ("rope", T)):
    CST[_n] = (_at, _at + _w)
    _at += _w
NCST = _at


def build(nc, xT_d, ctxT_d, vec_d, cst_d, mod_w, wq_a, wq_b, wkv_a, wkv_b, wo, pw1, pw2,
          router_w, router_bias, exp_w1, exp_w3, exp_w2, sh_w1, sh_w3, sh_w2, out):
    f32, bf16, i32, u32 = mybir.dt.float32, mybir.dt.bfloat16, mybir.dt.int32, mybir.dt.uint32
    ALU, ACT, AX = mybir.AluOpType, mybir.ActivationFunctionType, mybir.AxisListType
    ds = bass.ds
    L = 2

    h_rows = [nc.dram_tensor(f"h_rows{i}", (T, D), f32, kind="Internal").ap() for i in range(L)]
    y_rows = nc.dram_tensor("y_rows", (ROWS, D), f32, kind="Internal").ap()
    slots = [nc.dram_tensor(f"slots{i}", (ROWS, 1), i32, kind="Internal").ap() for i in range(L)]

    ctx = ExitStack()
    with ctx:
        def sb(name, shape, dt=f32):
            return ctx.enter_context(nc.sbuf_tensor(name, shape, dt))

        def sem(name):
            return ctx.enter_context(nc.semaphore(name))

        PS = ctx.enter_context(nc.psum_tensor("PS", [128, 8 * 512], f32))

        def bank(b, n=1):
            return PS[:, b * 512:(b + n) * 512]

        vec = sb("vec", [128, NVEC])
        cst = sb("cst", [128, NCST])
        xT = sb("xT", [128, DC, T])
        hT = sb("hT", [128, DC * KEYS])
        RING = 4
        SLOT = 3 * DC * F
        ring = sb("ring", [128, RING * SLOT])
        work = sb("work", [128, 12800])
        sq = sb("sq", [128, 2, T])
        rs = sb("rs", [128, T])
        small = sb("small", [128, 480])
        mean_w = sb("mean_w", [128, 128])
        upper_b = sb("upper_b", [128, 128], bf16)
        upto_b = sb("upto_b", [E, E], bf16)
        ones_b = sb("ones_b", [128, 128], bf16)
        chosen_b = sb("chosen_b", [128, TT * E], bf16)
        extra_b = sb("extra_b", [E, 128], bf16)
        zrow = sb("zrow", [128, 512])
        passed_b = sb("passed_b", [E, XMAX], bf16)
        tok_i = sb("tok_i", [128, TT], i32)
        idx = sb("idx", [128, E + XMAX], i32)
        col_i = sb("col_i", [128, 2], i32)
        row_i = sb("row_i", [128, K * TT], i32)
        unit_i = sb("unit_i", [1, XMAX + 1], i32)
        cs = sb("cs", [128, DC, 32])
        mod = [sb(f"mod{i}", [128, 6, DC, 2]) for i in range(L)]
        modA = [sb(f"modA{i}", [128, 2, DC, 2]) for i in range(L)]
        smx = sb("smx", [128, 4, 3])
        zero = sb("zero", [128, 1])
        tick = sb("tick", [1, 16])
        eps = sb("eps", [128, 1])

        def v(name, a=0, b=None):
            lo, hi = VEC[name]
            return vec[:, lo + a:(lo + b if b is not None else hi)]

        def k(name, a=0, b=None):
            lo, hi = CST[name]
            return cst[:, lo + a:(lo + b if b is not None else hi)]

        ident = k("ident")

        MODBUF = 4
        mw = [ring[:, n * DC * 512:(n + 1) * DC * 512].rearrange("p (c f) -> p c f", c=DC) for n in range(MODBUF)]
        mrow = [work[:, n * 512:(n + 1) * 512] for n in range(2)]
        AW = 2 * 8192
        wqa_sb = ring[:, AW:AW + DC * QL].rearrange("p (c f) -> p c f", c=DC)
        KVW = KVL + 2 * ROPE
        wkva_sb = ring[:, AW + DC * QL:AW + DC * QL + DC * KVW].rearrange("p (c f) -> p c f", c=DC)
        wo_sb = ring[:, AW:AW + DC * D].rearrange("p (c f) -> p c f", c=DC)
        wqb_sb = ring[:, 0:8192].rearrange("p (c h f) -> p c h f", c=QL // 128, h=H)
        wkvb_sb = ring[:, 8192:12288].rearrange("p (c h f) -> p c h f", c=KVL // 128, h=H)
        P = [ring[:, 12288 + n * KEYS:12288 + (n + 1) * KEYS] for n in range(2)]
        rope_t = [ring[:, 13824 + n * 512:13824 + (n + 1) * 512] for n in range(2)]
        ctxT = work[:, 1024:1024 + DC * C].rearrange("p (c t) -> p c t", c=DC)
        o = [0]

        def take(n):
            o[0] += n
            return work[:, o[0] - n:o[0]]

        pT = take(2 * 6 * T).rearrange("p (h j t) -> p h j t", h=2, j=6)
        ckv = take(2 * KEYS).rearrange("p (c t) -> p c t", c=2)
        qa = take(4 * T).rearrange("p (c t) -> p c t", c=4)
        kT = [[take(KEYS) for _ in range(2)] for _ in range(2)]
        vv = [ring[:, 14848 + n * 768:14848 + (n + 1) * 768].rearrange("p (j f) -> p j f", j=6) for n in range(2)]
        hA = hT[:, :].rearrange("p (c t) -> p c t", c=DC)
        oT = hT[:, 0:DC * T].rearrange("p (c t) -> p c t", c=DC)
        qT = [[hT[:, DC * T + (2 * a + b) * T:DC * T + (2 * a + b + 1) * T] for b in range(2)] for a in range(2)]
        assert o[0] <= 12800
        hM = hT[:, 0:DC * T].rearrange("p (c t) -> p c t", c=DC)

        o[0] = 0
        acc = take(TT * D).rearrange("p (t d) -> p t d", t=TT)
        xg = [take(D) for _ in range(2)]
        both = take(2 * D)
        xgT = [both[:, n * D:(n + 1) * D].rearrange("p (c t) -> p c t", c=DC) for n in range(2)]
        yb = [take(D) for _ in range(2)]
        gate = [take(F) for _ in range(2)]
        act = [take(F) for _ in range(2)]
        actT = [take(F).rearrange("p (k t) -> p k t", k=2) for _ in range(2)]
        hot = both[:, 0:K * TT * E]
        prod = work[:, 0:K * TT * E]
        comb = xg + [both[:, 0:D], both[:, D:2 * D]] + yb
        o2 = [0]

        def few(n):
            o2[0] += n
            return small[:, o2[0] - n:o2[0]]

        score = take(TT * E)
        select = take(TT * E)
        gtop = take(TT * G * 8)
        cmpa = take(TT * G * G)
        assert o[0] <= 12800
        gsum = few(TT * G)
        cmpb = few(TT * G * G)
        rank = few(TT * G)
        top = few(TT * 8)
        topi = few(TT * 8)
        wk = few(K * TT)
        wsum = few(TT)
        nbx = few(4)
        xrow = few(E)
        assert o2[0] <= 480
        topu = sb("topu", [128, TT * 8], u32)
        bias_sb = sb("bias_sb", [128, E])
        rw_sb = hT[:, DC * T:DC * T + DC * E].rearrange("p (c e) -> p c e", c=DC)

        def w13(s):
            return ring[:, s * SLOT:s * SLOT + 2 * DC * F].rearrange("p (a c f) -> p a c f", a=2, c=DC)

        def w2(s):
            return ring[:, s * SLOT + 2 * DC * F:(s + 1) * SLOT].rearrange("p (k d) -> p k d", k=2)

        pw1_sb = ring[:, 0:DC * 2 * D].rearrange("p (c f) -> p c f", c=DC)
        pw2_sb = ring[:, DC * 2 * D:DC * 3 * D].rearrange("p (c f) -> p c f", c=DC)
        PT_ = T + 2 * PAD
        up = [work[:, n * PT_:(n + 1) * PT_] for n in range(2)]
        CU = 2 * PT_
        conv = work[:, CU:CU + DC * T].rearrange("p (c t) -> p c t", c=DC)
        diag = [work[:, CU + DC * T + n * 128:CU + DC * T + (n + 1) * 128] for n in range(2 * PE_TAPS)]
        sg = [work[:, CU + DC * T + 2 * PE_TAPS * 128 + n * T:][:, 0:T] for n in range(2)]
        tmp = [work[:, CU + DC * T + 2 * PE_TAPS * 128 + (2 + n) * T:][:, 0:T] for n in range(2)]
        oF = conv

        cst_in, x_in, pool_cst, dve_cst, cs_rdy = (sem(n) for n in ("cst_in", "x_in", "pool_cst", "dve_cst", "cs_rdy"))
        modw_in = [sem(f"modw_in{n}") for n in range(MODBUF)]
        modrow_ps, modrow_sb, modcol_ps, mod_rdy = sem("modrow_ps"), sem("modrow_sb"), sem("modcol_ps"), sem("mod_rdy")
        sq_rdy, sq_used, rs_rdy, nrm_mul, nrm_out = (sem(n) for n in ("sq_rdy", "sq_used", "rs_rdy", "nrm_mul", "nrm_out"))
        aw_in, bw_in, wo_in = sem("aw_in"), sem("bw_in"), sem("wo_in")
        a_ps, a_ev, a_pe = sem("a_ps"), sem("a_ev"), sem("a_pe")
        lsq_rdy, lsq_used, lrs_rdy, lat_rdy = (sem(n) for n in ("lsq_rdy", "lsq_used", "lrs_rdy", "lat_rdy"))
        pj_ps, kv_ev, q_ev, q_rope = sem("pj_ps"), sem("kv_ev"), sem("q_ev"), sem("q_rope")
        s_ps, max_rdy, nmax_rdy, exp_rdy, p_rdy, pT_ps, pT_act, pT_dve, o_ps, o_ev = (
            sem(n) for n in ("s_ps", "max_rdy", "nmax_rdy", "exp_rdy", "p_rdy", "pT_ps", "pT_act", "pT_dve", "o_ps", "o_ev"))
        wo_ps, wo_ev = sem("wo_ps"), sem("wo_ev")
        std_rdy, lstd_rdy = sem("std_rdy"), sem("lstd_rdy")
        zero_out = sem("zero_out")
        den_rdy, dve_step = sem("den_rdy"), sem("dve_step")
        pw_in, glu_ps, sig_rdy, u_rdy, diag_rdy, tap_ps, cv_rdy, mean_ps, cent_rdy, pw2_ps, pw2_ev, pad_rdy = (
            sem(n) for n in ("pw_in", "glu_ps", "sig_rdy", "u_rdy", "diag_rdy", "tap_ps", "cv_rdy", "mean_ps",
                             "cent_rdy", "pw2_ps", "pw2_ev", "pad_rdy"))
        out_dn = sem("out_dn")

        (rw_in, logit_ps, score_rdy, chosen_rdy, pos_ps, rows_rdy, none_rdy, none_set, slots_set,
         idx_in, cnt_ps, nbx_rdy, end_ps, passed_rdy, unit_ps, unit_rdy, sh_in, xg_clr) = (
            sem(n) for n in ("rw_in", "logit_ps", "score_rdy", "chosen_rdy", "pos_ps", "rows_rdy", "none_rdy", "none_set", "slots_set",
                             "idx_in", "cnt_ps", "nbx_rdy", "end_ps", "passed_rdy", "unit_ps", "unit_rdy", "sh_in", "xg_clr"))

        hd_out = [sem(f"hd_out{s}") for s in range(2)]
        comb_in = [sem(f"comb_in{s}") for s in range(6)]

        hrow_ps, hrow_sb, comb_used, acc_ps, res_ev = (sem(n) for n in ("hrow_ps", "hrow_sb", "comb_used", "acc_ps", "res_ev"))

        M = []
        for i in range(L):
            m = {n: sem(f"{n}{i}") for n in (
                
                "up_ps",
                "gate_rdy", "act_rdy", "actT_ps", "actT_ev", "dn_ps", "y_ev", "xgT_ps", "xgT_ev", "t_w", "t_xg", "t_idx",
                "t_xgT_ps", "t_xgT_ev", "t_up", "t_gate", "t_act", "t_actT_ps", "t_actT_ev", "t_dn", "t_yev", "t_yout", "t_tick",
                "col_rdy")}
            m["w_in"] = [sem(f"w_in{i}_{s}") for s in range(RING)]
            m["xg_in"] = [sem(f"xg_in{i}_{s}") for s in range(2)]
            m["y_out"] = [sem(f"y_out{i}_{s}") for s in range(2)]
            M.append(m)

        def jobs():
            a = lambda i, n, c, w: modA[i][:, n, c, w:w + 1]
            b = lambda i, n, c, w: mod[i][:, 3 * n, c, w:w + 1]
            xs = lambda c: xT[:, c, :]
            return [
                (lambda c: ctxT[:, c, :], lambda c: hA[:, c, 0:C], C, lambda c: a(0, 0, c, 1), lambda c: b(0, 0, c, 1), ACT.Identity),
                (xs, lambda c: hA[:, c, C:KEYS], T, lambda c: a(0, 0, c, 0), lambda c: b(0, 0, c, 0), ACT.Identity),
                (xs, lambda c: hM[:, c, :], T, lambda c: a(0, 1, c, 0), lambda c: b(0, 1, c, 0), ACT.Identity),
                (xs, lambda c: hM[:, c, :], T, lambda c: a(1, 0, c, 0), lambda c: b(1, 0, c, 0), ACT.Identity),
                (lambda c: conv[:, c, :], lambda c: hM[:, c, :], T, lambda c: v("lnw", c, c + 1), lambda c: v("lnb", c, c + 1), ACT.Silu),
                (xs, lambda c: hM[:, c, :], T, lambda c: a(1, 1, c, 0), lambda c: b(1, 1, c, 0), ACT.Identity),
                (xs, lambda c: oF[:, c, :], T, lambda c: v("fin", c, c + 1), lambda c: zero[:, 0:1], ACT.Identity),
            ]

        JOBS = jobs()
        J_CTX, J_X, J_FFN0, J_MIX1, J_LN, J_FFN1, J_FIN = range(7)
        NB = 3

        AG = [("kv", 0, C, 0), ("kv", 0, C, 1), ("pe", 0, C, 2), ("kv", C, T, 0), ("kv", C, T, 1), ("pe", C, T, 2)] + \
             [("q", C, T, m) for m in range(QL // 128)]
        LAT = [(1, C, [0, 1], lambda j: ckv[:, j, 0:C], "kvn"), (2, T, [3, 4], lambda j: ckv[:, j, C:KEYS], "kvn"),
               (0, T, [6, 7, 8, 9], lambda j: qa[:, j, :], "qn")]
        LSQ = [g for _, _, gs, _, _ in LAT for g in gs]
        NPAIR = H // 2
        NS = H * TT

        def up_view(c):
            return up[c % 2]

        def pT_copy(eng, op, n, scalar):
            m, q, t = n // 8, (n // TT) % 2, n % TT
            eng.wait_ge(pT_ps, n + 1)
            if m:
                eng.wait_ge(o_ps, m)
            j0, j1 = (0, 4) if scalar else (4, 6)
            dst = pT[:, q, j0:j1, t * 128:(t + 1) * 128]
            src = bank(4, 2)[:, j0 * 128:j1 * 128].rearrange("p (j f) -> p j f", j=j1 - j0)
            if scalar:
                op(dst, src, ACT.Copy).then_inc(pT_act, 1)
            else:
                op(dst, src).then_inc(pT_dve, 1)

        block = ctx.enter_context(nc.Block())

        @block.sync
        def _(sp):
            sp.dma_start(cst[:, :], cst_d).then_inc(cst_in, 16)
            sp.dma_start(vec[:, :], vec_d).then_inc(cst_in, 16)
            sp.dma_start(xT[:, :, :], xT_d).then_inc(x_in, 16)
            sp.dma_start(ctxT, ctxT_d).then_inc(x_in, 16)

            def load_mod(i):
                for j in range(12):
                    n = 12 * i + j
                    if j >= MODBUF:
                        sp.wait_ge(modrow_ps, n - MODBUF + 1)
                    sp.dma_start(mw[n % MODBUF], mod_w[i, :, j * 512:(j + 1) * 512].rearrange("(c p) f -> p c f", p=128))\
                      .then_inc(modw_in[n % MODBUF], 16)

            def load_moe(i):
                m = M[i]
                sp.dma_start(rw_sb, router_w[i].rearrange("(c p) e -> p c e", p=128)).then_inc(rw_in, 16)
                sp.dma_start(bias_sb[:, :], router_bias[i].partition_broadcast(128)).then_inc(rw_in, 16)
                s = RING - 1
                sp.dma_start(w13(s)[:, 0], sh_w1[i].rearrange("(c p) f -> p c f", p=128)).then_inc(sh_in, 16)
                sp.dma_start(w13(s)[:, 1], sh_w3[i].rearrange("(c p) f -> p c f", p=128)).then_inc(sh_in, 16)
                sp.dma_start(w2(s), sh_w2[i].rearrange("(k p) d -> p k d", p=128)).then_inc(sh_in, 16)

                def expert(e, s, done):
                    sp.dma_start(w13(s)[:, 0], exp_w1[i, e].rearrange("o (p c) f -> p (o c) f", c=DC)).then_inc(done, 16)
                    sp.dma_start(w13(s)[:, 1], exp_w3[i, e].rearrange("o (p c) f -> p (o c) f", c=DC)).then_inc(done, 16)
                    sp.dma_start(w2(s), exp_w2[i, e].rearrange("o (k p) d -> p (o k) d", p=128)).then_inc(done, 16)

                for u in range(RING - 1):
                    expert(ds(u, 1), u, m["w_in"][u])
                sp.wait_ge(m["dn_ps"], TT)
                expert(ds(RING - 1, 1), RING - 1, m["w_in"][RING - 1])
                with nc.sync.Fori(0, E // RING - 1) as g:
                    for r in range(RING):
                        sp.wait_ge(m["dn_ps"], TT + 1 + r + g * RING)
                        expert(ds(g * RING + (RING + r), 1), r, m["w_in"][r])
                sp.wait_ge(unit_rdy, i + 1)
                total = nc.sync.value_load(unit_i[0:1, XMAX:XMAX + 1], min_val=0, max_val=XMAX)
                with nc.sync.If(total > 0):
                    with nc.sync.Fori(0, total) as j:
                        sp.wait_ge(m["dn_ps"], TT + E)
                        sp.wait_ge(m["t_dn"], j + 1)
                        e = nc.sync.value_load(unit_i[0:1, ds(j, 1)], min_val=0, max_val=E - 1)
                        expert(ds(e, 1), 0, m["t_w"])

            load_mod(0)
            sp.dma_start(wqa_sb, wq_a.rearrange("(c p) f -> p c f", p=128)).then_inc(aw_in, 16)
            sp.dma_start(wkva_sb, wkv_a.rearrange("(c p) f -> p c f", p=128)).then_inc(aw_in, 16)
            sp.wait_ge(modrow_ps, 12)
            sp.dma_start(wqb_sb, wq_b.rearrange("(c p) (h f) -> p c h f", p=128, h=H)).then_inc(bw_in, 16)
            sp.dma_start(wkvb_sb, wkv_b.rearrange("(c p) (h f) -> p c h f", p=128, h=H)).then_inc(bw_in, 16)
            sp.wait_ge(a_ps, len(AG))
            sp.dma_start(wo_sb, wo.rearrange("(c p) f -> p c f", p=128)).then_inc(wo_in, 16)
            sp.wait_ge(wo_ps, DC)
            load_moe(0)
            sp.wait_ge(acc_ps, DC)
            load_mod(1)
            sp.wait_ge(modrow_ps, 24)
            sp.dma_start(pw1_sb, pw1.rearrange("(c p) f -> p c f", p=128)).then_inc(pw_in, 16)
            sp.dma_start(pw2_sb, pw2.rearrange("(c p) f -> p c f", p=128)).then_inc(pw_in, 16)
            sp.wait_ge(pw2_ps, DC)
            load_moe(1)
            sp.wait_ge(nrm_out, 8 * (J_FIN + 1))
            sp.dma_start(out, oF).then_inc(out_dn, 16)
            sp.wait_ge(out_dn, 16)

        @block.gpsimd
        def _(pool):
            nc.gpsimd.memset(ones_b[:, :], 1.0).then_inc(pool_cst, 1)
            nc.gpsimd.memset(mean_w[:, :], 1.0 / D).then_inc(pool_cst, 1)
            pool.wait_ge(cst_in, 32)
            nc.gpsimd.tensor_copy(upper_b[:, :], k("upper")).then_inc(pool_cst, 1)
            nc.gpsimd.tensor_copy(upto_b[:, :], k("upto")[0:E, :]).then_inc(pool_cst, 1)
            nc.gpsimd.tensor_copy(tok_i[:, :], k("tok")).then_inc(pool_cst, 1)

            def moe(i):
                m = M[i]
                pool.wait_ge(dve_cst, 1)
                nc.gpsimd.memset(idx[:, :], NONE).then_inc(none_rdy, 1)
                pool.wait_ge(none_rdy, i + 1)
                pool.dma_start(slots[i].rearrange("(p n) o -> p (n o)", p=128), idx[:, :]).then_inc(none_set, 16)
                pool.wait_ge(rows_rdy, i + 1)
                for n in range(2):
                    nc.gpsimd.memset(xg[n], 0.0).then_inc(xg_clr, 1)
                pool.wait_ge(none_set, 16 * (i + 1))
                for n in range(K * TT):
                    pool.indirect_dma_start(out=slots[i], out_offset=bass.IndirectOffsetOnAxis(ap=row_i[:, n:n + 1], axis=0),
                                            in_=tok_i[:, n % TT:n % TT + 1], in_offset=None).then_inc(slots_set, 16)
                pool.wait_ge(slots_set, 16 * K * TT * (i + 1))
                pool.dma_start(idx[:, 0:E], slots[i][0:128 * E, :].rearrange("(p e) o -> p (e o)", e=E)).then_inc(idx_in, 16)
                pool.wait_ge(idx_in, 16 * (i + 1))
                for s in range(2):
                    pool.wait_ge(hd_out[s], 32 + 32 * i)
                pool.wait_ge(xg_clr, 2 * (i + 1))

                def gather(u, n, done):
                    nc.gpsimd.tensor_copy(col_i[:, n:n + 1], idx[:, ds(u, 1)]).then_inc(m["col_rdy"], 1)
                    pool.wait_ge(m["col_rdy"], u + 1)
                    nc.gpsimd.tensor_tensor(tick[0:1, 8 * i + 2:8 * i + 3], zero[0:1, 0:1], zero[0:1, 0:1], ALU.add)
                    pool.indirect_dma_start(out=xg[n], out_offset=None, in_=h_rows[i],
                                            in_offset=bass.IndirectOffsetOnAxis(ap=col_i[:, n:n + 1], axis=0),
                                            bounds_check=T - 1, oob_is_err=False).then_inc(done, 16)

                gather(0, 0, m["xg_in"][0])
                gather(1, 1, m["xg_in"][1])
                with nc.gpsimd.Fori(0, E // 2 - 1) as g:
                    for r in range(2):
                        pool.wait_ge(m["xgT_ps"], g * 2 + (1 + r))
                        gather(g * 2 + (2 + r), r, m["xg_in"][r])
                pool.wait_ge(unit_rdy, i + 1)
                pool.wait_ge(m["xgT_ps"], E)
                total = nc.gpsimd.value_load(unit_i[0:1, XMAX:XMAX + 1], min_val=0, max_val=XMAX)
                with nc.gpsimd.If(total > 0):
                    with nc.gpsimd.Fori(0, total) as j:
                        pool.wait_ge(m["t_xgT_ps"], j + 1)
                        nc.gpsimd.tensor_tensor(tick[0:1, 8 * i + 3:8 * i + 4], zero[0:1, 0:1], zero[0:1, 0:1], ALU.add)
                        pool.dma_start(idx[:, E:E + 1], slots[i][128 * E:ROWS, :].rearrange("(u p) o -> p u o", p=128)
                                       [:, ds(j, 1), :].rearrange("p u o -> p (u o)")).then_inc(m["t_idx"], 16)
                        pool.wait_ge(m["t_idx"], j * 16 + 16)
                        nc.gpsimd.tensor_tensor(tick[0:1, 8 * i + 6:8 * i + 7], zero[0:1, 0:1], zero[0:1, 0:1], ALU.add)
                        pool.indirect_dma_start(out=xg[0], out_offset=None, in_=h_rows[i],
                                                in_offset=bass.IndirectOffsetOnAxis(ap=idx[:, E:E + 1], axis=0),
                                                bounds_check=T - 1, oob_is_err=False).then_inc(m["t_xg"], 16)
                pool.wait_ge(zero_out, 32)
                for s in range(2):
                    pool.wait_ge(m["y_out"][s], 16 * E // 2)
                pool.wait_ge(m["dn_ps"], TT + E)
                with nc.gpsimd.If(total > 0):
                    pool.wait_ge(m["t_yout"], total * 16)
                    nc.gpsimd.tensor_tensor(tick[0:1, 8 * i + 4:8 * i + 5], zero[0:1, 0:1], zero[0:1, 0:1], ALU.add)
                for n in range(TT * K):
                    t, q = n // K, n % K
                    if n >= 6:
                        pool.wait_ge(comb_used, n - 5 + i * TT * K)
                    pool.indirect_dma_start(out=comb[n % 6], out_offset=None, in_=y_rows,
                                            in_offset=bass.IndirectOffsetOnAxis(ap=row_i[:, q * TT + t:q * TT + t + 1], axis=0))\
                        .then_inc(comb_in[n % 6], 16)

            pool.wait_ge(bw_in, 32)
            for n in range(2):
                pool.dma_start(y_rows[128 * E:ROWS, :].rearrange("(u p) (a d) -> p u a d", p=128, a=2)[:, :, n, :],
                               zrow[:, :].unsqueeze(1).to_broadcast([128, XMAX, 512])).then_inc(zero_out, 16)
            moe(0)
            pool.wait_ge(nrm_out, 8 * (J_MIX1 + 1))
            for c in range(DC):
                for q in range(PE_TAPS):
                    n = c * PE_TAPS + q
                    if q == 0 and c >= 2:
                        pool.wait_ge(tap_ps, c - 1)
                    nc.gpsimd.tensor_scalar(diag[n % (2 * PE_TAPS)], ident, v("dww", c * TAPS + q, c * TAPS + q + 1), None,
                                            ALU.mult).then_inc(diag_rdy, 1)
            moe(1)

        @block.scalar
        def _(a):
            A = nc.scalar.activation
            a.wait_ge(cst_in, 32)
            a.wait_ge(dve_cst, 1)
            A(cs[:, :, 0:2], v("c").rearrange("p (c w) -> p c w", w=2), ACT.Silu).then_inc(cs_rdy, 1)

            def mod_rows(i):
                for j in range(12):
                    n = 12 * i + j
                    a.wait_ge(modrow_ps, n + 1)
                    if n >= 2:
                        a.wait_ge(modcol_ps, n - 1)
                    A(mrow[n % 2], bank(n % 2), ACT.Copy).then_inc(modrow_sb, 1)

            def norm(j):
                src, dst, w, sc, sh, fn = JOBS[j]
                for c in range(DC):
                    n = 8 * j + c
                    if n >= 2:
                        a.wait_ge(sq_used, n - 1)
                    A(sq[:, n % 2, 0:w], src(c), ACT.Square).then_inc(sq_rdy, 1)
                a.wait_ge(sq_used, 8 * (j + 1))
                if j:
                    a.wait_ge(nrm_mul, 8 * j)
                A(rs[:, 0:w], bank(NB)[:, 0:w], ACT.Sqrt, bias=eps[:, 0:1]).then_inc(std_rdy, 1)
                for c in range(DC):
                    a.wait_ge(nrm_mul, 8 * j + c + 1)
                    A(dst(c), dst(c), fn, bias=sh(c), scale=sc(c)).then_inc(nrm_out, 1)

            def moe(i):
                m = M[i]
                a.wait_ge(logit_ps, i + 1)
                A(score, bank(0)[:, 0:TT * E], ACT.Sigmoid).then_inc(score_rdy, 1)
                for t in range(TT):
                    a.wait_ge(hrow_ps, t + 1 + i * TT)
                    if t >= 2:
                        a.wait_ge(hd_out[t % 2], 16 + 32 * i)
                    A(yb[t % 2].rearrange("p (c q) -> p q c", c=DC),
                      bank(1 if t % 2 == 0 else 4, 2).rearrange("p (q c) -> p q c", c=DC), ACT.Copy).then_inc(hrow_sb, 1)
                    a.wait_ge(hrow_sb, t + 1 + i * TT)
                    a.dma_start(h_rows[i][t * 128:(t + 1) * 128, :], yb[t % 2]).then_inc(hd_out[t % 2], 16)

                def silu(w, b, par):
                    a.wait_ge(m["up_ps"], w + 1)
                    if b:
                        a.wait_ge(m["act_rdy"], w - 1)
                    A(gate[par], bank(6)[:, 0:F], ACT.Silu).then_inc(m["gate_rdy"], 1)

                def store(u, wait_n, par):
                    a.wait_ge(m["dn_ps"], u + (TT + 1))
                    if not (isinstance(wait_n, int) and wait_n == 0):
                        a.wait_ge(m["y_out"][par], wait_n)
                    A(yb[par], bank(4, 2), ACT.Copy).then_inc(m["y_ev"], 1)
                    a.wait_ge(m["y_ev"], u + (TT + 1))
                    a.dma_start(y_rows[0:128 * E, :].rearrange("(p e) d -> p e d", e=E)[:, ds(u, 1), :]
                                .rearrange("p e d -> p (e d)"), yb[par]).then_inc(m["y_out"][par], 16)

                for w in range(TT):
                    silu(w, w >= 2, w % 2)
                    if w:
                        a.wait_ge(m["dn_ps"], w)
                        A(acc[:, w - 1, :], bank(4, 2), ACT.Copy).then_inc(m["y_ev"], 1)
                for s in range(2):
                    a.wait_ge(hd_out[s], 32 + 32 * i)
                silu(TT, 1, 0)
                a.wait_ge(m["dn_ps"], TT)
                A(acc[:, TT - 1, :], bank(4, 2), ACT.Copy).then_inc(m["y_ev"], 1)
                for u in range(1, 5):
                    silu(TT + u, 1, u % 2)
                    store(u - 1, 16 * ((u - 1) // 2), (u - 1) % 2)
                with nc.scalar.Fori(1, E // 4 - 1) as g:
                    for r in range(4):
                        silu(g * 4 + (TT + 1 + r), 1, (1 + r) % 2)
                        store(g * 4 + r, g * 32 + 16 * (r // 2), r % 2)
                for u in range(E - 3, E):
                    silu(TT + u, 1, u % 2)
                    store(u - 1, 16 * ((u - 1) // 2), (u - 1) % 2)
                store(E - 1, 16 * ((E - 1) // 2), 1)
                a.sem_inc(m["t_yev"], 1)
                a.wait_ge(unit_rdy, i + 1)
                total = nc.scalar.value_load(unit_i[0:1, XMAX:XMAX + 1], min_val=0, max_val=XMAX)
                with nc.scalar.If(total > 0):
                    a.wait_ge(m["y_out"][0], 16 * E // 2)
                    a.wait_ge(zero_out, 32)
                    with nc.scalar.Fori(0, total) as j:
                        a.wait_ge(m["t_up"], j + 1)
                        A(gate[0], bank(6)[:, 0:F], ACT.Silu).then_inc(m["t_gate"], 1)
                        a.wait_ge(m["t_dn"], j + 2)
                        A(yb[0], bank(4, 2), ACT.Copy).then_inc(m["t_yev"], 1)
                        a.wait_ge(m["t_yev"], j + 2)
                        a.dma_start(y_rows[128 * E:ROWS, :].rearrange("(u p) d -> p u d", p=128)[:, ds(j, 1), :]
                                    .rearrange("p u d -> p (u d)"), yb[0]).then_inc(m["t_yout"], 16)
                        a.wait_ge(m["t_yout"], j * 16 + 16)
                        A(tick[0:1, i:i + 1], zero[0:1, 0:1], ACT.Copy).then_inc(m["t_tick"], 1)

            mod_rows(0)
            a.wait_ge(x_in, 32)
            a.wait_ge(mod_rdy, 1)
            norm(J_CTX)
            norm(J_X)
            for s, g in enumerate(LSQ):
                kind, c0, w, blk = AG[g]
                a.wait_ge(a_ps, g + 1)
                if s >= 2:
                    a.wait_ge(lsq_used, s - 1)
                if kind == "kv":
                    A(ckv[:, blk, c0:c0 + w], bank(4 + g % 4)[:, 0:w], ACT.Copy)
                else:
                    A(qa[:, blk, :], bank(4 + g % 4), ACT.Copy)
                A(sq[:, s % 2, 0:w], bank(4 + g % 4)[:, 0:w], ACT.Square).then_inc(lsq_rdy, 1)
                for b, lw, gs, _, _ in LAT:
                    if g == gs[-1]:
                        a.wait_ge(lsq_used, s + 1)
                        if s >= len(gs):
                            a.wait_ge(lat_rdy, s + 1 - len(gs))
                        A(rs[:, 0:lw], bank(b)[:, 0:lw], ACT.Sqrt, bias=eps[:, 0:1], scale=D / (128.0 * len(gs))).then_inc(lstd_rdy, 1)

            def kv_out(m, part):
                n = 6 * m + part
                a.wait_ge(pj_ps, n + 1)
                if part == 0:
                    for q in range(2):
                        last = A(kT[m % 2][q][0:64, T:KEYS], bank(7)[64 * q:64 * q + 64, 0:C], ACT.Copy)
                elif part == 1:
                    for q in range(2):
                        last = A(kT[m % 2][q][0:64, 0:T], bank(6)[64 * q:64 * q + 64, :], ACT.Copy)
                elif part == 4:
                    last = A(vv[m % 2][:, 0:4, :], bank(7).rearrange("p (j f) -> p j f", j=4), ACT.Copy)
                else:
                    last = A(vv[m % 2][:, 4:6, :], bank(6)[:, 0:256].rearrange("p (j f) -> p j f", j=2), ACT.Copy)
                last.then_inc(kv_ev, 1)

            a.wait_ge(lat_rdy, 8)
            a.wait_ge(bw_in, 32)
            for part in (0, 1, 4, 5):
                kv_out(0, part)
            for n in range(NS):
                m, i8 = n // 8, n % 8
                a.wait_ge(nmax_rdy, n + 1)
                if n >= 2:
                    a.wait_ge(pT_ps, n - 1)
                A(P[n % 2], bank(2 * (n % 2), 2)[:, 0:KEYS], ACT.Exp, bias=smx[:, n % 4, 1:2], scale=SM_SCALE,
                  accum_out=smx[:, n % 4, 2:3]).then_inc(exp_rdy, 1)
                if m + 1 < NPAIR and i8 in (1, 2, 5, 6):
                    kv_out(m + 1, {1: 0, 2: 1, 5: 4, 6: 5}[i8])
                if n >= 1:
                    pT_copy(a, A, n - 1, True)
            pT_copy(a, A, NS - 1, True)
            a.wait_ge(wo_ev, DC)
            norm(J_FFN0)
            moe(0)
            mod_rows(1)
            a.wait_ge(res_ev, DC)
            a.wait_ge(mod_rdy, 2)
            norm(J_MIX1)
            for c in range(DC):
                a.wait_ge(glu_ps, c + 1)
                if c >= 2:
                    a.wait_ge(u_rdy, c - 1)
                A(sg[c % 2], bank(2 * (c % 2) + 1), ACT.Sigmoid, bias=v("pw1b", DC + c, DC + c + 1)).then_inc(sig_rdy, 1)
            a.wait_ge(cent_rdy, DC)
            norm(J_LN)
            a.wait_ge(pw2_ev, DC)
            norm(J_FFN1)
            moe(1)
            a.wait_ge(res_ev, 2 * DC)
            norm(J_FIN)

        @block.tensor
        def _(pe):
            mm, tr = nc.tensor.matmul, nc.tensor.transpose
            pe.wait_ge(pool_cst, 5)
            pe.wait_ge(cs_rdy, 1)

            def mod_cols(i):
                def columns(n):
                    pe.wait_ge(modrow_sb, n + 1)
                    for q in range(4):
                        at = 2 * (4 * (n % 12) + q)
                        last = mm(bank(2)[:, at:at + 2], mrow[n % 2][:, 128 * q:128 * q + 128], k("sel"), start=True, stop=True)
                    last.then_inc(modcol_ps, 1)

                for j in range(12):
                    n = 12 * i + j
                    pe.wait_ge(modw_in[n % MODBUF], 16 * (n // MODBUF + 1))
                    if n >= 2:
                        pe.wait_ge(modrow_sb, n - 1)
                    for c in range(DC):
                        t = c % 4
                        last = mm(bank(n % 2)[32 * t:32 * t + 32, :], cs[:, c, :], mw[n % MODBUF][:, c, :],
                                  start=(c < 4), stop=(c >= 4), tile_position=(0, 32 * t), skip_group_check=True)
                    last.then_inc(modrow_ps, 1)
                    if j:
                        columns(n - 1)
                columns(12 * i + 11)

            def norm(j):
                src, dst, w, sc, sh, fn = JOBS[j]
                if j:
                    pe.wait_ge(rs_rdy, j)
                for c in range(DC):
                    pe.wait_ge(sq_rdy, 8 * j + c + 1)
                    mm(bank(NB)[:, 0:w], mean_w[:, :], sq[:, c % 2, 0:w], start=(c == 0), stop=(c == DC - 1)).then_inc(sq_used, 1)

            mod_cols(0)
            norm(J_CTX)
            norm(J_X)
            pe.wait_ge(nrm_out, 16)
            pe.wait_ge(aw_in, 32)
            pe.wait_ge(rs_rdy, 2)

            def latent_sum(s):
                g = LSQ[s]
                b, w, gs, _, _ = [x for x in LAT if g in x[2]][0]
                pe.wait_ge(lsq_rdy, s + 1)
                mm(bank(b)[:, 0:w], mean_w[:, :], sq[:, s % 2, 0:w], start=(g == gs[0]),
                   stop=(g == gs[-1])).then_inc(lsq_used, 1)

            for g, (kind, c0, w, blk) in enumerate(AG):
                if g >= 4:
                    if AG[g - 4][0] == "pe":
                        pe.wait_ge(a_pe, (g - 4) // 3 + 1)
                    else:
                        pe.wait_ge(lsq_rdy, LSQ.index(g - 4) + 1)
                for c in range(DC):
                    if kind == "q":
                        lhs, M_ = wqa_sb[:, c, 128 * blk:128 * blk + 128], 128
                    elif kind == "kv":
                        lhs, M_ = wkva_sb[:, c, 128 * blk:128 * blk + 128], 128
                    else:
                        lhs, M_ = wkva_sb[:, c, KVL:KVW], 2 * ROPE
                    last = mm(bank(4 + g % 4)[0:M_, 0:w], lhs, hA[:, c, c0:c0 + w], start=(c == 0), stop=(c == DC - 1))
                last.then_inc(a_ps, 1)
                if g >= 1 and g - 1 in LSQ:
                    latent_sum(LSQ.index(g - 1))
            latent_sum(len(LSQ) - 1)

            def project(m, part):
                if part == 0 and m:
                    pe.wait_ge(kv_ev, 4 * m - 1)
                elif part == 1 and m:
                    pe.wait_ge(kv_ev, 4 * m)
                    pe.wait_ge(o_ev, m - 1)
                elif part == 2:
                    pe.wait_ge(kv_ev, 4 * m + 1)
                elif part == 3:
                    pe.wait_ge(kv_ev, 4 * m + 2)
                elif part == 4:
                    pe.wait_ge(q_ev, 2 * m + 1)
                elif part == 5:
                    pe.wait_ge(q_ev, 2 * m + 2)
                if part < 2:
                    b, w, c0 = ((7, C, T), (6, T, 0))[part]
                    for c in range(2):
                        last = mm(bank(b)[:, 0:w], wkvb_sb[:, c, 2 * m, :], ckv[:, c, c0:c0 + w],
                                  start=(c == 0), stop=(c == 1))
                elif part < 4:
                    for c in range(4):
                        last = mm(bank(7 if part == 2 else 6), wqb_sb[:, c, 2 * m + part - 2, :], qa[:, c, :],
                                  start=(c == 0), stop=(c == 3))
                else:
                    for j in (range(4) if part == 4 else range(4, 6)):
                        for c in range(2):
                            last = mm(bank(7 if part == 4 else 6)[:, (j % 4) * 128:(j % 4) * 128 + 128],
                                      ckv[:, c, j * 128:(j + 1) * 128], wkvb_sb[:, c, 2 * m + 1, :],
                                      start=(c == 0), stop=(c == 1))
                last.then_inc(pj_ps, 1)

            def scores(n):
                m, q, t = n // 8, (n // TT) % 2, n % TT
                pe.wait_ge(kv_ev, 4 * m + 2)
                pe.wait_ge(q_ev, 2 * m + 1 + q)
                if n >= 2:
                    pe.wait_ge(exp_rdy, n - 1)
                for c0, w in ((0, 512), (512, 256)):
                    last = mm(bank(2 * (n % 2), 2)[:, c0:c0 + w], qT[m % 2][q][0:96, t * 128:(t + 1) * 128],
                              kT[m % 2][q][0:96, c0:c0 + w], start=True, stop=True)
                last.then_inc(s_ps, 1)

            def turn(n):
                pe.wait_ge(p_rdy, n + 1)
                if n:
                    pe.wait_ge(pT_act, n)
                    pe.wait_ge(pT_dve, n)
                for j in range(6):
                    last = tr(bank(4, 2)[:, j * 128:(j + 1) * 128], P[n % 2][:, j * 128:(j + 1) * 128], ident)
                last.then_inc(pT_ps, 1)

            pe.wait_ge(lat_rdy, 8)
            pe.wait_ge(bw_in, 32)
            for part in range(6):
                project(0, part)
            scores(0)
            for n in range(NS):
                m, i8 = n // 8, n % 8
                if n + 1 < NS:
                    scores(n + 1)
                if m + 1 < NPAIR and i8 < 6:
                    project(m + 1, i8)
                turn(n)
                if i8 == 7:
                    pe.wait_ge(pT_act, n + 1)
                    pe.wait_ge(pT_dve, n + 1)
                    pe.wait_ge(kv_ev, 4 * min(m + 2, NPAIR))
                    for j in range(6):
                        for q in range(2):
                            last = mm(bank(6)[64 * q:64 * q + 64, :], vv[m % 2][:, j, 64 * q:64 * q + 64], pT[:, q, j, :],
                                      start=(j == 0), stop=(j == 5), tile_position=(0, 64 * q), skip_group_check=True)
                    last.then_inc(o_ps, 1)
            pe.wait_ge(o_ev, NPAIR)
            pe.wait_ge(wo_in, 16)
            for n in range(DC):
                if n >= 2:
                    pe.wait_ge(wo_ev, n - 1)
                for c in range(DC):
                    last = mm(bank(n % 2), wo_sb[:, c, n * 128:(n + 1) * 128], oT[:, c, :], start=(c == 0), stop=(c == DC - 1))
                last.then_inc(wo_ps, 1)

            def moe(i):
                m = M[i]
                pe.wait_ge(rw_in, 32 * (i + 1))
                for t in range(TT):
                    for c in range(DC):
                        last = mm(bank(0)[:, t * E:(t + 1) * E], hM[:, c, t * 128:(t + 1) * 128], rw_sb[:, c, :],
                                  start=(c == 0), stop=(c == DC - 1))
                last.then_inc(logit_ps, 1)
                for t in range(TT):
                    if t >= 2:
                        pe.wait_ge(hrow_sb, t - 1 + i * TT)
                    for c in range(DC):
                        last = tr(bank(1 if t % 2 == 0 else 4, 2)[:, c * 128:(c + 1) * 128], hM[:, c, t * 128:(t + 1) * 128], ident)
                    last.then_inc(hrow_ps, 1)
                pe.wait_ge(chosen_rdy, i + 1)
                for t in range(TT):
                    for s in range(t + 1):
                        last = mm(bank(3)[:, t * E:(t + 1) * E], upper_b[:, :] if s == t else ones_b[:, :],
                                  chosen_b[:, s * E:(s + 1) * E], start=(s == 0), stop=(s == t))
                last.then_inc(pos_ps, 1)
                for t in range(TT):
                    last = mm(bank(0)[0:E, 0:1], chosen_b[:, t * E:(t + 1) * E], ones_b[:, 0:1], start=(t == 0), stop=(t == TT - 1))
                last.then_inc(cnt_ps, 1)
                pe.wait_ge(nbx_rdy, i + 1)
                mm(bank(0)[0:E, 8:9], upto_b[:, :], extra_b[:, 0:1], start=True, stop=True)
                mm(bank(3)[:, TT * E:(TT + 1) * E], extra_b[:, :], upper_b[0:E, 0:E], start=True, stop=True).then_inc(end_ps, 1)
                pe.wait_ge(passed_rdy, i + 1)
                mm(bank(0)[0:1, 16:16 + XMAX], ones_b[0:E, 0:1], passed_b[:, :], start=True, stop=True)
                mm(bank(0)[0:1, 128:129], extra_b[:, 0:1], ones_b[0:E, 0:1], start=True, stop=True).then_inc(unit_ps, 1)

                def up_mm(lhs, s):
                    for c in range(DC):
                        last = mm(bank(6), lhs(c), w13(s)[:, :, c, :], start=(c == 0), stop=(c == DC - 1))
                    return last

                def down_mm(par, s):
                    for half in range(2):
                        for kk in range(2):
                            last = mm(bank(4 + half), actT[par][:, kk, :], w2(s)[:, kk, half * 512:(half + 1) * 512],
                                      start=(kk == 0), stop=(kk == 1))
                    return last

                def act_tr(par):
                    for kk in range(2):
                        last = tr(bank(7)[:, kk * 128:(kk + 1) * 128], act[par][:, kk * 128:(kk + 1) * 128], ident)
                    return last

                def rows_tr(par):
                    for c in range(DC):
                        last = tr(bank(1, 2)[:, c * 128:(c + 1) * 128], xg[par][:, c * 128:(c + 1) * 128], ident)
                    return last

                def up(w, lhs, s):
                    pe.wait_ge(m["act_rdy"], w)
                    up_mm(lhs, s).then_inc(m["up_ps"], 1)

                def down(w, par, s):
                    pe.wait_ge(m["actT_ev"], w + 1)
                    pe.wait_ge(m["y_ev"], w)
                    down_mm(par, s).then_inc(m["dn_ps"], 1)

                def turn_act(w, par):
                    pe.wait_ge(m["act_rdy"], w + 1)
                    pe.wait_ge(m["actT_ev"], w)
                    act_tr(par).then_inc(m["actT_ps"], 1)

                def turn_rows(u, n_in, par):
                    pe.wait_ge(m["xg_in"][par], n_in)
                    pe.wait_ge(m["xgT_ev"], u)
                    rows_tr(par).then_inc(m["xgT_ps"], 1)

                pe.wait_ge(sh_in, 48 * (i + 1))
                pe.wait_ge(hrow_sb, TT + i * TT)
                for w in range(TT):
                    up(w, lambda c, w=w: hM[:, c, w * 128:(w + 1) * 128], RING - 1)
                    if w:
                        down(w - 1, (w - 1) % 2, RING - 1)
                    turn_act(w, w % 2)
                turn_rows(0, 16, 0)
                pe.wait_ge(m["xgT_ev"], 1)
                pe.wait_ge(m["w_in"][0], 48)
                up(TT, lambda c: xgT[0][:, c, :], 0)
                turn_rows(1, 16, 1)
                down(TT - 1, 1, RING - 1)
                turn_act(TT, 0)

                def unit(u, slot, n_w, n_next, par):
                    w = u + TT
                    pe.wait_ge(m["xgT_ev"], u + 1)
                    pe.wait_ge(m["w_in"][slot], n_w)
                    up(w, lambda c: xgT[par][:, c, :], slot)
                    if n_next is not None:
                        turn_rows(u + 1, n_next, 1 - par)
                    down(w - 1, 1 - par, (slot - 1) % RING)
                    turn_act(w, par)

                with nc.tensor.Fori(0, E // 4 - 1) as g:
                    for r in range(4):
                        unit(g * 4 + (1 + r), (1 + r) % 4, g * 48 + 48 * ((1 + r) // 4 + 1), g * 32 + 16 * ((2 + r) // 2 + 1), (1 + r) % 2)
                for u in range(E - 3, E):
                    unit(u, u % 4, 48 * (u // 4 + 1), 16 * ((u + 1) // 2 + 1) if u + 1 < E else None, u % 2)
                down(TT + E - 1, 1, RING - 1)
                pe.sem_inc(m["t_dn"], 1)
                pe.sem_inc(m["t_xgT_ps"], 1)
                pe.wait_ge(unit_rdy, i + 1)
                total = nc.tensor.value_load(unit_i[0:1, XMAX:XMAX + 1], min_val=0, max_val=XMAX)
                with nc.tensor.If(total > 0):
                    pe.wait_ge(m["y_ev"], TT + E)
                    with nc.tensor.Fori(0, total) as j:
                        pe.wait_ge(m["t_xg"], j * 16 + 16)
                        rows_tr(0).then_inc(m["t_xgT_ps"], 1)
                        pe.wait_ge(m["t_xgT_ev"], j + 1)
                        pe.wait_ge(m["t_w"], j * 48 + 48)
                        up_mm(lambda c: xgT[0][:, c, :], 0).then_inc(m["t_up"], 1)
                        pe.wait_ge(m["t_act"], j + 1)
                        act_tr(0).then_inc(m["t_actT_ps"], 1)
                        pe.wait_ge(m["t_actT_ev"], j + 1)
                        pe.wait_ge(m["t_yev"], j + 1)
                        down_mm(0, 0).then_inc(m["t_dn"], 1)
                pe.wait_ge(comb_used, TT * K + i * TT * K)
                for c in range(DC):
                    if c >= 2:
                        pe.wait_ge(res_ev, c - 1 + i * DC)
                    for t in range(TT):
                        last = tr(bank(c % 2)[:, t * 128:(t + 1) * 128], acc[:, t, c * 128:(c + 1) * 128], ident)
                    last.then_inc(acc_ps, 1)

            norm(J_FFN0)
            pe.wait_ge(nrm_out, 8 * (J_FFN0 + 1))
            moe(0)
            pe.wait_ge(res_ev, DC)
            mod_cols(1)
            norm(J_MIX1)
            pe.wait_ge(nrm_out, 8 * (J_MIX1 + 1))
            pe.wait_ge(pw_in, 32)
            pe.wait_ge(mod_rdy, 2)

            def taps(c):
                pe.wait_ge(u_rdy, c + 1)
                pe.wait_ge(diag_rdy, PE_TAPS * (c + 1))
                if c >= 2:
                    pe.wait_ge(cv_rdy, c - 1)
                for q in range(PE_TAPS):
                    last = mm(bank(4 + c % 2), diag[(c * PE_TAPS + q) % (2 * PE_TAPS)], up_view(c)[:, q:q + T],
                              start=(q == 0), stop=(q == PE_TAPS - 1))
                last.then_inc(tap_ps, 1)

            for c in range(DC):
                if c >= 2:
                    pe.wait_ge(u_rdy, c - 1)
                for half in range(2):
                    for kk in range(DC):
                        last = mm(bank(2 * (c % 2) + half), pw1_sb[:, kk, half * D + c * 128:half * D + (c + 1) * 128], hM[:, kk, :],
                                  start=(kk == 0), stop=(kk == DC - 1))
                last.then_inc(glu_ps, 1)
                if c:
                    taps(c - 1)
            taps(DC - 1)
            for c in range(DC):
                pe.wait_ge(cv_rdy, c + 1)
                last = mm(bank(6), mean_w[:, :], conv[:, c, :], start=(c == 0), stop=(c == DC - 1))
            last.then_inc(mean_ps, 1)
            norm(J_LN)
            pe.wait_ge(nrm_out, 8 * (J_LN + 1))
            for n in range(DC):
                if n >= 2:
                    pe.wait_ge(pw2_ev, n - 1)
                for c in range(DC):
                    last = mm(bank(n % 2), pw2_sb[:, c, n * 128:(n + 1) * 128], hM[:, c, :], start=(c == 0), stop=(c == DC - 1))
                last.then_inc(pw2_ps, 1)
            norm(J_FFN1)
            pe.wait_ge(nrm_out, 8 * (J_FFN1 + 1))
            moe(1)
            norm(J_FIN)

        @block.vector
        def _(dve):
            V = nc.vector
            step = [0]

            def link(ins):
                step[0] += 1
                ins.then_inc(dve_step, 1)
                dve.wait_ge(dve_step, step[0])

            V.memset(cs[:, :, :], 0.0)
            V.memset(eps[:, :], EPS)
            V.memset(zrow[:, :], 0.0)
            V.memset(zero[:, :], 0.0).then_inc(dve_cst, 1)

            def mod_out(i):
                dve.wait_ge(cst_in, 32)
                dve.wait_ge(modcol_ps, 12 * (i + 1))
                for w in range(2):
                    last = V.tensor_tensor(mod[i][:, :, :, w].rearrange("p s c -> p (s c)"), bank(2)[:, w:96:2],
                                           v("modb", 48 * i, 48 * i + 48), ALU.add)
                link(last)
                for n, g in ((0, "nmix"), (1, "nffn")):
                    for w in range(2):
                        last = V.scalar_tensor_tensor(modA[i][:, n, :, w], mod[i][:, 3 * n + 1, :, w], 1.0,
                                                      v(g, DC * i, DC * i + DC), ALU.add, ALU.mult)
                last.then_inc(mod_rdy, 1)

            def norm(j):
                src, dst, w, sc, sh, fn = JOBS[j]
                dve.wait_ge(std_rdy, j + 1)
                V.reciprocal(rs[:, 0:w], rs[:, 0:w]).then_inc(rs_rdy, 1)
                dve.wait_ge(rs_rdy, j + 1)
                for c in range(DC):
                    V.tensor_tensor(dst(c), src(c), rs[:, 0:w], ALU.mult).then_inc(nrm_mul, 1)

            mod_out(0)
            dve.wait_ge(x_in, 32)
            norm(J_CTX)
            norm(J_X)
            dve.wait_ge(nrm_out, 16)
            dve.wait_ge(a_ps, 3)
            for a_ in range(2):
                for b_ in range(2):
                    last = V.tensor_copy(kT[a_][b_][64:96, 0:C], bank(4 + 2)[0:ROPE, 0:C])
            last.then_inc(a_pe, 1)
            rope_x = bank(4 + 5 % 4)
            dve.wait_ge(a_ps, 6)
            V.tensor_tensor(rope_t[0][0:32, :], rope_x[0:32, :], k("rope")[0:32, :], ALU.mult)
            link(V.tensor_tensor(rope_t[1][0:32, :], rope_x[32:64, :], k("rope")[32:64, :], ALU.mult))
            for a_ in range(2):
                for b_ in range(2):
                    last = V.tensor_tensor(kT[a_][b_][64:96, C:KEYS], rope_t[0][0:32, :], rope_t[1][0:32, :], ALU.add)
            last.then_inc(a_pe, 1)
            for J, (b, w, gs, lat, gain) in enumerate(LAT):
                dve.wait_ge(lstd_rdy, J + 1)
                V.reciprocal(rs[:, 0:w], rs[:, 0:w]).then_inc(lrs_rdy, 1)
                dve.wait_ge(lrs_rdy, J + 1)
                for j in range(len(gs)):
                    V.scalar_tensor_tensor(lat(j), lat(j), v(gain, j, j + 1), rs[:, 0:w], ALU.mult, ALU.mult).then_inc(lat_rdy, 1)

            dve.wait_ge(lat_rdy, 8)

            def q_out(m, q):
                b = bank(7 if q == 0 else 6)
                dve.wait_ge(pj_ps, 6 * m + 3 + q)
                dve.wait_ge(q_ev, 2 * m + q)
                dst = qT[m % 2][q]
                V.tensor_copy(dst[0:64, :], b[0:64, :])
                V.tensor_tensor(rope_t[0][64:96, :], b[64:96, :], k("rope")[64:96, :], ALU.mult)
                V.tensor_tensor(rope_t[1][64:96, :], b[96:128, :], k("rope")[96:128, :], ALU.mult).then_inc(q_rope, 1)
                dve.wait_ge(q_rope, 2 * m + q + 1)
                V.tensor_tensor(dst[64:96, :], rope_t[0][64:96, :], rope_t[1][64:96, :], ALU.add).then_inc(q_ev, 1)

            q_out(0, 0)
            q_out(0, 1)

            def top_score(n):
                dve.wait_ge(s_ps, n + 1)
                if n >= 4:
                    dve.wait_ge(p_rdy, n - 3)
                V.tensor_reduce(smx[:, n % 4, 0:1], bank(2 * (n % 2), 2)[:, 0:KEYS], AX.X, ALU.max).then_inc(max_rdy, 1)
                dve.wait_ge(max_rdy, n + 1)
                V.tensor_scalar(smx[:, n % 4, 1:2], smx[:, n % 4, 0:1], -SM_SCALE, None, ALU.mult).then_inc(nmax_rdy, 1)

            def divide(n):
                dve.wait_ge(exp_rdy, n + 1)
                V.reciprocal(smx[:, n % 4, 0:1], smx[:, n % 4, 2:3]).then_inc(den_rdy, 1)
                dve.wait_ge(den_rdy, n + 1)
                V.tensor_scalar(P[n % 2], P[n % 2], smx[:, n % 4, 0:1], None, ALU.mult).then_inc(p_rdy, 1)

            top_score(0)
            for n in range(NS):
                m, i8 = n // 8, n % 8
                divide(n)
                if n + 1 < NS:
                    top_score(n + 1)
                if m + 1 < NPAIR and i8 in (3, 4):
                    q_out(m + 1, i8 - 3)
                if i8 == 0 and m:
                    dve.wait_ge(o_ps, m)
                    V.tensor_copy(oT[:, m - 1, :], bank(6)).then_inc(o_ev, 1)
                pT_copy(dve, V.tensor_copy, n, False)
            dve.wait_ge(o_ps, NPAIR)
            V.tensor_copy(oT[:, NPAIR - 1, :], bank(6)).then_inc(o_ev, 1)
            for n in range(DC):
                dve.wait_ge(wo_ps, n + 1)
                V.scalar_tensor_tensor(xT[:, n, :], bank(n % 2), mod[0][:, 2, n, 0:1], xT[:, n, :], ALU.mult, ALU.add).then_inc(wo_ev, 1)
            dve.wait_ge(wo_ev, DC)
            norm(J_FFN0)

            def moe(i):
                m = M[i]
                TE = TT * E
                te = lambda ap: ap.rearrange("p (t e) -> p t e", t=TT)
                dve.wait_ge(score_rdy, i + 1)
                dve.wait_ge(rw_in, 32 * (i + 1))
                link(V.tensor_tensor(te(select), te(score), bias_sb[:, :].unsqueeze(1).to_broadcast([128, TT, E]), ALU.add))
                for n in range(TT * G):
                    last = V.max(gtop[:, 8 * n:8 * n + 8], select[:, 8 * n:8 * n + 8])
                link(last)
                link(V.tensor_tensor(gsum, gtop[:, 0:8 * TT * G:8], gtop[:, 1:8 * TT * G:8], ALU.add))
                gs3 = gsum.rearrange("p (t g) -> p t g", t=TT)
                one = gs3.unsqueeze(3).to_broadcast([128, TT, G, G])
                other = gs3.unsqueeze(2).to_broadcast([128, TT, G, G])
                g4 = lambda ap: ap.rearrange("p (t g h) -> p t g h", t=TT, g=G)
                V.tensor_tensor(g4(cmpa), other, one, ALU.is_gt)
                link(V.tensor_tensor(g4(cmpb), other, one, ALU.is_equal))
                link(V.tensor_tensor(cmpb.rearrange("p (t x) -> p t x", t=TT), cmpb.rearrange("p (t x) -> p t x", t=TT),
                                     k("before").unsqueeze(1).to_broadcast([128, TT, G * G]), ALU.mult))
                link(V.tensor_tensor(cmpa, cmpa, cmpb, ALU.add))
                link(V.tensor_reduce(rank, cmpa.rearrange("p (n h) -> p n h", h=G), AX.X, ALU.add))
                link(V.tensor_scalar(rank, rank, TOPG - 0.5, -3e38, ALU.is_gt, ALU.mult))
                link(V.tensor_tensor(select.rearrange("p (n e) -> p n e", e=G), select.rearrange("p (n e) -> p n e", e=G),
                                     rank.unsqueeze(2).to_broadcast([128, TT * G, G]), ALU.add))
                for t in range(TT):
                    last = V.max(top[:, 8 * t:8 * t + 8], select[:, t * E:(t + 1) * E])
                link(last)
                for t in range(TT):
                    last = V.max_index(topu[:, 8 * t:8 * t + 8], top[:, 8 * t:8 * t + 8], select[:, t * E:(t + 1) * E])
                link(last)
                link(V.tensor_copy(topi, topu[:, :]))
                hot4 = hot.rearrange("p (k t e) -> p k t e", k=K, t=TT)
                for q in range(K):
                    last = V.tensor_tensor(hot4[:, q], k("iota").unsqueeze(1).to_broadcast([128, TT, E]),
                                           topi[:, q:8 * TT:8].unsqueeze(2).to_broadcast([128, TT, E]), ALU.is_equal)
                link(last)
                link(V.tensor_reduce(cmpb, hot.rearrange("p (k x) -> p x k", k=K), AX.X, ALU.add))
                V.tensor_copy(chosen_b[:, :], cmpb).then_inc(chosen_rdy, 1)
                hot3, prod3 = hot.rearrange("p (k x) -> p k x", k=K), prod.rearrange("p (k x) -> p k x", k=K)
                link(V.tensor_tensor(prod3, hot3, score.unsqueeze(1).to_broadcast([128, K, TE]), ALU.mult))
                link(V.tensor_reduce(wk, prod.rearrange("p (n e) -> p n e", e=E), AX.X, ALU.add))
                link(V.tensor_reduce(wsum, wk.rearrange("p (k t) -> p t k", k=K), AX.X, ALU.add))
                link(V.reciprocal(wsum, wsum))
                link(V.scalar_tensor_tensor(wk.rearrange("p (k t) -> p k t", k=K), wk.rearrange("p (k t) -> p k t", k=K), ROUTED,
                                            wsum.unsqueeze(1).to_broadcast([128, K, TT]), ALU.mult, ALU.mult))
                dve.wait_ge(cnt_ps, i + 1)
                for n in range(BLOCKS - 1):
                    last = V.tensor_scalar(nbx[0:E, n:n + 1], bank(0)[0:E, 0:1], 128.0 * (n + 1), None, ALU.is_gt)
                link(last)
                link(V.tensor_reduce(nbx[0:E, 3:4], nbx[0:E, 0:3], AX.X, ALU.add))
                V.tensor_copy(extra_b[:, :], nbx[0:E, 3:4].to_broadcast([E, 128])).then_inc(nbx_rdy, 1)
                dve.wait_ge(end_ps, i + 1)
                link(V.tensor_copy(nbx[0:E, 0:1], bank(0)[0:E, 8:9]))
                V.tensor_scalar(passed_b[:, :], k("iota")[0:E, 0:XMAX], nbx[0:E, 0:1], None, ALU.is_ge).then_inc(passed_rdy, 1)
                bc = lambda ap: ap.unsqueeze(1).to_broadcast([128, TT, E])
                V.scalar_tensor_tensor(te(cmpa), te(bank(3)[:, 0:TE]), float(E), bc(k("iota")), ALU.mult, ALU.add)
                link(V.tensor_scalar(xrow, bank(3)[:, TE:TE + E], 128.0, 128.0 * (E - 1), ALU.mult, ALU.add))
                V.tensor_scalar(gtop, bank(3)[:, 0:TE], 127.5, None, ALU.is_gt)
                link(V.tensor_tensor(te(select), te(bank(3)[:, 0:TE]), bc(xrow), ALU.add))
                link(V.tensor_tensor(select, select, cmpa, ALU.subtract))
                link(V.tensor_tensor(select, select, gtop, ALU.mult))
                link(V.tensor_tensor(cmpa, cmpa, select, ALU.add))
                link(V.tensor_tensor(prod3, hot3, cmpa.unsqueeze(1).to_broadcast([128, K, TE]), ALU.mult))
                link(V.tensor_reduce(gtop[:, 0:K * TT], prod.rearrange("p (n e) -> p n e", e=E), AX.X, ALU.add))
                V.tensor_copy(row_i[:, :], gtop[:, 0:K * TT]).then_inc(rows_rdy, 1)
                dve.wait_ge(unit_ps, i + 1)
                V.tensor_scalar(unit_i[0:1, 0:XMAX], bank(0)[0:1, 16:16 + XMAX], float(E - 1), None, ALU.min)
                V.tensor_copy(unit_i[0:1, XMAX:XMAX + 1], bank(0)[0:1, 128:129]).then_inc(unit_rdy, 1)

                def product(w, b, par):
                    dve.wait_ge(m["gate_rdy"], w + 1)
                    if b:
                        dve.wait_ge(m["actT_ps"], w - 1)
                    V.tensor_tensor(act[par], gate[par], bank(6)[:, F:2 * F], ALU.mult).then_inc(m["act_rdy"], 1)

                def rows_out(u, par, w):
                    dve.wait_ge(m["xgT_ps"], u + 1)
                    dve.wait_ge(m["up_ps"], w)
                    V.tensor_copy(xgT[par].rearrange("p c t -> p (c t)"), bank(1, 2)).then_inc(m["xgT_ev"], 1)

                def act_out(w, b, par):
                    dve.wait_ge(m["actT_ps"], w + 1)
                    if b:
                        dve.wait_ge(m["dn_ps"], w - 1)
                    V.tensor_copy(actT[par].rearrange("p k t -> p (k t)"), bank(7)[:, 0:F]).then_inc(m["actT_ev"], 1)

                for w in range(TT):
                    product(w, w >= 2, w % 2)
                    act_out(w, w >= 2, w % 2)
                rows_out(0, 0, 0)
                product(TT, 1, 0)
                rows_out(1, 1, 0)
                act_out(TT, 1, 0)
                with nc.vector.Fori(0, E // 4 - 1) as g:
                    for r in range(4):
                        w = g * 4 + (TT + 1 + r)
                        product(w, 1, (1 + r) % 2)
                        rows_out(g * 4 + (2 + r), r % 2, g * 4 + (TT + 1 + r))
                        act_out(w, 1, (1 + r) % 2)
                for u in range(E - 3, E):
                    product(TT + u, 1, u % 2)
                    if u + 1 < E:
                        rows_out(u + 1, (u + 1) % 2, TT + u)
                    act_out(TT + u, 1, u % 2)
                total = nc.vector.value_load(unit_i[0:1, XMAX:XMAX + 1], min_val=0, max_val=XMAX)
                with nc.vector.If(total > 0):
                    dve.wait_ge(m["dn_ps"], TT + E)
                    with nc.vector.Fori(0, total) as j:
                        dve.wait_ge(m["t_xgT_ps"], j + 2)
                        V.tensor_copy(xgT[0].rearrange("p c t -> p (c t)"), bank(1, 2)).then_inc(m["t_xgT_ev"], 1)
                        dve.wait_ge(m["t_gate"], j + 1)
                        V.tensor_tensor(act[0], gate[0], bank(6)[:, F:2 * F], ALU.mult).then_inc(m["t_act"], 1)
                        dve.wait_ge(m["t_actT_ps"], j + 1)
                        V.tensor_copy(actT[0].rearrange("p k t -> p (k t)"), bank(7)[:, 0:F]).then_inc(m["t_actT_ev"], 1)
                dve.wait_ge(m["y_ev"], TT)
                for n in range(TT * K):
                    t, q = n // K, n % K
                    dve.wait_ge(comb_in[n % 6], 16 * (n // 6 + 1 + i * TT * K // 6))
                    if n:
                        dve.wait_ge(comb_used, n + i * TT * K)
                    V.scalar_tensor_tensor(acc[:, t, :], comb[n % 6], wk[:, q * TT + t:q * TT + t + 1], acc[:, t, :],
                                           ALU.mult, ALU.add).then_inc(comb_used, 1)
                for c in range(DC):
                    dve.wait_ge(acc_ps, c + 1 + i * DC)
                    V.scalar_tensor_tensor(xT[:, c, :], bank(c % 2), mod[i][:, 5, c, 0:1], xT[:, c, :], ALU.mult, ALU.add)\
                        .then_inc(res_ev, 1)
                dve.wait_ge(res_ev, DC + i * DC)

            moe(0)
            mod_out(1)
            norm(J_MIX1)
            for n in range(2):
                V.memset(up[n][:, 0:PAD], 0.0)
                V.memset(up[n][:, PAD + T:PT_], 0.0).then_inc(pad_rdy, 1)
            dve.wait_ge(pad_rdy, 2)
            for c in range(DC):
                dve.wait_ge(sig_rdy, c + 1)
                if c >= 2:
                    dve.wait_ge(tap_ps, c - 1)
                V.scalar_tensor_tensor(up[c % 2][:, PAD:PAD + T], bank(2 * (c % 2)), v("pw1b", c, c + 1), sg[c % 2],
                                       ALU.add, ALU.mult).then_inc(u_rdy, 1)
                dve.wait_ge(u_rdy, c + 1)
                tap = lambda q: v("dww", c * TAPS + q, c * TAPS + q + 1)
                link(V.tensor_scalar(conv[:, c, :], up[c % 2][:, PE_TAPS:PE_TAPS + T], tap(PE_TAPS), v("dwb", c, c + 1), ALU.mult, ALU.add))
                for q in range(PE_TAPS + 1, TAPS):
                    link(V.scalar_tensor_tensor(conv[:, c, :], up[c % 2][:, q:q + T], tap(q), conv[:, c, :], ALU.mult, ALU.add))
                dve.wait_ge(tap_ps, c + 1)
                V.tensor_tensor(conv[:, c, :], conv[:, c, :], bank(4 + c % 2), ALU.add).then_inc(cv_rdy, 1)
            dve.wait_ge(mean_ps, 1)
            dve.wait_ge(cv_rdy, DC)
            for c in range(DC):
                V.tensor_tensor(conv[:, c, :], conv[:, c, :], bank(6), ALU.subtract).then_inc(cent_rdy, 1)
            dve.wait_ge(cent_rdy, DC)
            norm(J_LN)
            for c in range(DC):
                dve.wait_ge(pw2_ps, c + 1)
                link(V.tensor_scalar(tmp[c % 2], bank(c % 2), v("pw2b", c, c + 1), mod[1][:, 2, c, 0:1], ALU.add, ALU.mult))
                V.tensor_tensor(xT[:, c, :], xT[:, c, :], tmp[c % 2], ALU.add).then_inc(pw2_ev, 1)
            dve.wait_ge(pw2_ev, DC)
            norm(J_FFN1)
            moe(1)
            norm(J_FIN)


def constants():
    c = np.zeros((128, NCST), np.float32)
    p = np.arange(128)

    def put(name, a):
        lo, hi = CST[name]
        c[:a.shape[0], lo:hi] = a

    put("ident", np.eye(128))
    put("sel", (p[:, None] % 32 == np.arange(2)[None]).astype(np.float32))
    put("iota", np.tile(np.arange(E), (128, 1)))
    put("before", np.tile((np.arange(G)[None, :] < np.arange(G)[:, None]).reshape(1, -1), (128, 1)))
    put("upper", (p[:, None] < p[None, :]))
    put("upto", (np.arange(E)[:, None] <= np.arange(E)[None, :]))
    put("tok", p[:, None] + 128 * np.arange(TT)[None])
    tok = np.arange(T, dtype=np.float32)
    row, col = np.floor(tok / 64), tok % 64
    inv = (np.float32(10000.0) ** (-np.arange(0, 16, 2, dtype=np.float32) / np.float32(16))).astype(np.float32)
    ang = np.concatenate([row[:, None] * inv, row[:, None] * inv, col[:, None] * inv, col[:, None] * inv], -1).T
    sign = np.where(np.arange(ROPE) % 16 < 8, -1.0, 1.0)[:, None]
    cos, sin = np.cos(ang.astype(np.float32)), np.sin(ang.astype(np.float32)) * sign
    put("rope", np.concatenate([cos, sin, cos, sin]))
    return c


SWAP = np.arange(ROPE) ^ 8


def kernel(**inputs):
    import concourse.bacc as _bacc
    from concourse import mybir as _mybir
    from concourse.bass_utils import run_bass_kernel_spmd as _run

    a = {n: np.asarray(x) for n, x in inputs.items()}

    def cols(x):
        return x.reshape(-1, 128).T

    def feats(x):
        return np.ascontiguousarray(x.T.reshape(DC, 128, -1).transpose(1, 0, 2))

    vec = np.concatenate([
        np.stack([cols(a["c"][0]), cols(a["c_ctx"])], -1).reshape(128, -1),
        cols(a["mod_b"][0]), cols(a["mod_b"][1]), cols(a["norm_mix_w"].reshape(-1)), cols(a["norm_ffn_w"].reshape(-1)),
        cols(a["mla_q_norm"][0]), cols(a["mla_kv_norm"][0]), cols(a["conv_pw1_b"][0]), cols(a["conv_dw_b"][0]),
        cols(a["conv_norm_w"][0]), cols(a["conv_norm_b"][0]), cols(a["conv_pw2_b"][0]), cols(a["final_norm_w"]),
        a["conv_dw_w"][0].T.reshape(DC, 128, TAPS).transpose(1, 0, 2).reshape(128, -1)], axis=1)
    wq_b = a["mla_wq_b"][0].reshape(QL, H, NOPE + ROPE)
    wq_b = np.concatenate([wq_b, wq_b[:, :, NOPE + SWAP]], axis=2).reshape(QL, H * 128)
    wkv_a = a["mla_wkv_a"][0]
    wkv_a = np.concatenate([wkv_a, wkv_a[:, KVL + SWAP]], axis=1)
    wkv_b = a["mla_wkv_b"][0].reshape(KVL, H // 2, 2, 2, NOPE).transpose(0, 1, 3, 2, 4).reshape(KVL, -1)
    ins = [feats(a["x"][0]), feats(a["ctx"][0]), vec, constants(), a["mod_w"], a["mla_wq_a"][0], wq_b, wkv_a, wkv_b,
           a["mla_wo"][0], a["conv_pw1_w"][0], a["conv_pw2_w"][0], a["router_w"], a["router_bias"], a["exp_w1"], a["exp_w3"],
           a["exp_w2"], a["shared_w1"], a["shared_w3"], a["shared_w2"]]
    nc = _bacc.Bacc("TRN2", target_bir_lowering=False, num_devices=1)
    arrays, args = {}, []
    for n, x in enumerate(ins):
        x = np.ascontiguousarray(x)
        arrays[f"in_{n}"] = x
        args.append(nc.dram_tensor(f"in_{n}", x.shape, _mybir.dt.from_np(x.dtype), kind="ExternalInput").ap())
    args.append(nc.dram_tensor("out_0", (128, DC, T), _mybir.dt.float32, kind="ExternalOutput").ap())
    build(nc, *args)
    r = _run(nc, [arrays], core_ids=[0])
    y = r.results[0]["out_0"]
    return np.ascontiguousarray(y.transpose(1, 0, 2).reshape(D, T).T).reshape(1, T, D)
```

```python
import concourse.bass as bass
from concourse import mybir
import numpy as np
from contextlib import ExitStack

D = 1024
T = 512
C = 256
H = 16
NOPE, ROPE, VD = 64, 32, 64
QL, KVL = 512, 256
E = 64
K = 6
G = 8
TOPG = 4
F = 256
TAPS = 31
PAD = TAPS // 2
DC = D // 128
TT = T // 128
KEYS = C + T
EPS = 1e-6
SM_SCALE = float(NOPE + ROPE) ** -0.5
ROUTED = 2.5
CAP = T
BLOCKS = CAP // 128
XMAX = T * K // 128
ROWS = 128 * (E + XMAX)
NONE = 1 << 20
SIDE_TAPS = 9

VEC = {}
_at = 0
for _n, _w in (("c", 2 * DC), ("modb", 96), ("nmix", 2 * DC), ("nffn", 2 * DC), ("qn", QL // 128),
               ("kvn", KVL // 128), ("pw1b", 2 * DC), ("dwb", DC), ("lnw", DC), ("lnb", DC), ("pw2b", DC),
               ("fin", DC), ("dww", DC * TAPS)):
    VEC[_n] = (_at, _at + _w)
    _at += _w
NVEC = _at
CST = {}
_at = 0
for _n, _w in (("ident", 128), ("sel", 2), ("iota", E), ("before", G * G), ("upper", 128), ("upto", E),
               ("tok", TT), ("rope", T)):
    CST[_n] = (_at, _at + _w)
    _at += _w
NCST = _at


def build(nc, xT_d, ctxT_d, vec_d, cst_d, mod_w, wq_a, wq_b, wkv_a, wkv_b, wo, pw1, pw2,
          router_w, router_bias, exp_w1, exp_w3, exp_w2, sh_w1, sh_w3, sh_w2, out):
    f32, bf16, i32, u32 = mybir.dt.float32, mybir.dt.bfloat16, mybir.dt.int32, mybir.dt.uint32
    ALU, ACT, AX = mybir.AluOpType, mybir.ActivationFunctionType, mybir.AxisListType
    ds = bass.ds
    L = 2

    h_rows = [nc.dram_tensor(f"h_rows{i}", (T, D), f32, kind="Internal").ap() for i in range(L)]
    y_rows = nc.dram_tensor("y_rows", (ROWS, D), f32, kind="Internal").ap()
    slots = [nc.dram_tensor(f"slots{i}", (ROWS, 1), i32, kind="Internal").ap() for i in range(L)]

    ctx = ExitStack()
    with ctx:
        def sb(name, shape, dt=f32):
            return ctx.enter_context(nc.sbuf_tensor(name, shape, dt))

        def sem(name):
            return ctx.enter_context(nc.semaphore(name))

        PS = ctx.enter_context(nc.psum_tensor("PS", [128, 8 * 512], f32))

        def bank(b, n=1):
            return PS[:, b * 512:(b + n) * 512]

        vec = sb("vec", [128, NVEC])
        cst = sb("cst", [128, NCST])
        xT = sb("xT", [128, DC, T])
        hT = sb("hT", [128, DC * KEYS])
        RING = 4
        SLOT = 3 * DC * F
        ring = sb("ring", [128, RING * SLOT])
        work = sb("work", [128, 12800])
        sq = sb("sq", [128, 2, T])
        rs = sb("rs", [128, T])
        small = sb("small", [128, 480])
        mean_w = sb("mean_w", [128, 128])
        upper_b = sb("upper_b", [128, 128], bf16)
        upto_b = sb("upto_b", [E, E], bf16)
        ones_b = sb("ones_b", [128, 128], bf16)
        chosen_b = sb("chosen_b", [128, TT * E], bf16)
        extra_b = sb("extra_b", [E, 128], bf16)
        zrow = sb("zrow", [128, 512])
        big_i = sb("big_i", [1, E], i32)
        passed_b = sb("passed_b", [E, XMAX], bf16)
        tok_i = sb("tok_i", [128, TT], i32)
        idx = sb("idx", [128, E + XMAX], i32)
        col_i = sb("col_i", [128, 2], i32)
        row_i = sb("row_i", [128, K * TT], i32)
        unit_i = sb("unit_i", [1, XMAX + 1], i32)
        cs = sb("cs", [128, DC, 32])
        mod = [sb(f"mod{i}", [128, 6, DC, 2]) for i in range(L)]
        modA = [sb(f"modA{i}", [128, 2, DC, 2]) for i in range(L)]
        smx = sb("smx", [128, 4, 3])
        zero = sb("zero", [128, 1])
        tick = sb("tick", [1, 16])
        eps = sb("eps", [128, 1])

        def v(name, a=0, b=None):
            lo, hi = VEC[name]
            return vec[:, lo + a:(lo + b if b is not None else hi)]

        def k(name, a=0, b=None):
            lo, hi = CST[name]
            return cst[:, lo + a:(lo + b if b is not None else hi)]

        ident = k("ident")

        MODBUF = 4
        mw = [ring[:, n * DC * 512:(n + 1) * DC * 512].rearrange("p (c f) -> p c f", c=DC) for n in range(MODBUF)]
        mrow = [work[:, n * 512:(n + 1) * 512] for n in range(2)]
        AW = 2 * 8192
        wqa_sb = ring[:, AW:AW + DC * QL].rearrange("p (c f) -> p c f", c=DC)
        KVW = KVL + 2 * ROPE
        wkva_sb = ring[:, AW + DC * QL:AW + DC * QL + DC * KVW].rearrange("p (c f) -> p c f", c=DC)
        wo_sb = ring[:, AW:AW + DC * D].rearrange("p (c f) -> p c f", c=DC)
        wqb_sb = ring[:, 0:8192].rearrange("p (c h f) -> p c h f", c=QL // 128, h=H)
        wkvb_sb = ring[:, 8192:12288].rearrange("p (c h f) -> p c h f", c=KVL // 128, h=H)
        P = [ring[:, 12288 + n * KEYS:12288 + (n + 1) * KEYS] for n in range(2)]
        rope_t = [ring[:, 13824 + n * 512:13824 + (n + 1) * 512] for n in range(2)]
        ctxT = work[:, 1024:1024 + DC * C].rearrange("p (c t) -> p c t", c=DC)
        o = [0]

        def take(n):
            o[0] += n
            return work[:, o[0] - n:o[0]]

        pT = take(2 * 6 * T).rearrange("p (h j t) -> p h j t", h=2, j=6)
        ckv = take(2 * KEYS).rearrange("p (c t) -> p c t", c=2)
        qa = take(4 * T).rearrange("p (c t) -> p c t", c=4)
        kT = [[take(KEYS) for _ in range(2)] for _ in range(2)]
        vv = [ring[:, 14848 + n * 768:14848 + (n + 1) * 768].rearrange("p (j f) -> p j f", j=6) for n in range(2)]
        hA = hT[:, :].rearrange("p (c t) -> p c t", c=DC)
        oT = hT[:, 0:DC * T].rearrange("p (c t) -> p c t", c=DC)
        qT = [[hT[:, DC * T + (2 * a + b) * T:DC * T + (2 * a + b + 1) * T] for b in range(2)] for a in range(2)]
        assert o[0] <= 12800
        hM = hT[:, 0:DC * T].rearrange("p (c t) -> p c t", c=DC)

        o[0] = 0
        acc = take(TT * D).rearrange("p (t d) -> p t d", t=TT)
        xg = [take(D) for _ in range(2)]
        both = take(2 * D)
        xgT = [both[:, n * D:(n + 1) * D].rearrange("p (c t) -> p c t", c=DC) for n in range(2)]
        yb = [take(D) for _ in range(2)]
        gate = [take(F) for _ in range(2)]
        act = [take(F) for _ in range(2)]
        actT = [take(F).rearrange("p (k t) -> p k t", k=2) for _ in range(2)]
        hot = both[:, 0:K * TT * E]
        scoreT = yb[0][0:E, 0:T]
        prod = work[:, 0:K * TT * E]
        comb = xg + [both[:, 0:D], both[:, D:2 * D]] + yb
        o2 = [0]

        def few(n):
            o2[0] += n
            return small[:, o2[0] - n:o2[0]]

        score = take(TT * E)
        select = take(TT * E)
        gtop = take(TT * G * 8)
        cmpa = take(TT * G * G)
        assert o[0] <= 12800
        gsum = few(TT * G)
        cmpb = few(TT * G * G)
        rank = few(TT * G)
        top = few(TT * 8)
        topi = few(TT * 8)
        wk = few(K * TT)
        wsum = few(TT)
        nbx = few(4)
        xrow = few(E)
        assert o2[0] <= 480
        topu = sb("topu", [128, TT * 8], u32)
        bias_sb = sb("bias_sb", [128, E])
        rw_sb = hT[:, DC * T:DC * T + DC * E].rearrange("p (c e) -> p c e", c=DC)

        def w13(s):
            return ring[:, s * SLOT:s * SLOT + 2 * DC * F].rearrange("p (a c f) -> p a c f", a=2, c=DC)

        def w2(s):
            return ring[:, s * SLOT + 2 * DC * F:(s + 1) * SLOT].rearrange("p (k d) -> p k d", k=2)

        pw1_sb = ring[:, 0:DC * 2 * D].rearrange("p (c f) -> p c f", c=DC)
        pw2_sb = ring[:, DC * 2 * D:DC * 3 * D].rearrange("p (c f) -> p c f", c=DC)
        PT_ = T + 2 * PAD
        up = [work[:, n * PT_:(n + 1) * PT_] for n in range(2)]
        CU = 2 * PT_
        conv = work[:, CU:CU + DC * T].rearrange("p (c t) -> p c t", c=DC)
        rest = [work[:, CU + DC * T + n * T:CU + DC * T + (n + 1) * T] for n in range(10)]
        sg, tmp, tap_prod, side = rest[0:2], rest[2:4], rest[4:8], rest[8:10]
        oF = conv

        cst_in, x_in, pool_cst, dve_cst, cs_rdy = (sem(n) for n in ("cst_in", "x_in", "pool_cst", "dve_cst", "cs_rdy"))
        modw_in = [sem(f"modw_in{n}") for n in range(MODBUF)]
        modrow_ps, modrow_sb, modcol_ps, mod_rdy = sem("modrow_ps"), sem("modrow_sb"), sem("modcol_ps"), sem("mod_rdy")
        sq_rdy, sq_used, rs_rdy, nrm_mul, nrm_out = (sem(n) for n in ("sq_rdy", "sq_used", "rs_rdy", "nrm_mul", "nrm_out"))
        aw_in, bw_in, wo_in = sem("aw_in"), sem("bw_in"), sem("wo_in")
        a_ps, a_ev, a_pe = sem("a_ps"), sem("a_ev"), sem("a_pe")
        lsq_rdy, lsq_used, lrs_rdy, lat_rdy = (sem(n) for n in ("lsq_rdy", "lsq_used", "lrs_rdy", "lat_rdy"))
        pj_ps, kv_ev, q_ev, q_rope = sem("pj_ps"), sem("kv_ev"), sem("q_ev"), sem("q_rope")
        s_ps, max_rdy, nmax_rdy, exp_rdy, p_rdy, pT_ps, pT_act, pT_dve, o_ps, o_ev = (
            sem(n) for n in ("s_ps", "max_rdy", "nmax_rdy", "exp_rdy", "p_rdy", "pT_ps", "pT_act", "pT_dve", "o_ps", "o_ev"))
        wo_ps, wo_ev = sem("wo_ps"), sem("wo_ev")
        std_rdy, lstd_rdy = sem("std_rdy"), sem("lstd_rdy")
        zero_out = sem("zero_out")
        den_rdy, dve_step = sem("den_rdy"), sem("dve_step")
        pw_in, glu_ps, sig_rdy, u_rdy, side_mul, side_add, cv_rdy, mean_ps, cent_rdy, pw2_ps, pw2_ev, pad_rdy = (
            sem(n) for n in ("pw_in", "glu_ps", "sig_rdy", "u_rdy", "side_mul", "side_add", "cv_rdy", "mean_ps",
                             "cent_rdy", "pw2_ps", "pw2_ev", "pad_rdy"))
        out_dn = sem("out_dn")

        (rw_in, logit_ps, scoreT_rdy, chosen_rdy, pos_ps, rows_rdy, none_rdy, none_set, slots_set,
         score_ps, idx_in, cnt_ps, nbx_rdy, end_ps, passed_rdy, unit_ps, unit_rdy, sh_in, xg_clr) = (
            sem(n) for n in ("rw_in", "logit_ps", "scoreT_rdy", "chosen_rdy", "pos_ps", "rows_rdy", "none_rdy", "none_set", "slots_set",
                             "score_ps", "idx_in", "cnt_ps", "nbx_rdy", "end_ps", "passed_rdy", "unit_ps", "unit_rdy", "sh_in", "xg_clr"))

        hd_out = [sem(f"hd_out{s}") for s in range(2)]
        comb_in = [sem(f"comb_in{s}") for s in range(6)]

        col_rdy, xgT_ps, xgT_ev = sem("col_rdy"), sem("xgT_ps"), sem("xgT_ev")
        xg_in = [sem(f"xg_in{s}") for s in range(2)]
        y_out = [sem(f"y_out{s}") for s in range(2)]
        hrow_ps, hrow_sb, comb_used, acc_ps, res_ev = (sem(n) for n in ("hrow_ps", "hrow_sb", "comb_used", "acc_ps", "res_ev"))

        M = []
        for i in range(L):
            m = {n: sem(f"{n}{i}") for n in (
                "up_ps", "gate_rdy", "act_rdy", "actT_ps", "actT_ev", "dn_ps", "y_ev", "t_w", "t_xg", "t_idx",
                "t_xgT_ps", "t_xgT_ev", "t_up", "t_gate", "t_act", "t_actT_ps", "t_actT_ev", "t_dn", "t_yev", "t_yout", "t_tick")}
            m["w_in"] = [sem(f"w_in{i}_{s}") for s in range(RING)]
            M.append(m)

        def jobs():
            a = lambda i, n, c, w: modA[i][:, n, c, w:w + 1]
            b = lambda i, n, c, w: mod[i][:, 3 * n, c, w:w + 1]
            xs = lambda c: xT[:, c, :]
            return [
                (lambda c: ctxT[:, c, :], lambda c: hA[:, c, 0:C], C, lambda c: a(0, 0, c, 1), lambda c: b(0, 0, c, 1), ACT.Identity),
                (xs, lambda c: hA[:, c, C:KEYS], T, lambda c: a(0, 0, c, 0), lambda c: b(0, 0, c, 0), ACT.Identity),
                (xs, lambda c: hM[:, c, :], T, lambda c: a(0, 1, c, 0), lambda c: b(0, 1, c, 0), ACT.Identity),
                (xs, lambda c: hM[:, c, :], T, lambda c: a(1, 0, c, 0), lambda c: b(1, 0, c, 0), ACT.Identity),
                (lambda c: conv[:, c, :], lambda c: hM[:, c, :], T, lambda c: v("lnw", c, c + 1), lambda c: v("lnb", c, c + 1), ACT.Silu),
                (xs, lambda c: hM[:, c, :], T, lambda c: a(1, 1, c, 0), lambda c: b(1, 1, c, 0), ACT.Identity),
                (xs, lambda c: oF[:, c, :], T, lambda c: v("fin", c, c + 1), lambda c: zero[:, 0:1], ACT.Identity),
            ]

        JOBS = jobs()
        J_CTX, J_X, J_FFN0, J_MIX1, J_LN, J_FFN1, J_FIN = range(7)
        NB = 3

        AG = [("kv", 0, C, 0), ("kv", 0, C, 1), ("pe", 0, C, 2), ("kv", C, T, 0), ("kv", C, T, 1), ("pe", C, T, 2)] + \
             [("q", C, T, m) for m in range(QL // 128)]
        LAT = [(1, C, [0, 1], lambda j: ckv[:, j, 0:C], "kvn"), (2, T, [3, 4], lambda j: ckv[:, j, C:KEYS], "kvn"),
               (0, T, [6, 7, 8, 9], lambda j: qa[:, j, :], "qn")]
        LSQ = [g for _, _, gs, _, _ in LAT for g in gs]
        NPAIR = H // 2
        NS = H * TT

        def pT_copy(eng, op, n, scalar):
            m, q, t = n // 8, (n // TT) % 2, n % TT
            eng.wait_ge(pT_ps, n + 1)
            if m:
                eng.wait_ge(o_ps, m)
            j0, j1 = (0, 4) if scalar else (4, 6)
            dst = pT[:, q, j0:j1, t * 128:(t + 1) * 128]
            src = bank(4, 2)[:, j0 * 128:j1 * 128].rearrange("p (j f) -> p j f", j=j1 - j0)
            if scalar:
                op(dst, src, ACT.Copy).then_inc(pT_act, 1)
            else:
                op(dst, src).then_inc(pT_dve, 1)

        block = ctx.enter_context(nc.Block())

        @block.sync
        def _(sp):
            sp.dma_start(cst[:, :], cst_d).then_inc(cst_in, 16)
            sp.dma_start(vec[:, :], vec_d).then_inc(cst_in, 16)
            sp.dma_start(xT[:, :, :], xT_d).then_inc(x_in, 16)
            sp.dma_start(ctxT, ctxT_d).then_inc(x_in, 16)

            def load_mod(i):
                for j in range(12):
                    n = 12 * i + j
                    if j >= MODBUF:
                        sp.wait_ge(modrow_ps, n - MODBUF + 1)
                    sp.dma_start(mw[n % MODBUF], mod_w[i, :, j * 512:(j + 1) * 512].rearrange("(c p) f -> p c f", p=128))\
                      .then_inc(modw_in[n % MODBUF], 16)

            def load_moe(i):
                m = M[i]
                sp.dma_start(rw_sb, router_w[i].rearrange("(c p) e -> p c e", p=128)).then_inc(rw_in, 16)
                sp.dma_start(bias_sb[:, :], router_bias[i].partition_broadcast(128)).then_inc(rw_in, 16)
                s = RING - 1
                sp.dma_start(w13(s)[:, 0], sh_w1[i].rearrange("(c p) f -> p c f", p=128)).then_inc(sh_in, 16)
                sp.dma_start(w13(s)[:, 1], sh_w3[i].rearrange("(c p) f -> p c f", p=128)).then_inc(sh_in, 16)
                sp.dma_start(w2(s), sh_w2[i].rearrange("(k p) d -> p k d", p=128)).then_inc(sh_in, 16)

                def expert(e, s, done):
                    sp.dma_start(w13(s)[:, 0], exp_w1[i, e].rearrange("o (p c) f -> p (o c) f", c=DC)).then_inc(done, 16)
                    sp.dma_start(w13(s)[:, 1], exp_w3[i, e].rearrange("o (p c) f -> p (o c) f", c=DC)).then_inc(done, 16)
                    sp.dma_start(w2(s), exp_w2[i, e].rearrange("o (k p) d -> p (o k) d", p=128)).then_inc(done, 16)

                for u in range(RING - 1):
                    expert(ds(u, 1), u, m["w_in"][u])
                sp.wait_ge(m["dn_ps"], TT)
                expert(ds(RING - 1, 1), RING - 1, m["w_in"][RING - 1])
                with nc.sync.Fori(0, E // RING - 1) as g:
                    for r in range(RING):
                        sp.wait_ge(m["dn_ps"], TT + 1 + r + g * RING)
                        expert(ds(g * RING + (RING + r), 1), r, m["w_in"][r])
                sp.wait_ge(unit_rdy, i + 1)
                total = nc.sync.value_load(unit_i[0:1, XMAX:XMAX + 1], min_val=0, max_val=XMAX)
                with nc.sync.If(total > 0):
                    with nc.sync.Fori(0, total) as j:
                        sp.wait_ge(m["dn_ps"], TT + E - 3)
                        sp.wait_ge(m["t_dn"], j + 1)
                        e = nc.sync.value_load(unit_i[0:1, ds(j, 1)], min_val=0, max_val=E - 1)
                        expert(ds(e, 1), 0, m["t_w"])

            load_mod(0)
            sp.dma_start(wqa_sb, wq_a.rearrange("(c p) f -> p c f", p=128)).then_inc(aw_in, 16)
            sp.dma_start(wkva_sb, wkv_a.rearrange("(c p) f -> p c f", p=128)).then_inc(aw_in, 16)
            sp.wait_ge(modrow_ps, 12)
            sp.dma_start(wqb_sb, wq_b.rearrange("(c p) (h f) -> p c h f", p=128, h=H)).then_inc(bw_in, 16)
            sp.dma_start(wkvb_sb, wkv_b.rearrange("(c p) (h f) -> p c h f", p=128, h=H)).then_inc(bw_in, 16)
            sp.wait_ge(a_ps, len(AG))
            sp.dma_start(wo_sb, wo.rearrange("(c p) f -> p c f", p=128)).then_inc(wo_in, 16)
            sp.wait_ge(wo_ps, DC)
            load_moe(0)
            sp.wait_ge(acc_ps, DC)
            load_mod(1)
            sp.wait_ge(modrow_ps, 24)
            sp.dma_start(pw1_sb, pw1.rearrange("(c p) f -> p c f", p=128)).then_inc(pw_in, 16)
            sp.dma_start(pw2_sb, pw2.rearrange("(c p) f -> p c f", p=128)).then_inc(pw_in, 16)
            sp.wait_ge(pw2_ps, DC)
            load_moe(1)
            sp.wait_ge(nrm_out, 8 * (J_FIN + 1))
            sp.dma_start(out, oF).then_inc(out_dn, 16)
            sp.wait_ge(out_dn, 16)

        @block.gpsimd
        def _(pool):
            nc.gpsimd.memset(ones_b[:, :], 1.0).then_inc(pool_cst, 1)
            nc.gpsimd.memset(mean_w[:, :], 1.0 / D).then_inc(pool_cst, 1)
            pool.wait_ge(cst_in, 32)
            nc.gpsimd.tensor_copy(upper_b[:, :], k("upper")).then_inc(pool_cst, 1)
            nc.gpsimd.tensor_copy(upto_b[:, :], k("upto")[0:E, :]).then_inc(pool_cst, 1)
            nc.gpsimd.tensor_copy(tok_i[:, :], k("tok")).then_inc(pool_cst, 1)

            def moe(i):
                m = M[i]
                pool.wait_ge(dve_cst, 1)
                nc.gpsimd.memset(idx[:, :], NONE).then_inc(none_rdy, 1)
                pool.wait_ge(none_rdy, i + 1)
                pool.dma_start(slots[i].rearrange("(p n) o -> p (n o)", p=128), idx[:, :]).then_inc(none_set, 16)
                pool.wait_ge(rows_rdy, i + 1)
                for n in range(2):
                    nc.gpsimd.memset(xg[n], 0.0).then_inc(xg_clr, 1)
                pool.wait_ge(none_set, 16 * (i + 1))
                for n in range(K * TT):
                    pool.indirect_dma_start(out=slots[i], out_offset=bass.IndirectOffsetOnAxis(ap=row_i[:, n:n + 1], axis=0),
                                            in_=tok_i[:, n % TT:n % TT + 1], in_offset=None).then_inc(slots_set, 16)
                pool.wait_ge(slots_set, 16 * K * TT * (i + 1))
                pool.dma_start(idx[:, 0:E], slots[i][0:128 * E, :].rearrange("(p e) o -> p (e o)", e=E)).then_inc(idx_in, 16)
                pool.wait_ge(idx_in, 16 * (i + 1))
                for s in range(2):
                    pool.wait_ge(hd_out[s], 32 + 32 * i)
                pool.wait_ge(xg_clr, 2 * (i + 1))

                def gather(u, n, done):
                    nc.gpsimd.tensor_copy(col_i[:, n:n + 1], idx[:, ds(u, 1)]).then_inc(col_rdy, 1)
                    pool.wait_ge(col_rdy, u + 1 + i * E)
                    nc.gpsimd.tensor_tensor(tick[0:1, 8 * i + 2:8 * i + 3], zero[0:1, 0:1], zero[0:1, 0:1], ALU.add)
                    big = nc.gpsimd.value_load(big_i[0:1, ds(u, 1)], min_val=0, max_val=1)

                    def rows(p):
                        pool.indirect_dma_start(out=xg[n][0:p], out_offset=None, in_=h_rows[i],
                                                in_offset=bass.IndirectOffsetOnAxis(ap=col_i[0:p, n:n + 1], axis=0),
                                                bounds_check=T - 1, oob_is_err=False).then_inc(done, 16)

                    with nc.gpsimd.If(big > 0):
                        rows(128)
                    with nc.gpsimd.Else():
                        rows(64)

                pool.wait_ge(unit_rdy, i + 1)
                gather(0, 0, xg_in[0])
                gather(1, 1, xg_in[1])
                with nc.gpsimd.Fori(0, E // 2 - 1) as g:
                    for r in range(2):
                        pool.wait_ge(xgT_ps, g * 2 + (1 + r) + i * E)
                        gather(g * 2 + (2 + r), r, xg_in[r])
                pool.wait_ge(xgT_ps, E - 1 + i * E)
                total = nc.gpsimd.value_load(unit_i[0:1, XMAX:XMAX + 1], min_val=0, max_val=XMAX)
                with nc.gpsimd.If(total > 0):
                    with nc.gpsimd.Fori(0, total) as j:
                        pool.wait_ge(m["t_xgT_ps"], j + 1)
                        nc.gpsimd.tensor_tensor(tick[0:1, 8 * i + 3:8 * i + 4], zero[0:1, 0:1], zero[0:1, 0:1], ALU.add)
                        pool.dma_start(idx[:, E:E + 1], slots[i][128 * E:ROWS, :].rearrange("(u p) o -> p u o", p=128)
                                       [:, ds(j, 1), :].rearrange("p u o -> p (u o)")).then_inc(m["t_idx"], 16)
                        pool.wait_ge(m["t_idx"], j * 16 + 16)
                        nc.gpsimd.tensor_tensor(tick[0:1, 8 * i + 6:8 * i + 7], zero[0:1, 0:1], zero[0:1, 0:1], ALU.add)
                        pool.indirect_dma_start(out=xg[0], out_offset=None, in_=h_rows[i],
                                                in_offset=bass.IndirectOffsetOnAxis(ap=idx[:, E:E + 1], axis=0),
                                                bounds_check=T - 1, oob_is_err=False).then_inc(m["t_xg"], 16)
                pool.wait_ge(zero_out, 32)
                for s in range(2):
                    pool.wait_ge(y_out[s], 32 * E // 2 + i * 16 * E)
                pool.wait_ge(m["dn_ps"], TT + E)
                with nc.gpsimd.If(total > 0):
                    pool.wait_ge(m["t_yout"], total * 16)
                    nc.gpsimd.tensor_tensor(tick[0:1, 8 * i + 4:8 * i + 5], zero[0:1, 0:1], zero[0:1, 0:1], ALU.add)
                for n in range(TT * K):
                    t, q = n // K, n % K
                    if n >= 6:
                        pool.wait_ge(comb_used, n - 5 + i * TT * K)
                    pool.indirect_dma_start(out=comb[n % 6], out_offset=None, in_=y_rows,
                                            in_offset=bass.IndirectOffsetOnAxis(ap=row_i[:, q * TT + t:q * TT + t + 1], axis=0))\
                        .then_inc(comb_in[n % 6], 16)

            pool.wait_ge(bw_in, 32)
            for n in range(2):
                pool.dma_start(y_rows[64 * E:ROWS, :].rearrange("(u p) (a d) -> p u a d", p=128, a=2)[:, :, n, :],
                               zrow[:, :].unsqueeze(1).to_broadcast([128, E // 2 + XMAX, 512])).then_inc(zero_out, 16)
            moe(0)
            for c in range(DC):
                for q in range(1, SIDE_TAPS):
                    n = c * SIDE_TAPS + q
                    pool.wait_ge(side_mul, n + 1)
                    if q == 1:
                        if c >= 2:
                            pool.wait_ge(cv_rdy, c - 1)
                        before = tap_prod[(n - 1) % 4]
                    else:
                        pool.wait_ge(side_add, n - c - 1)
                        before = side[c % 2]
                    nc.gpsimd.tensor_tensor(side[c % 2], before, tap_prod[n % 4], ALU.add).then_inc(side_add, 1)
            moe(1)

        @block.scalar
        def _(a):
            A = nc.scalar.activation
            a.wait_ge(cst_in, 32)
            a.wait_ge(dve_cst, 1)
            A(cs[:, :, 0:2], v("c").rearrange("p (c w) -> p c w", w=2), ACT.Silu).then_inc(cs_rdy, 1)

            def mod_rows(i):
                for j in range(12):
                    n = 12 * i + j
                    a.wait_ge(modrow_ps, n + 1)
                    if n >= 2:
                        a.wait_ge(modcol_ps, n - 1)
                    A(mrow[n % 2], bank(n % 2), ACT.Copy).then_inc(modrow_sb, 1)

            def norm(j):
                src, dst, w, sc, sh, fn = JOBS[j]
                for c in range(DC):
                    n = 8 * j + c
                    if n >= 2:
                        a.wait_ge(sq_used, n - 1)
                    A(sq[:, n % 2, 0:w], src(c), ACT.Square).then_inc(sq_rdy, 1)
                a.wait_ge(sq_used, 8 * (j + 1))
                if j:
                    a.wait_ge(nrm_mul, 8 * j)
                A(rs[:, 0:w], bank(NB)[:, 0:w], ACT.Sqrt, bias=eps[:, 0:1]).then_inc(std_rdy, 1)
                for c in range(DC):
                    a.wait_ge(nrm_mul, 8 * j + c + 1)
                    A(dst(c), dst(c), fn, bias=sh(c), scale=sc(c)).then_inc(nrm_out, 1)

            def moe(i):
                m = M[i]
                a.wait_ge(logit_ps, i + 1)
                A(scoreT, bank(0)[0:E, :], ACT.Sigmoid).then_inc(scoreT_rdy, 1)
                for t in range(TT):
                    a.wait_ge(hrow_ps, t + 1 + i * TT)
                    if t >= 2:
                        a.wait_ge(hd_out[t % 2], 16 + 32 * i)
                    A(yb[t % 2].rearrange("p (c q) -> p q c", c=DC),
                      bank(1 if t % 2 == 0 else 4, 2).rearrange("p (q c) -> p q c", c=DC), ACT.Copy).then_inc(hrow_sb, 1)
                    a.wait_ge(hrow_sb, t + 1 + i * TT)
                    a.dma_start(h_rows[i][t * 128:(t + 1) * 128, :], yb[t % 2]).then_inc(hd_out[t % 2], 16)

                def silu(w, b, par, big=True):
                    a.wait_ge(m["up_ps"], w + 1)
                    if b:
                        a.wait_ge(m["act_rdy"], w - 1)
                    if big:
                        A(gate[par], bank(6)[:, 0:F], ACT.Silu).then_inc(m["gate_rdy"], 1)
                    else:
                        A(gate[par][64:128], bank(6)[0:64, 0:F], ACT.Silu).then_inc(m["gate_rdy"], 1)

                def either(u, emit):
                    flag = nc.scalar.value_load(big_i[0:1, ds(u, 1)], min_val=0, max_val=1)
                    with nc.scalar.If(flag > 0):
                        emit(True)
                    with nc.scalar.Else():
                        emit(False)

                def store(u, wait_n, par, big):
                    a.wait_ge(m["dn_ps"], u + (TT + 1))
                    if not (isinstance(wait_n, int) and wait_n == 0):
                        a.wait_ge(y_out[par], wait_n + i * 16 * E)
                    if big:
                        A(yb[par], bank(4, 2), ACT.Copy).then_inc(m["y_ev"], 1)
                    else:
                        A(yb[par][:, 0:512], bank(4), ACT.Copy).then_inc(m["y_ev"], 1)
                    a.wait_ge(m["y_ev"], u + (TT + 1))
                    p = 128 if big else 64
                    rows = y_rows[0:p * E, :].rearrange("(p e) d -> p e d", e=E)
                    for half in range(2):
                        src = yb[par][:, half * 512:(half + 1) * 512] if big else yb[par][64 * half:64 * half + 64, 0:512]
                        a.dma_start(rows[:, ds(u, 1), half * 512:(half + 1) * 512].rearrange("p e d -> p (e d)"), src)\
                         .then_inc(y_out[par], 16)

                for w in range(TT):
                    silu(w, w >= 2, w % 2)
                    if w:
                        a.wait_ge(m["dn_ps"], w)
                        A(acc[:, w - 1, :], bank(4, 2), ACT.Copy).then_inc(m["y_ev"], 1)
                for s in range(2):
                    a.wait_ge(hd_out[s], 32 + 32 * i)
                a.wait_ge(unit_rdy, i + 1)
                a.wait_ge(zero_out, 32)
                either(0, lambda big: silu(TT, 1, 0, big))
                a.wait_ge(m["dn_ps"], TT)
                A(acc[:, TT - 1, :], bank(4, 2), ACT.Copy).then_inc(m["y_ev"], 1)
                for u in range(1, 5):
                    either(u, lambda big: silu(TT + u, 1, u % 2, big))
                    either(u - 1, lambda big: store(u - 1, 32 * ((u - 1) // 2), (u - 1) % 2, big))
                with nc.scalar.Fori(1, E // 4 - 1) as g:
                    for r in range(4):
                        either(g * 4 + (1 + r), lambda big: silu(g * 4 + (TT + 1 + r), 1, (1 + r) % 2, big))
                        either(g * 4 + r, lambda big: store(g * 4 + r, g * 64 + 32 * (r // 2), r % 2, big))
                for u in range(E - 3, E):
                    either(u, lambda big: silu(TT + u, 1, u % 2, big))
                    either(u - 1, lambda big: store(u - 1, 32 * ((u - 1) // 2), (u - 1) % 2, big))
                either(E - 1, lambda big: store(E - 1, 32 * ((E - 1) // 2), 1, big))
                a.sem_inc(m["t_yev"], 1)
                a.wait_ge(unit_rdy, i + 1)
                total = nc.scalar.value_load(unit_i[0:1, XMAX:XMAX + 1], min_val=0, max_val=XMAX)
                with nc.scalar.If(total > 0):
                    a.wait_ge(y_out[0], 32 * E // 2 + i * 16 * E)
                    with nc.scalar.Fori(0, total) as j:
                        a.wait_ge(m["t_up"], j + 1)
                        A(gate[0], bank(6)[:, 0:F], ACT.Silu).then_inc(m["t_gate"], 1)
                        a.wait_ge(m["t_dn"], j + 2)
                        A(yb[0], bank(4, 2), ACT.Copy).then_inc(m["t_yev"], 1)
                        a.wait_ge(m["t_yev"], j + 2)
                        a.dma_start(y_rows[128 * E:ROWS, :].rearrange("(u p) d -> p u d", p=128)[:, ds(j, 1), :]
                                    .rearrange("p u d -> p (u d)"), yb[0]).then_inc(m["t_yout"], 16)
                        a.wait_ge(m["t_yout"], j * 16 + 16)
                        A(tick[0:1, i:i + 1], zero[0:1, 0:1], ACT.Copy).then_inc(m["t_tick"], 1)

            mod_rows(0)
            a.wait_ge(x_in, 32)
            a.wait_ge(mod_rdy, 1)
            norm(J_CTX)
            norm(J_X)
            for s, g in enumerate(LSQ):
                kind, c0, w, blk = AG[g]
                a.wait_ge(a_ps, g + 1)
                if s >= 2:
                    a.wait_ge(lsq_used, s - 1)
                if kind == "kv":
                    A(ckv[:, blk, c0:c0 + w], bank(4 + g % 4)[:, 0:w], ACT.Copy)
                else:
                    A(qa[:, blk, :], bank(4 + g % 4), ACT.Copy)
                A(sq[:, s % 2, 0:w], bank(4 + g % 4)[:, 0:w], ACT.Square).then_inc(lsq_rdy, 1)
                for b, lw, gs, _, _ in LAT:
                    if g == gs[-1]:
                        a.wait_ge(lsq_used, s + 1)
                        if s >= len(gs):
                            a.wait_ge(lat_rdy, s + 1 - len(gs))
                        A(rs[:, 0:lw], bank(b)[:, 0:lw], ACT.Sqrt, bias=eps[:, 0:1], scale=D / (128.0 * len(gs))).then_inc(lstd_rdy, 1)

            def kv_out(m, part):
                n = 6 * m + part
                a.wait_ge(pj_ps, n + 1)
                if part == 0:
                    for q in range(2):
                        last = A(kT[m % 2][q][0:64, T:KEYS], bank(7)[64 * q:64 * q + 64, 0:C], ACT.Copy)
                elif part == 1:
                    for q in range(2):
                        last = A(kT[m % 2][q][0:64, 0:T], bank(6)[64 * q:64 * q + 64, :], ACT.Copy)
                elif part == 4:
                    last = A(vv[m % 2][:, 0:4, :], bank(7).rearrange("p (j f) -> p j f", j=4), ACT.Copy)
                else:
                    last = A(vv[m % 2][:, 4:6, :], bank(6)[:, 0:256].rearrange("p (j f) -> p j f", j=2), ACT.Copy)
                last.then_inc(kv_ev, 1)

            a.wait_ge(lat_rdy, 8)
            a.wait_ge(bw_in, 32)
            for part in (0, 1, 4, 5):
                kv_out(0, part)
            for n in range(NS):
                m, i8 = n // 8, n % 8
                a.wait_ge(nmax_rdy, n + 1)
                if n >= 2:
                    a.wait_ge(pT_ps, n - 1)
                A(P[n % 2], bank(2 * (n % 2), 2)[:, 0:KEYS], ACT.Exp, bias=smx[:, n % 4, 1:2], scale=SM_SCALE,
                  accum_out=smx[:, n % 4, 2:3]).then_inc(exp_rdy, 1)
                if m + 1 < NPAIR and i8 in (1, 2, 5, 6):
                    kv_out(m + 1, {1: 0, 2: 1, 5: 4, 6: 5}[i8])
                if n >= 1:
                    pT_copy(a, A, n - 1, True)
            pT_copy(a, A, NS - 1, True)
            a.wait_ge(wo_ev, DC)
            norm(J_FFN0)
            moe(0)
            mod_rows(1)
            a.wait_ge(res_ev, DC)
            a.wait_ge(mod_rdy, 2)
            norm(J_MIX1)
            def side_taps(c):
                a.wait_ge(u_rdy, c + 1)
                for q in range(SIDE_TAPS):
                    n = c * SIDE_TAPS + q
                    if n >= 4:
                        a.wait_ge(side_add, (n - 4) // SIDE_TAPS * (SIDE_TAPS - 1) + max(1, (n - 4) % SIDE_TAPS))
                    at = TAPS - SIDE_TAPS + q
                    A(tap_prod[n % 4], up[c % 2][:, at:at + T], ACT.Copy, scale=v("dww", c * TAPS + at, c * TAPS + at + 1))\
                        .then_inc(side_mul, 1)

            for c in range(DC):
                a.wait_ge(glu_ps, c + 1)
                if c >= 2:
                    a.wait_ge(u_rdy, c - 1)
                A(sg[c % 2], bank(2 * (c % 2) + 1), ACT.Sigmoid, bias=v("pw1b", DC + c, DC + c + 1)).then_inc(sig_rdy, 1)
                if c:
                    side_taps(c - 1)
            side_taps(DC - 1)
            a.wait_ge(cent_rdy, DC)
            norm(J_LN)
            a.wait_ge(pw2_ev, DC)
            norm(J_FFN1)
            moe(1)
            a.wait_ge(res_ev, 2 * DC)
            norm(J_FIN)

        @block.tensor
        def _(pe):
            mm, tr = nc.tensor.matmul, nc.tensor.transpose
            pe.wait_ge(pool_cst, 5)
            pe.wait_ge(cs_rdy, 1)

            def mod_cols(i):
                def columns(n):
                    pe.wait_ge(modrow_sb, n + 1)
                    for q in range(4):
                        at = 2 * (4 * (n % 12) + q)
                        last = mm(bank(2)[:, at:at + 2], mrow[n % 2][:, 128 * q:128 * q + 128], k("sel"), start=True, stop=True)
                    last.then_inc(modcol_ps, 1)

                for j in range(12):
                    n = 12 * i + j
                    pe.wait_ge(modw_in[n % MODBUF], 16 * (n // MODBUF + 1))
                    if n >= 2:
                        pe.wait_ge(modrow_sb, n - 1)
                    for c in range(DC):
                        t = c % 4
                        last = mm(bank(n % 2)[32 * t:32 * t + 32, :], cs[:, c, :], mw[n % MODBUF][:, c, :],
                                  start=(c < 4), stop=(c >= 4), tile_position=(0, 32 * t), skip_group_check=True)
                    last.then_inc(modrow_ps, 1)
                    if j:
                        columns(n - 1)
                columns(12 * i + 11)

            def norm(j):
                src, dst, w, sc, sh, fn = JOBS[j]
                if j:
                    pe.wait_ge(rs_rdy, j)
                for c in range(DC):
                    pe.wait_ge(sq_rdy, 8 * j + c + 1)
                    mm(bank(NB)[:, 0:w], mean_w[:, :], sq[:, c % 2, 0:w], start=(c == 0), stop=(c == DC - 1)).then_inc(sq_used, 1)

            mod_cols(0)
            norm(J_CTX)
            norm(J_X)
            pe.wait_ge(nrm_out, 16)
            pe.wait_ge(aw_in, 32)
            pe.wait_ge(rs_rdy, 2)

            def latent_sum(s):
                g = LSQ[s]
                b, w, gs, _, _ = [x for x in LAT if g in x[2]][0]
                pe.wait_ge(lsq_rdy, s + 1)
                mm(bank(b)[:, 0:w], mean_w[:, :], sq[:, s % 2, 0:w], start=(g == gs[0]),
                   stop=(g == gs[-1])).then_inc(lsq_used, 1)

            for g, (kind, c0, w, blk) in enumerate(AG):
                if g >= 4:
                    if AG[g - 4][0] == "pe":
                        pe.wait_ge(a_pe, (g - 4) // 3 + 1)
                    else:
                        pe.wait_ge(lsq_rdy, LSQ.index(g - 4) + 1)
                for c in range(DC):
                    if kind == "q":
                        lhs, M_ = wqa_sb[:, c, 128 * blk:128 * blk + 128], 128
                    elif kind == "kv":
                        lhs, M_ = wkva_sb[:, c, 128 * blk:128 * blk + 128], 128
                    else:
                        lhs, M_ = wkva_sb[:, c, KVL:KVW], 2 * ROPE
                    last = mm(bank(4 + g % 4)[0:M_, 0:w], lhs, hA[:, c, c0:c0 + w], start=(c == 0), stop=(c == DC - 1))
                last.then_inc(a_ps, 1)
                if g >= 1 and g - 1 in LSQ:
                    latent_sum(LSQ.index(g - 1))
            latent_sum(len(LSQ) - 1)

            def project(m, part):
                if part == 0 and m:
                    pe.wait_ge(kv_ev, 4 * m - 1)
                elif part == 1 and m:
                    pe.wait_ge(kv_ev, 4 * m)
                    pe.wait_ge(o_ev, m - 1)
                elif part == 2:
                    pe.wait_ge(kv_ev, 4 * m + 1)
                elif part == 3:
                    pe.wait_ge(kv_ev, 4 * m + 2)
                elif part == 4:
                    pe.wait_ge(q_ev, 2 * m + 1)
                elif part == 5:
                    pe.wait_ge(q_ev, 2 * m + 2)
                if part < 2:
                    b, w, c0 = ((7, C, T), (6, T, 0))[part]
                    for c in range(2):
                        last = mm(bank(b)[:, 0:w], wkvb_sb[:, c, 2 * m, :], ckv[:, c, c0:c0 + w],
                                  start=(c == 0), stop=(c == 1))
                elif part < 4:
                    for c in range(4):
                        last = mm(bank(7 if part == 2 else 6), wqb_sb[:, c, 2 * m + part - 2, :], qa[:, c, :],
                                  start=(c == 0), stop=(c == 3))
                else:
                    for j in (range(4) if part == 4 else range(4, 6)):
                        for c in range(2):
                            last = mm(bank(7 if part == 4 else 6)[:, (j % 4) * 128:(j % 4) * 128 + 128],
                                      ckv[:, c, j * 128:(j + 1) * 128], wkvb_sb[:, c, 2 * m + 1, :],
                                      start=(c == 0), stop=(c == 1))
                last.then_inc(pj_ps, 1)

            def scores(n):
                m, q, t = n // 8, (n // TT) % 2, n % TT
                pe.wait_ge(kv_ev, 4 * m + 2)
                pe.wait_ge(q_ev, 2 * m + 1 + q)
                if n >= 2:
                    pe.wait_ge(exp_rdy, n - 1)
                for c0, w in ((0, 512), (512, 256)):
                    last = mm(bank(2 * (n % 2), 2)[:, c0:c0 + w], qT[m % 2][q][0:96, t * 128:(t + 1) * 128],
                              kT[m % 2][q][0:96, c0:c0 + w], start=True, stop=True)
                last.then_inc(s_ps, 1)

            def turn(n):
                pe.wait_ge(p_rdy, n + 1)
                if n:
                    pe.wait_ge(pT_act, n)
                    pe.wait_ge(pT_dve, n)
                for j in range(6):
                    last = tr(bank(4, 2)[:, j * 128:(j + 1) * 128], P[n % 2][:, j * 128:(j + 1) * 128], ident)
                last.then_inc(pT_ps, 1)

            pe.wait_ge(lat_rdy, 8)
            pe.wait_ge(bw_in, 32)
            for part in range(6):
                project(0, part)
            scores(0)
            for n in range(NS):
                m, i8 = n // 8, n % 8
                if n + 1 < NS:
                    scores(n + 1)
                if m + 1 < NPAIR and i8 < 6:
                    project(m + 1, i8)
                turn(n)
                if i8 == 7:
                    pe.wait_ge(pT_act, n + 1)
                    pe.wait_ge(pT_dve, n + 1)
                    pe.wait_ge(kv_ev, 4 * min(m + 2, NPAIR))
                    for j in range(6):
                        for q in range(2):
                            last = mm(bank(6)[64 * q:64 * q + 64, :], vv[m % 2][:, j, 64 * q:64 * q + 64], pT[:, q, j, :],
                                      start=(j == 0), stop=(j == 5), tile_position=(0, 64 * q), skip_group_check=True)
                    last.then_inc(o_ps, 1)
            pe.wait_ge(o_ev, NPAIR)
            pe.wait_ge(wo_in, 16)
            for n in range(DC):
                if n >= 2:
                    pe.wait_ge(wo_ev, n - 1)
                for c in range(DC):
                    last = mm(bank(n % 2), wo_sb[:, c, n * 128:(n + 1) * 128], oT[:, c, :], start=(c == 0), stop=(c == DC - 1))
                last.then_inc(wo_ps, 1)

            def moe(i):
                m = M[i]
                pe.wait_ge(rw_in, 32 * (i + 1))
                for c in range(DC):
                    last = mm(bank(0)[0:E, :], rw_sb[:, c, :], hM[:, c, :], start=(c == 0), stop=(c == DC - 1))
                last.then_inc(logit_ps, 1)
                for t in range(TT):
                    if t == 0:
                        pe.wait_ge(scoreT_rdy, i + 1)
                    last = tr(bank(3)[:, t * E:(t + 1) * E], scoreT[:, t * 128:(t + 1) * 128], ident[0:E, 0:E])
                last.then_inc(score_ps, 1)
                for t in range(TT):
                    if t >= 2:
                        pe.wait_ge(hrow_sb, t - 1 + i * TT)
                    for c in range(DC):
                        last = tr(bank(1 if t % 2 == 0 else 4, 2)[:, c * 128:(c + 1) * 128], hM[:, c, t * 128:(t + 1) * 128], ident)
                    last.then_inc(hrow_ps, 1)
                pe.wait_ge(chosen_rdy, i + 1)
                for t in range(TT):
                    for s in range(t + 1):
                        last = mm(bank(3)[:, t * E:(t + 1) * E], upper_b[:, :] if s == t else ones_b[:, :],
                                  chosen_b[:, s * E:(s + 1) * E], start=(s == 0), stop=(s == t))
                last.then_inc(pos_ps, 1)
                for t in range(TT):
                    last = mm(bank(0)[0:E, 0:1], chosen_b[:, t * E:(t + 1) * E], ones_b[:, 0:1], start=(t == 0), stop=(t == TT - 1))
                for t in range(TT):
                    last = mm(bank(0)[0:1, 256:256 + E], ones_b[:, 0:1], chosen_b[:, t * E:(t + 1) * E], start=(t == 0), stop=(t == TT - 1))
                last.then_inc(cnt_ps, 1)
                pe.wait_ge(nbx_rdy, i + 1)
                mm(bank(0)[0:E, 8:9], upto_b[:, :], extra_b[:, 0:1], start=True, stop=True)
                mm(bank(3)[:, TT * E:(TT + 1) * E], extra_b[:, :], upper_b[0:E, 0:E], start=True, stop=True).then_inc(end_ps, 1)
                pe.wait_ge(passed_rdy, i + 1)
                mm(bank(0)[0:1, 16:16 + XMAX], ones_b[0:E, 0:1], passed_b[:, :], start=True, stop=True)
                mm(bank(0)[0:1, 128:129], extra_b[:, 0:1], ones_b[0:E, 0:1], start=True, stop=True).then_inc(unit_ps, 1)

                def up_mm(lhs, s):
                    for c in range(DC):
                        last = mm(bank(6), lhs(c), w13(s)[:, :, c, :], start=(c == 0), stop=(c == DC - 1))
                    return last

                def up_small(lhs, s):
                    for c in range(DC):
                        for q in range(2):
                            last = mm(bank(6)[64 * q:64 * q + 64, 0:F], lhs(c)[:, 0:64], w13(s)[:, q, c, :], start=(c == 0),
                                      stop=(c == DC - 1), tile_position=(0, 64 * q), skip_group_check=True)
                    return last

                def down_small(par, s):
                    for kk in range(2):
                        for q in range(2):
                            last = mm(bank(4)[64 * q:64 * q + 64, :], actT[par][:, kk, 0:64], w2(s)[:, kk, q * 512:(q + 1) * 512],
                                      start=(kk == 0), stop=(kk == 1), tile_position=(0, 64 * q), skip_group_check=True)
                    return last

                def either(u, emit):
                    flag = nc.tensor.value_load(big_i[0:1, ds(u, 1)], min_val=0, max_val=1)
                    with nc.tensor.If(flag > 0):
                        emit(True)
                    with nc.tensor.Else():
                        emit(False)

                def down_mm(par, s):
                    for half in range(2):
                        for kk in range(2):
                            last = mm(bank(4 + half), actT[par][:, kk, :], w2(s)[:, kk, half * 512:(half + 1) * 512],
                                      start=(kk == 0), stop=(kk == 1))
                    return last

                def act_tr(par):
                    for kk in range(2):
                        last = tr(bank(7)[:, kk * 128:(kk + 1) * 128], act[par][:, kk * 128:(kk + 1) * 128], ident)
                    return last

                def rows_tr(par):
                    for c in range(DC):
                        last = tr(bank(1, 2)[:, c * 128:(c + 1) * 128], xg[par][:, c * 128:(c + 1) * 128], ident)
                    return last

                def up(w, lhs, s, big=True):
                    pe.wait_ge(m["act_rdy"], w)
                    (up_mm if big else up_small)(lhs, s).then_inc(m["up_ps"], 1)

                def down(w, par, s, big=True):
                    pe.wait_ge(m["actT_ev"], w + 1)
                    pe.wait_ge(m["y_ev"], w)
                    (down_mm if big else down_small)(par, s).then_inc(m["dn_ps"], 1)

                def turn_act(w, par):
                    pe.wait_ge(m["act_rdy"], w + 1)
                    pe.wait_ge(m["actT_ev"], w)
                    act_tr(par).then_inc(m["actT_ps"], 1)

                def turn_rows(u, n_in, par):
                    pe.wait_ge(xg_in[par], n_in + i * 8 * E)
                    pe.wait_ge(xgT_ev, u + i * E)
                    rows_tr(par).then_inc(xgT_ps, 1)

                pe.wait_ge(sh_in, 48 * (i + 1))
                pe.wait_ge(hrow_sb, TT + i * TT)
                for w in range(TT):
                    up(w, lambda c, w=w: hM[:, c, w * 128:(w + 1) * 128], RING - 1)
                    if w:
                        down(w - 1, (w - 1) % 2, RING - 1)
                    turn_act(w, w % 2)
                pe.wait_ge(unit_rdy, i + 1)
                pe.sem_inc(m["t_dn"], 1)
                pe.sem_inc(m["t_xgT_ps"], 1)
                turn_rows(0, 16, 0)
                pe.wait_ge(xgT_ev, 1 + i * E)
                pe.wait_ge(m["w_in"][0], 48)
                either(0, lambda big: up(TT, lambda c: xgT[0][:, c, :], 0, big))
                turn_rows(1, 16, 1)
                down(TT - 1, 1, RING - 1)
                turn_act(TT, 0)

                def unit(u, slot, n_w, n_next, par):
                    w = u + TT
                    pe.wait_ge(xgT_ev, u + 1 + i * E)
                    pe.wait_ge(m["w_in"][slot], n_w)
                    either(u, lambda big: up(w, lambda c: xgT[par][:, c, :], slot, big))
                    if n_next is not None:
                        turn_rows(u + 1, n_next, 1 - par)
                    either(u - 1, lambda big: down(w - 1, 1 - par, (slot - 1) % RING, big))
                    turn_act(w, par)

                with nc.tensor.Fori(0, E // 4 - 1) as g:
                    for r in range(4):
                        unit(g * 4 + (1 + r), (1 + r) % 4, g * 48 + 48 * ((1 + r) // 4 + 1), g * 32 + 16 * ((2 + r) // 2 + 1), (1 + r) % 2)
                for u in range(E - 3, E):
                    unit(u, u % 4, 48 * (u // 4 + 1), 16 * ((u + 1) // 2 + 1) if u + 1 < E else None, u % 2)
                either(E - 1, lambda big: down(TT + E - 1, 1, RING - 1, big))
                total = nc.tensor.value_load(unit_i[0:1, XMAX:XMAX + 1], min_val=0, max_val=XMAX)
                with nc.tensor.If(total > 0):
                    with nc.tensor.Fori(0, total) as j:
                        pe.wait_ge(m["t_xg"], j * 16 + 16)
                        rows_tr(0).then_inc(m["t_xgT_ps"], 1)
                        pe.wait_ge(m["t_xgT_ev"], j + 1)
                        pe.wait_ge(m["t_w"], j * 48 + 48)
                        up_mm(lambda c: xgT[0][:, c, :], 0).then_inc(m["t_up"], 1)
                        pe.wait_ge(m["t_act"], j + 1)
                        act_tr(0).then_inc(m["t_actT_ps"], 1)
                        pe.wait_ge(m["t_actT_ev"], j + 1)
                        pe.wait_ge(m["t_yev"], j + 1)
                        pe.wait_ge(m["y_ev"], TT + E)
                        down_mm(0, 0).then_inc(m["t_dn"], 1)
                pe.wait_ge(comb_used, TT * K + i * TT * K)
                for c in range(DC):
                    if c >= 2:
                        pe.wait_ge(res_ev, c - 1 + i * DC)
                    for t in range(TT):
                        last = tr(bank(c % 2)[:, t * 128:(t + 1) * 128], acc[:, t, c * 128:(c + 1) * 128], ident)
                    last.then_inc(acc_ps, 1)

            norm(J_FFN0)
            pe.wait_ge(nrm_out, 8 * (J_FFN0 + 1))
            moe(0)
            pe.wait_ge(res_ev, DC)
            mod_cols(1)
            norm(J_MIX1)
            pe.wait_ge(nrm_out, 8 * (J_MIX1 + 1))
            pe.wait_ge(pw_in, 32)
            pe.wait_ge(mod_rdy, 2)

            for c in range(DC):
                if c >= 2:
                    pe.wait_ge(u_rdy, c - 1)
                for half in range(2):
                    for kk in range(DC):
                        last = mm(bank(2 * (c % 2) + half), pw1_sb[:, kk, half * D + c * 128:half * D + (c + 1) * 128], hM[:, kk, :],
                                  start=(kk == 0), stop=(kk == DC - 1))
                last.then_inc(glu_ps, 1)
            for c in range(DC):
                pe.wait_ge(cv_rdy, c + 1)
                last = mm(bank(6), mean_w[:, :], conv[:, c, :], start=(c == 0), stop=(c == DC - 1))
            last.then_inc(mean_ps, 1)
            norm(J_LN)
            pe.wait_ge(nrm_out, 8 * (J_LN + 1))
            for n in range(DC):
                if n >= 2:
                    pe.wait_ge(pw2_ev, n - 1)
                for c in range(DC):
                    last = mm(bank(n % 2), pw2_sb[:, c, n * 128:(n + 1) * 128], hM[:, c, :], start=(c == 0), stop=(c == DC - 1))
                last.then_inc(pw2_ps, 1)
            norm(J_FFN1)
            pe.wait_ge(nrm_out, 8 * (J_FFN1 + 1))
            moe(1)
            norm(J_FIN)

        @block.vector
        def _(dve):
            V = nc.vector
            step = [0]

            def link(ins):
                step[0] += 1
                ins.then_inc(dve_step, 1)
                dve.wait_ge(dve_step, step[0])

            V.memset(cs[:, :, :], 0.0)
            V.memset(eps[:, :], EPS)
            V.memset(zrow[:, :], 0.0)
            V.memset(zero[:, :], 0.0).then_inc(dve_cst, 1)

            def mod_out(i):
                dve.wait_ge(cst_in, 32)
                dve.wait_ge(modcol_ps, 12 * (i + 1))
                for w in range(2):
                    last = V.tensor_tensor(mod[i][:, :, :, w].rearrange("p s c -> p (s c)"), bank(2)[:, w:96:2],
                                           v("modb", 48 * i, 48 * i + 48), ALU.add)
                link(last)
                for n, g in ((0, "nmix"), (1, "nffn")):
                    for w in range(2):
                        last = V.scalar_tensor_tensor(modA[i][:, n, :, w], mod[i][:, 3 * n + 1, :, w], 1.0,
                                                      v(g, DC * i, DC * i + DC), ALU.add, ALU.mult)
                last.then_inc(mod_rdy, 1)

            def norm(j):
                src, dst, w, sc, sh, fn = JOBS[j]
                dve.wait_ge(std_rdy, j + 1)
                V.reciprocal(rs[:, 0:w], rs[:, 0:w]).then_inc(rs_rdy, 1)
                dve.wait_ge(rs_rdy, j + 1)
                for c in range(DC):
                    V.tensor_tensor(dst(c), src(c), rs[:, 0:w], ALU.mult).then_inc(nrm_mul, 1)

            mod_out(0)
            dve.wait_ge(x_in, 32)
            norm(J_CTX)
            norm(J_X)
            dve.wait_ge(nrm_out, 16)
            dve.wait_ge(a_ps, 3)
            for a_ in range(2):
                for b_ in range(2):
                    last = V.tensor_copy(kT[a_][b_][64:96, 0:C], bank(4 + 2)[0:ROPE, 0:C])
            last.then_inc(a_pe, 1)
            rope_x = bank(4 + 5 % 4)
            dve.wait_ge(a_ps, 6)
            V.tensor_tensor(rope_t[0][0:32, :], rope_x[0:32, :], k("rope")[0:32, :], ALU.mult)
            link(V.tensor_tensor(rope_t[1][0:32, :], rope_x[32:64, :], k("rope")[32:64, :], ALU.mult))
            for a_ in range(2):
                for b_ in range(2):
                    last = V.tensor_tensor(kT[a_][b_][64:96, C:KEYS], rope_t[0][0:32, :], rope_t[1][0:32, :], ALU.add)
            last.then_inc(a_pe, 1)
            for J, (b, w, gs, lat, gain) in enumerate(LAT):
                dve.wait_ge(lstd_rdy, J + 1)
                V.reciprocal(rs[:, 0:w], rs[:, 0:w]).then_inc(lrs_rdy, 1)
                dve.wait_ge(lrs_rdy, J + 1)
                for j in range(len(gs)):
                    V.scalar_tensor_tensor(lat(j), lat(j), v(gain, j, j + 1), rs[:, 0:w], ALU.mult, ALU.mult).then_inc(lat_rdy, 1)

            dve.wait_ge(lat_rdy, 8)

            def q_out(m, q):
                b = bank(7 if q == 0 else 6)
                dve.wait_ge(pj_ps, 6 * m + 3 + q)
                dve.wait_ge(q_ev, 2 * m + q)
                dst = qT[m % 2][q]
                V.tensor_copy(dst[0:64, :], b[0:64, :])
                V.tensor_tensor(rope_t[0][64:96, :], b[64:96, :], k("rope")[64:96, :], ALU.mult)
                V.tensor_tensor(rope_t[1][64:96, :], b[96:128, :], k("rope")[96:128, :], ALU.mult).then_inc(q_rope, 1)
                dve.wait_ge(q_rope, 2 * m + q + 1)
                V.tensor_tensor(dst[64:96, :], rope_t[0][64:96, :], rope_t[1][64:96, :], ALU.add).then_inc(q_ev, 1)

            q_out(0, 0)
            q_out(0, 1)

            def top_score(n):
                dve.wait_ge(s_ps, n + 1)
                if n >= 4:
                    dve.wait_ge(p_rdy, n - 3)
                V.tensor_reduce(smx[:, n % 4, 0:1], bank(2 * (n % 2), 2)[:, 0:KEYS], AX.X, ALU.max).then_inc(max_rdy, 1)
                dve.wait_ge(max_rdy, n + 1)
                V.tensor_scalar(smx[:, n % 4, 1:2], smx[:, n % 4, 0:1], -SM_SCALE, None, ALU.mult).then_inc(nmax_rdy, 1)

            def divide(n):
                dve.wait_ge(exp_rdy, n + 1)
                V.reciprocal(smx[:, n % 4, 0:1], smx[:, n % 4, 2:3]).then_inc(den_rdy, 1)
                dve.wait_ge(den_rdy, n + 1)
                V.tensor_scalar(P[n % 2], P[n % 2], smx[:, n % 4, 0:1], None, ALU.mult).then_inc(p_rdy, 1)

            top_score(0)
            for n in range(NS):
                m, i8 = n // 8, n % 8
                divide(n)
                if n + 1 < NS:
                    top_score(n + 1)
                if m + 1 < NPAIR and i8 in (3, 4):
                    q_out(m + 1, i8 - 3)
                if i8 == 0 and m:
                    dve.wait_ge(o_ps, m)
                    V.tensor_copy(oT[:, m - 1, :], bank(6)).then_inc(o_ev, 1)
                pT_copy(dve, V.tensor_copy, n, False)
            dve.wait_ge(o_ps, NPAIR)
            V.tensor_copy(oT[:, NPAIR - 1, :], bank(6)).then_inc(o_ev, 1)
            for n in range(DC):
                dve.wait_ge(wo_ps, n + 1)
                V.scalar_tensor_tensor(xT[:, n, :], bank(n % 2), mod[0][:, 2, n, 0:1], xT[:, n, :], ALU.mult, ALU.add).then_inc(wo_ev, 1)
            dve.wait_ge(wo_ev, DC)
            norm(J_FFN0)

            def moe(i):
                m = M[i]
                TE = TT * E
                te = lambda ap: ap.rearrange("p (t e) -> p t e", t=TT)
                dve.wait_ge(score_ps, i + 1)
                link(V.tensor_copy(score, bank(3)[:, 0:TE]))
                dve.wait_ge(rw_in, 32 * (i + 1))
                link(V.tensor_tensor(te(select), te(score), bias_sb[:, :].unsqueeze(1).to_broadcast([128, TT, E]), ALU.add))
                for n in range(TT * G):
                    last = V.max(gtop[:, 8 * n:8 * n + 8], select[:, 8 * n:8 * n + 8])
                link(last)
                link(V.tensor_tensor(gsum, gtop[:, 0:8 * TT * G:8], gtop[:, 1:8 * TT * G:8], ALU.add))
                gs3 = gsum.rearrange("p (t g) -> p t g", t=TT)
                one = gs3.unsqueeze(3).to_broadcast([128, TT, G, G])
                other = gs3.unsqueeze(2).to_broadcast([128, TT, G, G])
                g4 = lambda ap: ap.rearrange("p (t g h) -> p t g h", t=TT, g=G)
                V.tensor_tensor(g4(cmpa), other, one, ALU.is_gt)
                link(V.tensor_tensor(g4(cmpb), other, one, ALU.is_equal))
                link(V.tensor_tensor(cmpb.rearrange("p (t x) -> p t x", t=TT), cmpb.rearrange("p (t x) -> p t x", t=TT),
                                     k("before").unsqueeze(1).to_broadcast([128, TT, G * G]), ALU.mult))
                link(V.tensor_tensor(cmpa, cmpa, cmpb, ALU.add))
                link(V.tensor_reduce(rank, cmpa.rearrange("p (n h) -> p n h", h=G), AX.X, ALU.add))
                link(V.tensor_scalar(rank, rank, TOPG - 0.5, -3e38, ALU.is_gt, ALU.mult))
                link(V.tensor_tensor(select.rearrange("p (n e) -> p n e", e=G), select.rearrange("p (n e) -> p n e", e=G),
                                     rank.unsqueeze(2).to_broadcast([128, TT * G, G]), ALU.add))
                for t in range(TT):
                    last = V.max(top[:, 8 * t:8 * t + 8], select[:, t * E:(t + 1) * E])
                link(last)
                for t in range(TT):
                    last = V.max_index(topu[:, 8 * t:8 * t + 8], top[:, 8 * t:8 * t + 8], select[:, t * E:(t + 1) * E])
                link(last)
                link(V.tensor_copy(topi, topu[:, :]))
                hot4 = hot.rearrange("p (k t e) -> p k t e", k=K, t=TT)
                for q in range(K):
                    last = V.tensor_tensor(hot4[:, q], k("iota").unsqueeze(1).to_broadcast([128, TT, E]),
                                           topi[:, q:8 * TT:8].unsqueeze(2).to_broadcast([128, TT, E]), ALU.is_equal)
                link(last)
                link(V.tensor_reduce(cmpb, hot.rearrange("p (k x) -> p x k", k=K), AX.X, ALU.add))
                V.tensor_copy(chosen_b[:, :], cmpb).then_inc(chosen_rdy, 1)
                hot3, prod3 = hot.rearrange("p (k x) -> p k x", k=K), prod.rearrange("p (k x) -> p k x", k=K)
                link(V.tensor_tensor(prod3, hot3, score.unsqueeze(1).to_broadcast([128, K, TE]), ALU.mult))
                link(V.tensor_reduce(wk, prod.rearrange("p (n e) -> p n e", e=E), AX.X, ALU.add))
                link(V.tensor_reduce(wsum, wk.rearrange("p (k t) -> p t k", k=K), AX.X, ALU.add))
                link(V.reciprocal(wsum, wsum))
                link(V.scalar_tensor_tensor(wk.rearrange("p (k t) -> p k t", k=K), wk.rearrange("p (k t) -> p k t", k=K), ROUTED,
                                            wsum.unsqueeze(1).to_broadcast([128, K, TT]), ALU.mult, ALU.mult))
                dve.wait_ge(cnt_ps, i + 1)
                for n in range(BLOCKS - 1):
                    last = V.tensor_scalar(nbx[0:E, n:n + 1], bank(0)[0:E, 0:1], 128.0 * (n + 1), None, ALU.is_gt)
                link(last)
                V.tensor_scalar(big_i[0:1, :], bank(0)[0:1, 256:256 + E], 64.5, None, ALU.is_gt)
                link(V.tensor_reduce(nbx[0:E, 3:4], nbx[0:E, 0:3], AX.X, ALU.add))
                V.tensor_copy(extra_b[:, :], nbx[0:E, 3:4].to_broadcast([E, 128])).then_inc(nbx_rdy, 1)
                dve.wait_ge(end_ps, i + 1)
                link(V.tensor_copy(nbx[0:E, 0:1], bank(0)[0:E, 8:9]))
                V.tensor_scalar(passed_b[:, :], k("iota")[0:E, 0:XMAX], nbx[0:E, 0:1], None, ALU.is_ge).then_inc(passed_rdy, 1)
                bc = lambda ap: ap.unsqueeze(1).to_broadcast([128, TT, E])
                V.scalar_tensor_tensor(te(cmpa), te(bank(3)[:, 0:TE]), float(E), bc(k("iota")), ALU.mult, ALU.add)
                link(V.tensor_scalar(xrow, bank(3)[:, TE:TE + E], 128.0, 128.0 * (E - 1), ALU.mult, ALU.add))
                V.tensor_scalar(gtop, bank(3)[:, 0:TE], 127.5, None, ALU.is_gt)
                link(V.tensor_tensor(te(select), te(bank(3)[:, 0:TE]), bc(xrow), ALU.add))
                link(V.tensor_tensor(select, select, cmpa, ALU.subtract))
                link(V.tensor_tensor(select, select, gtop, ALU.mult))
                link(V.tensor_tensor(cmpa, cmpa, select, ALU.add))
                link(V.tensor_tensor(prod3, hot3, cmpa.unsqueeze(1).to_broadcast([128, K, TE]), ALU.mult))
                link(V.tensor_reduce(gtop[:, 0:K * TT], prod.rearrange("p (n e) -> p n e", e=E), AX.X, ALU.add))
                V.tensor_copy(row_i[:, :], gtop[:, 0:K * TT]).then_inc(rows_rdy, 1)
                dve.wait_ge(unit_ps, i + 1)
                V.tensor_scalar(unit_i[0:1, 0:XMAX], bank(0)[0:1, 16:16 + XMAX], float(E - 1), None, ALU.min)
                V.tensor_copy(unit_i[0:1, XMAX:XMAX + 1], bank(0)[0:1, 128:129]).then_inc(unit_rdy, 1)

                def either(u, emit):
                    flag = nc.vector.value_load(big_i[0:1, ds(u, 1)], min_val=0, max_val=1)
                    with nc.vector.If(flag > 0):
                        emit(True)
                    with nc.vector.Else():
                        emit(False)

                def product(w, b, par, big=True):
                    dve.wait_ge(m["gate_rdy"], w + 1)
                    if b:
                        dve.wait_ge(m["actT_ps"], w - 1)
                    if big:
                        V.tensor_tensor(act[par], gate[par], bank(6)[:, F:2 * F], ALU.mult).then_inc(m["act_rdy"], 1)
                    else:
                        V.tensor_tensor(act[par][0:64], gate[par][64:128], bank(6)[64:128, 0:F], ALU.mult).then_inc(m["act_rdy"], 1)

                def rows_out(u, par, w):
                    dve.wait_ge(xgT_ps, u + 1 + i * E)
                    dve.wait_ge(m["up_ps"], w)
                    V.tensor_copy(xgT[par].rearrange("p c t -> p (c t)"), bank(1, 2)).then_inc(xgT_ev, 1)

                def act_out(w, b, par):
                    dve.wait_ge(m["actT_ps"], w + 1)
                    if b:
                        dve.wait_ge(m["dn_ps"], w - 1)
                    V.tensor_copy(actT[par].rearrange("p k t -> p (k t)"), bank(7)[:, 0:F]).then_inc(m["actT_ev"], 1)

                for w in range(TT):
                    product(w, w >= 2, w % 2)
                    act_out(w, w >= 2, w % 2)
                rows_out(0, 0, 0)
                either(0, lambda big: product(TT, 1, 0, big))
                rows_out(1, 1, 0)
                act_out(TT, 1, 0)
                with nc.vector.Fori(0, E // 4 - 1) as g:
                    for r in range(4):
                        w = g * 4 + (TT + 1 + r)
                        either(g * 4 + (1 + r), lambda big: product(w, 1, (1 + r) % 2, big))
                        rows_out(g * 4 + (2 + r), r % 2, g * 4 + (TT + 1 + r))
                        act_out(w, 1, (1 + r) % 2)
                for u in range(E - 3, E):
                    either(u, lambda big: product(TT + u, 1, u % 2, big))
                    if u + 1 < E:
                        rows_out(u + 1, (u + 1) % 2, TT + u)
                    act_out(TT + u, 1, u % 2)
                total = nc.vector.value_load(unit_i[0:1, XMAX:XMAX + 1], min_val=0, max_val=XMAX)
                with nc.vector.If(total > 0):
                    dve.wait_ge(m["up_ps"], TT + E - 1)
                    with nc.vector.Fori(0, total) as j:
                        dve.wait_ge(m["t_xgT_ps"], j + 2)
                        V.tensor_copy(xgT[0].rearrange("p c t -> p (c t)"), bank(1, 2)).then_inc(m["t_xgT_ev"], 1)
                        dve.wait_ge(m["t_gate"], j + 1)
                        V.tensor_tensor(act[0], gate[0], bank(6)[:, F:2 * F], ALU.mult).then_inc(m["t_act"], 1)
                        dve.wait_ge(m["t_actT_ps"], j + 1)
                        V.tensor_copy(actT[0].rearrange("p k t -> p (k t)"), bank(7)[:, 0:F]).then_inc(m["t_actT_ev"], 1)
                dve.wait_ge(m["y_ev"], TT)
                for n in range(TT * K):
                    t, q = n // K, n % K
                    dve.wait_ge(comb_in[n % 6], 16 * (n // 6 + 1 + i * TT * K // 6))
                    if n:
                        dve.wait_ge(comb_used, n + i * TT * K)
                    V.scalar_tensor_tensor(acc[:, t, :], comb[n % 6], wk[:, q * TT + t:q * TT + t + 1], acc[:, t, :],
                                           ALU.mult, ALU.add).then_inc(comb_used, 1)
                for c in range(DC):
                    dve.wait_ge(acc_ps, c + 1 + i * DC)
                    V.scalar_tensor_tensor(xT[:, c, :], bank(c % 2), mod[i][:, 5, c, 0:1], xT[:, c, :], ALU.mult, ALU.add)\
                        .then_inc(res_ev, 1)
                dve.wait_ge(res_ev, DC + i * DC)

            moe(0)
            mod_out(1)
            norm(J_MIX1)
            for n in range(2):
                V.memset(up[n][:, 0:PAD], 0.0)
                V.memset(up[n][:, PAD + T:PT_], 0.0).then_inc(pad_rdy, 1)
            dve.wait_ge(pad_rdy, 2)
            for c in range(DC):
                dve.wait_ge(sig_rdy, c + 1)
                if c >= 2:
                    dve.wait_ge(side_mul, SIDE_TAPS * (c - 1))
                V.scalar_tensor_tensor(up[c % 2][:, PAD:PAD + T], bank(2 * (c % 2)), v("pw1b", c, c + 1), sg[c % 2],
                                       ALU.add, ALU.mult).then_inc(u_rdy, 1)
                dve.wait_ge(u_rdy, c + 1)
                tap = lambda q: v("dww", c * TAPS + q, c * TAPS + q + 1)
                link(V.tensor_scalar(conv[:, c, :], up[c % 2][:, 0:T], tap(0), v("dwb", c, c + 1), ALU.mult, ALU.add))
                for q in range(1, TAPS - SIDE_TAPS):
                    link(V.scalar_tensor_tensor(conv[:, c, :], up[c % 2][:, q:q + T], tap(q), conv[:, c, :], ALU.mult, ALU.add))
                dve.wait_ge(side_add, (SIDE_TAPS - 1) * (c + 1))
                V.tensor_tensor(conv[:, c, :], conv[:, c, :], side[c % 2], ALU.add).then_inc(cv_rdy, 1)
            dve.wait_ge(mean_ps, 1)
            dve.wait_ge(cv_rdy, DC)
            for c in range(DC):
                V.tensor_tensor(conv[:, c, :], conv[:, c, :], bank(6), ALU.subtract).then_inc(cent_rdy, 1)
            dve.wait_ge(cent_rdy, DC)
            norm(J_LN)
            for c in range(DC):
                dve.wait_ge(pw2_ps, c + 1)
                link(V.tensor_scalar(tmp[c % 2], bank(c % 2), v("pw2b", c, c + 1), mod[1][:, 2, c, 0:1], ALU.add, ALU.mult))
                V.tensor_tensor(xT[:, c, :], xT[:, c, :], tmp[c % 2], ALU.add).then_inc(pw2_ev, 1)
            dve.wait_ge(pw2_ev, DC)
            norm(J_FFN1)
            moe(1)
            norm(J_FIN)


def constants():
    c = np.zeros((128, NCST), np.float32)
    p = np.arange(128)

    def put(name, a):
        lo, hi = CST[name]
        c[:a.shape[0], lo:hi] = a

    put("ident", np.eye(128))
    put("sel", (p[:, None] % 32 == np.arange(2)[None]).astype(np.float32))
    put("iota", np.tile(np.arange(E), (128, 1)))
    put("before", np.tile((np.arange(G)[None, :] < np.arange(G)[:, None]).reshape(1, -1), (128, 1)))
    put("upper", (p[:, None] < p[None, :]))
    put("upto", (np.arange(E)[:, None] <= np.arange(E)[None, :]))
    put("tok", p[:, None] + 128 * np.arange(TT)[None])
    tok = np.arange(T, dtype=np.float32)
    row, col = np.floor(tok / 64), tok % 64
    inv = (np.float32(10000.0) ** (-np.arange(0, 16, 2, dtype=np.float32) / np.float32(16))).astype(np.float32)
    ang = np.concatenate([row[:, None] * inv, row[:, None] * inv, col[:, None] * inv, col[:, None] * inv], -1).T
    sign = np.where(np.arange(ROPE) % 16 < 8, -1.0, 1.0)[:, None]
    cos, sin = np.cos(ang.astype(np.float32)), np.sin(ang.astype(np.float32)) * sign
    put("rope", np.concatenate([cos, sin, cos, sin]))
    return c


SWAP = np.arange(ROPE) ^ 8


def kernel(**inputs):
    import concourse.bacc as _bacc
    from concourse import mybir as _mybir
    from concourse.bass_utils import run_bass_kernel_spmd as _run

    a = {n: np.asarray(x) for n, x in inputs.items()}

    def cols(x):
        return x.reshape(-1, 128).T

    def feats(x):
        return np.ascontiguousarray(x.T.reshape(DC, 128, -1).transpose(1, 0, 2))

    vec = np.concatenate([
        np.stack([cols(a["c"][0]), cols(a["c_ctx"])], -1).reshape(128, -1),
        cols(a["mod_b"][0]), cols(a["mod_b"][1]), cols(a["norm_mix_w"].reshape(-1)), cols(a["norm_ffn_w"].reshape(-1)),
        cols(a["mla_q_norm"][0]), cols(a["mla_kv_norm"][0]), cols(a["conv_pw1_b"][0]), cols(a["conv_dw_b"][0]),
        cols(a["conv_norm_w"][0]), cols(a["conv_norm_b"][0]), cols(a["conv_pw2_b"][0]), cols(a["final_norm_w"]),
        a["conv_dw_w"][0].T.reshape(DC, 128, TAPS).transpose(1, 0, 2).reshape(128, -1)], axis=1)
    wq_b = a["mla_wq_b"][0].reshape(QL, H, NOPE + ROPE)
    wq_b = np.concatenate([wq_b, wq_b[:, :, NOPE + SWAP]], axis=2).reshape(QL, H * 128)
    wkv_a = a["mla_wkv_a"][0]
    wkv_a = np.concatenate([wkv_a, wkv_a[:, KVL + SWAP]], axis=1)
    wkv_b = a["mla_wkv_b"][0].reshape(KVL, H // 2, 2, 2, NOPE).transpose(0, 1, 3, 2, 4).reshape(KVL, -1)
    ins = [feats(a["x"][0]), feats(a["ctx"][0]), vec, constants(), a["mod_w"], a["mla_wq_a"][0], wq_b, wkv_a, wkv_b,
           a["mla_wo"][0], a["conv_pw1_w"][0], a["conv_pw2_w"][0], a["router_w"], a["router_bias"], a["exp_w1"], a["exp_w3"],
           a["exp_w2"], a["shared_w1"], a["shared_w3"], a["shared_w2"]]
    nc = _bacc.Bacc("TRN2", target_bir_lowering=False, num_devices=1)
    arrays, args = {}, []
    for n, x in enumerate(ins):
        x = np.ascontiguousarray(x)
        arrays[f"in_{n}"] = x
        args.append(nc.dram_tensor(f"in_{n}", x.shape, _mybir.dt.from_np(x.dtype), kind="ExternalInput").ap())
    args.append(nc.dram_tensor("out_0", (128, DC, T), _mybir.dt.float32, kind="ExternalOutput").ap())
    build(nc, *args)
    r = _run(nc, [arrays], core_ids=[0])
    y = r.results[0]["out_0"]
    return np.ascontiguousarray(y.transpose(1, 0, 2).reshape(D, T).T).reshape(1, T, D)
```

```python
import concourse.bass as bass
from concourse import mybir
import numpy as np
from contextlib import ExitStack

D = 1024
T = 512
C = 256
H = 16
NOPE, ROPE, VD = 64, 32, 64
QL, KVL = 512, 256
E = 64
K = 6
G = 8
TOPG = 4
F = 256
TAPS = 31
PAD = TAPS // 2
DC = D // 128
TT = T // 128
KEYS = C + T
EPS = 1e-6
SM_SCALE = float(NOPE + ROPE) ** -0.5
ROUTED = 2.5
CAP = T
BLOCKS = CAP // 128
XMAX = T * K // 128
ROWS = 128 * (E + XMAX)
NONE = 1 << 20
SIDE_TAPS = 12

VEC = {}
_at = 0
for _n, _w in (("c", 2 * DC), ("modb", 96), ("nmix", 2 * DC), ("nffn", 2 * DC), ("qn", QL // 128),
               ("kvn", KVL // 128), ("pw1b", 2 * DC), ("dwb", DC), ("lnw", DC), ("lnb", DC), ("pw2b", DC),
               ("fin", DC), ("dww", DC * TAPS)):
    VEC[_n] = (_at, _at + _w)
    _at += _w
NVEC = _at
CST = {}
_at = 0
for _n, _w in (("ident", 128), ("sel", 2), ("iota", E), ("before", G * G), ("upper", 128), ("upto", E),
               ("tok", TT), ("rope", T)):
    CST[_n] = (_at, _at + _w)
    _at += _w
NCST = _at


def build(nc, xT_d, ctxT_d, vec_d, cst_d, mod_w, wq_a, wq_b, wkv_a, wkv_b, wo, pw1, pw2,
          router_w, router_bias, exp_w1, exp_w3, exp_w2, sh_w1, sh_w3, sh_w2, out):
    f32, bf16, i32, u32 = mybir.dt.float32, mybir.dt.bfloat16, mybir.dt.int32, mybir.dt.uint32
    ALU, ACT, AX = mybir.AluOpType, mybir.ActivationFunctionType, mybir.AxisListType
    ds = bass.ds
    L = 2

    h_rows = [nc.dram_tensor(f"h_rows{i}", (T, D), f32, kind="Internal").ap() for i in range(L)]
    y_rows = nc.dram_tensor("y_rows", (ROWS, D), f32, kind="Internal").ap()
    slots = [nc.dram_tensor(f"slots{i}", (ROWS, 1), i32, kind="Internal").ap() for i in range(L)]

    ctx = ExitStack()
    with ctx:
        def sb(name, shape, dt=f32):
            return ctx.enter_context(nc.sbuf_tensor(name, shape, dt))

        def sem(name):
            return ctx.enter_context(nc.semaphore(name))

        PS = ctx.enter_context(nc.psum_tensor("PS", [128, 8 * 512], f32))

        def bank(b, n=1):
            return PS[:, b * 512:(b + n) * 512]

        vec = sb("vec", [128, NVEC])
        cst = sb("cst", [128, NCST])
        xT = sb("xT", [128, DC, T])
        hT = sb("hT", [128, DC * KEYS])
        RING = 4
        SLOT = 3 * DC * F
        ring = sb("ring", [128, RING * SLOT])
        work = sb("work", [128, 12800])
        sq = sb("sq", [128, 2, T])
        rs = sb("rs", [128, T])
        small = sb("small", [128, 480])
        mean_w = sb("mean_w", [128, 128])
        upper_b = sb("upper_b", [128, 128], bf16)
        upto_b = sb("upto_b", [E, E], bf16)
        ones_b = sb("ones_b", [128, 128], bf16)
        chosen_b = sb("chosen_b", [128, TT * E], bf16)
        extra_b = sb("extra_b", [E, 128], bf16)
        zrow = sb("zrow", [128, 512])
        big_i = sb("big_i", [1, E], i32)
        passed_b = sb("passed_b", [E, XMAX], bf16)
        tok_i = sb("tok_i", [128, TT], i32)
        idx = sb("idx", [128, E + XMAX], i32)
        col_i = sb("col_i", [128, 2], i32)
        row_i = sb("row_i", [128, K * TT], i32)
        unit_i = sb("unit_i", [1, XMAX + 1], i32)
        cs = sb("cs", [128, DC, 32])
        mod = [sb(f"mod{i}", [128, 6, DC, 2]) for i in range(L)]
        modA = [sb(f"modA{i}", [128, 2, DC, 2]) for i in range(L)]
        smx = sb("smx", [128, 4, 3])
        zero = sb("zero", [128, 1])
        tick = sb("tick", [1, 16])
        eps = sb("eps", [128, 1])

        def v(name, a=0, b=None):
            lo, hi = VEC[name]
            return vec[:, lo + a:(lo + b if b is not None else hi)]

        def k(name, a=0, b=None):
            lo, hi = CST[name]
            return cst[:, lo + a:(lo + b if b is not None else hi)]

        ident = k("ident")

        MODBUF = 4
        mw = [ring[:, n * DC * 512:(n + 1) * DC * 512].rearrange("p (c f) -> p c f", c=DC) for n in range(MODBUF)]
        mrow = [work[:, n * 512:(n + 1) * 512] for n in range(12)]
        AW = 2 * 8192
        wqa_sb = ring[:, AW:AW + DC * QL].rearrange("p (c f) -> p c f", c=DC)
        KVW = KVL + 2 * ROPE
        wkva_sb = ring[:, AW + DC * QL:AW + DC * QL + DC * KVW].rearrange("p (c f) -> p c f", c=DC)
        wo_sb = ring[:, AW:AW + DC * D].rearrange("p (c f) -> p c f", c=DC)
        wqb_sb = ring[:, 0:8192].rearrange("p (c h f) -> p c h f", c=QL // 128, h=H)
        wkvb_sb = ring[:, 8192:12288].rearrange("p (c h f) -> p c h f", c=KVL // 128, h=H)
        P = [ring[:, 12288 + n * KEYS:12288 + (n + 1) * KEYS] for n in range(2)]
        rope_t = [ring[:, 13824 + n * 512:13824 + (n + 1) * 512] for n in range(2)]
        ctxT = work[:, 4096:4096 + DC * C].rearrange("p (c t) -> p c t", c=DC)
        o = [0]

        def take(n):
            o[0] += n
            return work[:, o[0] - n:o[0]]

        pT = take(2 * 6 * T).rearrange("p (h j t) -> p h j t", h=2, j=6)
        ckv = take(2 * KEYS).rearrange("p (c t) -> p c t", c=2)
        qa = take(4 * T).rearrange("p (c t) -> p c t", c=4)
        kT = [[take(KEYS) for _ in range(2)] for _ in range(2)]
        vv = [ring[:, 14848 + n * 768:14848 + (n + 1) * 768].rearrange("p (j f) -> p j f", j=6) for n in range(2)]
        hA = hT[:, :].rearrange("p (c t) -> p c t", c=DC)
        oT = hT[:, 0:DC * T].rearrange("p (c t) -> p c t", c=DC)
        qT = [[hT[:, DC * T + (2 * a + b) * T:DC * T + (2 * a + b + 1) * T] for b in range(2)] for a in range(2)]
        assert o[0] <= 12800
        hM = hT[:, 0:DC * T].rearrange("p (c t) -> p c t", c=DC)

        o[0] = 0
        acc = take(TT * D).rearrange("p (t d) -> p t d", t=TT)
        xg = [take(D) for _ in range(2)]
        both = take(2 * D)
        xgT = [both[:, n * D:(n + 1) * D].rearrange("p (c t) -> p c t", c=DC) for n in range(2)]
        yb = [take(D) for _ in range(2)]
        gate = [take(F) for _ in range(2)]
        act = [take(F) for _ in range(2)]
        actT = [take(F).rearrange("p (k t) -> p k t", k=2) for _ in range(2)]
        hot = both[:, 0:K * TT * E]
        scoreT = yb[0][0:E, 0:T]
        prod = work[:, 0:K * TT * E]
        comb = xg + [both[:, 0:D], both[:, D:2 * D]] + yb
        o2 = [0]

        def few(n):
            o2[0] += n
            return small[:, o2[0] - n:o2[0]]

        score = take(TT * E)
        select = take(TT * E)
        gtop = take(TT * G * 8)
        cmpa = take(TT * G * G)
        assert o[0] <= 12800
        gsum = few(TT * G)
        cmpb = few(TT * G * G)
        rank = few(TT * G)
        top = few(TT * 8)
        topi = few(TT * 8)
        wk = few(K * TT)
        wsum = few(TT)
        nbx = few(4)
        xrow = few(E)
        assert o2[0] <= 480
        topu = sb("topu", [128, TT * 8], u32)
        bias_sb = sb("bias_sb", [128, E])
        rw_sb = hT[:, DC * T:DC * T + DC * E].rearrange("p (c e) -> p c e", c=DC)

        def w13(s):
            return ring[:, s * SLOT:s * SLOT + 2 * DC * F].rearrange("p (a c f) -> p a c f", a=2, c=DC)

        def w2(s):
            return ring[:, s * SLOT + 2 * DC * F:(s + 1) * SLOT].rearrange("p (k d) -> p k d", k=2)

        pw1_sb = ring[:, 0:DC * 2 * D].rearrange("p (c f) -> p c f", c=DC)
        pw2_sb = ring[:, DC * 2 * D:DC * 3 * D].rearrange("p (c f) -> p c f", c=DC)
        PT_ = T + 2 * PAD
        up = [work[:, n * PT_:(n + 1) * PT_] for n in range(2)]
        CU = 2 * PT_
        conv = work[:, CU:CU + DC * T].rearrange("p (c t) -> p c t", c=DC)
        rest = [work[:, CU + DC * T + n * T:CU + DC * T + (n + 1) * T] for n in range(10)]
        sg, tmp, tap_prod, side = rest[0:2], rest[2:4], rest[4:8], rest[8:10]
        oF = conv

        cst_in, x_in, pool_cst, dve_cst, cs_rdy = (sem(n) for n in ("cst_in", "x_in", "pool_cst", "dve_cst", "cs_rdy"))
        modw_in = [sem(f"modw_in{n}") for n in range(MODBUF)]
        modrow_ps, modrow_sb, modcol_ps, mod_rdy = sem("modrow_ps"), sem("modrow_sb"), sem("modcol_ps"), sem("mod_rdy")
        sq_rdy, sq_used, rs_rdy, nrm_mul, nrm_out = (sem(n) for n in ("sq_rdy", "sq_used", "rs_rdy", "nrm_mul", "nrm_out"))
        aw_in, bw_in, wo_in = sem("aw_in"), sem("bw_in"), sem("wo_in")
        a_ps, a_ev, a_pe = sem("a_ps"), sem("a_ev"), sem("a_pe")
        lsq_rdy, lsq_used, lrs_rdy, lat_rdy = (sem(n) for n in ("lsq_rdy", "lsq_used", "lrs_rdy", "lat_rdy"))
        pj_ps, kv_ev, q_ev, q_rope = sem("pj_ps"), sem("kv_ev"), sem("q_ev"), sem("q_rope")
        s_ps, max_rdy, nmax_rdy, exp_rdy, p_rdy, pT_ps, pT_act, pT_dve, o_ps, o_ev = (
            sem(n) for n in ("s_ps", "max_rdy", "nmax_rdy", "exp_rdy", "p_rdy", "pT_ps", "pT_act", "pT_dve", "o_ps", "o_ev"))
        wo_ps, wo_ev = sem("wo_ps"), sem("wo_ev")
        std_rdy, lstd_rdy = sem("std_rdy"), sem("lstd_rdy")
        zero_out = sem("zero_out")
        den_rdy, dve_step = sem("den_rdy"), sem("dve_step")
        pw_in, glu_ps, sig_rdy, u_rdy, side_mul, side_add, cv_rdy, mean_ps, cent_rdy, pw2_ps, pw2_ev, pad_rdy = (
            sem(n) for n in ("pw_in", "glu_ps", "sig_rdy", "u_rdy", "side_mul", "side_add", "cv_rdy", "mean_ps",
                             "cent_rdy", "pw2_ps", "pw2_ev", "pad_rdy"))
        out_dn, pw2_in = sem("out_dn"), sem("pw2_in")

        (rw_in, logit_ps, scoreT_rdy, chosen_rdy, pos_ps, rows_rdy, none_rdy, none_set, slots_set,
         score_ps, idx_in, cnt_ps, nbx_rdy, end_ps, passed_rdy, unit_ps, unit_rdy, sh_in, xg_clr) = (
            sem(n) for n in ("rw_in", "logit_ps", "scoreT_rdy", "chosen_rdy", "pos_ps", "rows_rdy", "none_rdy", "none_set", "slots_set",
                             "score_ps", "idx_in", "cnt_ps", "nbx_rdy", "end_ps", "passed_rdy", "unit_ps", "unit_rdy", "sh_in", "xg_clr"))

        hd_out = [sem(f"hd_out{s}") for s in range(2)]
        comb_in = [sem(f"comb_in{s}") for s in range(6)]

        col_rdy, xgT_ps, xgT_ev = sem("col_rdy"), sem("xgT_ps"), sem("xgT_ev")
        xg_in = [sem(f"xg_in{s}") for s in range(2)]
        y_out = [sem(f"y_out{s}") for s in range(2)]
        hrow_ps, hrow_sb, comb_used, acc_ps, res_ev = (sem(n) for n in ("hrow_ps", "hrow_sb", "comb_used", "acc_ps", "res_ev"))

        M = []
        for i in range(L):
            m = {n: sem(f"{n}{i}") for n in (
                "up_ps", "gate_rdy", "act_rdy", "actT_ps", "actT_ev", "dn_ps", "y_ev", "t_w", "t_xg", "t_idx",
                "t_xgT_ps", "t_xgT_ev", "t_up", "t_gate", "t_act", "t_actT_ps", "t_actT_ev", "t_dn", "t_yev", "t_yout", "t_tick", "t_pool")}
            m["w_in"] = [sem(f"w_in{i}_{s}") for s in range(RING)]
            M.append(m)

        def jobs():
            a = lambda i, n, c, w: modA[i][:, n, c, w:w + 1]
            b = lambda i, n, c, w: mod[i][:, 3 * n, c, w:w + 1]
            xs = lambda c: xT[:, c, :]
            return [
                (lambda c: ctxT[:, c, :], lambda c: hA[:, c, 0:C], C, lambda c: a(0, 0, c, 1), lambda c: b(0, 0, c, 1), ACT.Identity),
                (xs, lambda c: hA[:, c, C:KEYS], T, lambda c: a(0, 0, c, 0), lambda c: b(0, 0, c, 0), ACT.Identity),
                (xs, lambda c: hM[:, c, :], T, lambda c: a(0, 1, c, 0), lambda c: b(0, 1, c, 0), ACT.Identity),
                (xs, lambda c: hM[:, c, :], T, lambda c: a(1, 0, c, 0), lambda c: b(1, 0, c, 0), ACT.Identity),
                (lambda c: conv[:, c, :], lambda c: hM[:, c, :], T, lambda c: v("lnw", c, c + 1), lambda c: v("lnb", c, c + 1), ACT.Silu),
                (xs, lambda c: hM[:, c, :], T, lambda c: a(1, 1, c, 0), lambda c: b(1, 1, c, 0), ACT.Identity),
                (xs, lambda c: oF[:, c, :], T, lambda c: v("fin", c, c + 1), lambda c: zero[:, 0:1], ACT.Identity),
            ]

        JOBS = jobs()
        J_CTX, J_X, J_FFN0, J_MIX1, J_LN, J_FFN1, J_FIN = range(7)
        ROW_BANK = [n % 2 for n in range(4)] + [3, 0] * 4 + [(2, 4, 5, 6)[n % 4] for n in range(12)]
        COL_BANK = [2] * 4 + [3] * 8 + [7] * 12
        NB = 3

        AG = [("kv", 0, C, 0), ("kv", 0, C, 1), ("pe", 0, C, 2), ("kv", C, T, 0), ("kv", C, T, 1), ("pe", C, T, 2)] + \
             [("q", C, T, m) for m in range(QL // 128)]
        LAT = [(1, C, [0, 1], lambda j: ckv[:, j, 0:C], "kvn"), (2, T, [3, 4], lambda j: ckv[:, j, C:KEYS], "kvn"),
               (0, T, [6, 7, 8, 9], lambda j: qa[:, j, :], "qn")]
        LSQ = [g for _, _, gs, _, _ in LAT for g in gs]
        LATE = [[], [4, 5], [6, 7], [8, 9], [10, 11], [], [], []]
        NPAIR = H // 2
        NS = H * TT

        def pT_copy(eng, op, n, scalar):
            m, q, t = n // 8, (n // TT) % 2, n % TT
            eng.wait_ge(pT_ps, n + 1)
            if m:
                eng.wait_ge(o_ps, m)
            j0, j1 = (0, 4) if scalar else (4, 6)
            dst = pT[:, q, j0:j1, t * 128:(t + 1) * 128]
            src = bank(4, 2)[:, j0 * 128:j1 * 128].rearrange("p (j f) -> p j f", j=j1 - j0)
            if scalar:
                op(dst, src, ACT.Copy).then_inc(pT_act, 1)
            else:
                op(dst, src).then_inc(pT_dve, 1)

        block = ctx.enter_context(nc.Block())

        @block.sync
        def _(sp):
            sp.dma_start(cst[:, :], cst_d).then_inc(cst_in, 16)
            sp.dma_start(vec[:, :], vec_d).then_inc(cst_in, 16)
            sp.dma_start(xT[:, :, :], xT_d).then_inc(x_in, 16)
            sp.dma_start(ctxT, ctxT_d).then_inc(x_in, 16)

            def load_mod(n):
                if n % 12 >= MODBUF:
                    sp.wait_ge(modrow_ps, n - MODBUF + 1)
                j = n % 12
                sp.dma_start(mw[n % MODBUF], mod_w[n // 12, :, j * 512:(j + 1) * 512].rearrange("(c p) f -> p c f", p=128))\
                  .then_inc(modw_in[n % MODBUF], 16)

            def load_moe(i):
                m = M[i]
                sp.dma_start(rw_sb, router_w[i].rearrange("(c p) e -> p c e", p=128)).then_inc(rw_in, 16)
                sp.dma_start(bias_sb[:, :], router_bias[i].partition_broadcast(128)).then_inc(rw_in, 16)
                s = RING - 1
                sp.dma_start(w13(s)[:, 0], sh_w1[i].rearrange("(c p) f -> p c f", p=128)).then_inc(sh_in, 16)
                sp.dma_start(w13(s)[:, 1], sh_w3[i].rearrange("(c p) f -> p c f", p=128)).then_inc(sh_in, 16)
                sp.dma_start(w2(s), sh_w2[i].rearrange("(k p) d -> p k d", p=128)).then_inc(sh_in, 16)

                def expert_up(e, s, done):
                    sp.dma_start(w13(s)[:, 0], exp_w1[i, e].rearrange("o (p c) f -> p (o c) f", c=DC)).then_inc(done, 16)
                    sp.dma_start(w13(s)[:, 1], exp_w3[i, e].rearrange("o (p c) f -> p (o c) f", c=DC)).then_inc(done, 16)

                def expert_down(e, s, done):
                    sp.dma_start(w2(s), exp_w2[i, e].rearrange("o (k p) d -> p (o k) d", p=128)).then_inc(done, 16)

                def expert(e, s, done):
                    expert_up(e, s, done)
                    expert_down(e, s, done)

                if i == 0:
                    sp.wait_ge(modrow_ps, 24)
                for u in range(RING - 1):
                    expert(ds(u, 1), u, m["w_in"][u])
                sp.wait_ge(m["up_ps"], TT)
                expert_up(ds(RING - 1, 1), RING - 1, m["w_in"][RING - 1])
                sp.wait_ge(m["dn_ps"], TT)
                expert_down(ds(RING - 1, 1), RING - 1, m["w_in"][RING - 1])

                def refill_up(u, s):
                    sp.wait_ge(m["up_ps"], u + (TT + 1))
                    expert_up(ds(u + RING, 1), s, m["w_in"][s])

                def refill_down(u, s):
                    sp.wait_ge(m["dn_ps"], u + (TT + 1))
                    expert_down(ds(u + RING, 1), s, m["w_in"][s])

                refill_up(0, 0)
                with nc.sync.Fori(0, E // RING - 2) as g:
                    for r in range(RING):
                        refill_up(g * RING + (1 + r), (1 + r) % RING)
                        refill_down(g * RING + r, r)
                for u in range(E - 2 * RING + 1, E - RING):
                    refill_up(u, u % RING)
                    refill_down(u - 1, (u - 1) % RING)
                refill_down(E - RING - 1, RING - 1)
                sp.wait_ge(unit_rdy, i + 1)
                total = nc.sync.value_load(unit_i[0:1, XMAX:XMAX + 1], min_val=0, max_val=XMAX)
                with nc.sync.If(total > 0):
                    with nc.sync.Fori(0, total) as j:
                        sp.wait_ge(m["dn_ps"], TT + E - 3)
                        sp.wait_ge(m["t_dn"], j + 1)
                        e = nc.sync.value_load(unit_i[0:1, ds(j, 1)], min_val=0, max_val=E - 1)
                        expert(ds(e, 1), 0, m["t_w"])

            for n in range(MODBUF):
                load_mod(n)
            sp.dma_start(wqa_sb, wq_a.rearrange("(c p) f -> p c f", p=128)).then_inc(aw_in, 16)
            sp.dma_start(wkva_sb, wkv_a.rearrange("(c p) f -> p c f", p=128)).then_inc(aw_in, 16)
            for n in range(MODBUF, 12):
                load_mod(n)
            sp.wait_ge(modrow_ps, 12)
            sp.dma_start(wqb_sb, wq_b.rearrange("(c p) (h f) -> p c h f", p=128, h=H)).then_inc(bw_in, 16)
            sp.dma_start(wkvb_sb, wkv_b.rearrange("(c p) (h f) -> p c h f", p=128, h=H)).then_inc(bw_in, 16)
            sp.wait_ge(a_ps, len(AG))
            sp.dma_start(wo_sb, wo.rearrange("(c p) f -> p c f", p=128)).then_inc(wo_in, 16)
            sp.wait_ge(pj_ps, 6 * NPAIR)
            for n in range(12, 15):
                load_mod(n)
            sp.wait_ge(o_ps, NPAIR)
            for n in range(15, 24):
                load_mod(n)
            sp.wait_ge(wo_ps, DC)
            load_moe(0)
            sp.wait_ge(comb_used, TT * K - 4)
            sp.dma_start(pw1_sb, pw1.rearrange("(c p) f -> p c f", p=128)).then_inc(pw_in, 16)
            sp.dma_start(pw2_sb, pw2.rearrange("(c p) f -> p c f", p=128)).then_inc(pw2_in, 16)
            sp.wait_ge(pw2_ps, DC)
            load_moe(1)
            sp.wait_ge(nrm_out, 8 * (J_FIN + 1))
            sp.dma_start(out, oF).then_inc(out_dn, 16)
            sp.wait_ge(out_dn, 16)

        @block.gpsimd
        def _(pool):
            nc.gpsimd.memset(ones_b[:, :], 1.0).then_inc(pool_cst, 1)
            nc.gpsimd.memset(mean_w[:, :], 1.0 / D).then_inc(pool_cst, 1)
            pool.wait_ge(cst_in, 32)
            nc.gpsimd.tensor_copy(upper_b[:, :], k("upper")).then_inc(pool_cst, 1)
            nc.gpsimd.tensor_copy(upto_b[:, :], k("upto")[0:E, :]).then_inc(pool_cst, 1)
            nc.gpsimd.tensor_copy(tok_i[:, :], k("tok")).then_inc(pool_cst, 1)

            def moe(i):
                m = M[i]
                pool.wait_ge(dve_cst, 1)
                nc.gpsimd.memset(idx[:, :], NONE).then_inc(none_rdy, 1)
                pool.wait_ge(none_rdy, i + 1)
                pool.dma_start(slots[i].rearrange("(p n) o -> p (n o)", p=128), idx[:, :]).then_inc(none_set, 16)
                pool.wait_ge(rows_rdy, i + 1)
                for n in range(2):
                    nc.gpsimd.memset(xg[n], 0.0).then_inc(xg_clr, 1)
                pool.wait_ge(none_set, 16 * (i + 1))
                for n in range(K * TT):
                    pool.indirect_dma_start(out=slots[i], out_offset=bass.IndirectOffsetOnAxis(ap=row_i[:, n:n + 1], axis=0),
                                            in_=tok_i[:, n % TT:n % TT + 1], in_offset=None).then_inc(slots_set, 16)
                pool.wait_ge(slots_set, 16 * K * TT * (i + 1))
                pool.dma_start(idx[:, 0:E], slots[i][0:128 * E, :].rearrange("(p e) o -> p (e o)", e=E)).then_inc(idx_in, 16)
                pool.wait_ge(idx_in, 16 * (i + 1))
                for s in range(2):
                    pool.wait_ge(hd_out[s], 32 + 32 * i)
                pool.wait_ge(xg_clr, 2 * (i + 1))

                def gather(u, n, done):
                    nc.gpsimd.tensor_copy(col_i[:, n:n + 1], idx[:, ds(u, 1)]).then_inc(col_rdy, 1)
                    pool.wait_ge(col_rdy, u + 1 + i * E)
                    nc.gpsimd.tensor_tensor(tick[0:1, 8 * i + 2:8 * i + 3], zero[0:1, 0:1], zero[0:1, 0:1], ALU.add)
                    big = nc.gpsimd.value_load(big_i[0:1, ds(u, 1)], min_val=0, max_val=1)

                    def rows(p):
                        pool.indirect_dma_start(out=xg[n][0:p], out_offset=None, in_=h_rows[i],
                                                in_offset=bass.IndirectOffsetOnAxis(ap=col_i[0:p, n:n + 1], axis=0),
                                                bounds_check=T - 1, oob_is_err=False).then_inc(done, 16)

                    with nc.gpsimd.If(big > 0):
                        rows(128)
                    with nc.gpsimd.Else():
                        rows(64)

                pool.wait_ge(unit_rdy, i + 1)
                gather(0, 0, xg_in[0])
                gather(1, 1, xg_in[1])
                with nc.gpsimd.Fori(0, E // 2 - 1) as g:
                    for r in range(2):
                        pool.wait_ge(xgT_ps, g * 2 + (1 + r) + i * E)
                        gather(g * 2 + (2 + r), r, xg_in[r])
                pool.wait_ge(xgT_ps, E - 1 + i * E)
                total = nc.gpsimd.value_load(unit_i[0:1, XMAX:XMAX + 1], min_val=0, max_val=XMAX)
                with nc.gpsimd.If(total > 0):
                    with nc.gpsimd.Fori(0, total) as j:
                        pool.wait_ge(m["t_xgT_ps"], j + 1)
                        nc.gpsimd.tensor_tensor(tick[0:1, 8 * i + 3:8 * i + 4], zero[0:1, 0:1], zero[0:1, 0:1], ALU.add)
                        pool.dma_start(idx[:, E:E + 1], slots[i][128 * E:ROWS, :].rearrange("(u p) o -> p u o", p=128)
                                       [:, ds(j, 1), :].rearrange("p u o -> p (u o)")).then_inc(m["t_idx"], 16)
                        pool.wait_ge(m["t_idx"], j * 16 + 16)
                        nc.gpsimd.tensor_tensor(tick[0:1, 8 * i + 6:8 * i + 7], zero[0:1, 0:1], zero[0:1, 0:1], ALU.add)\
                            .then_inc(m["t_pool"], 1)
                        pool.wait_ge(m["t_pool"], j + 1)
                        nc.gpsimd.tensor_tensor(tick[0:1, 8 * i + 7:8 * i + 8], zero[0:1, 0:1], zero[0:1, 0:1], ALU.add)
                        pool.indirect_dma_start(out=xg[0], out_offset=None, in_=h_rows[i],
                                                in_offset=bass.IndirectOffsetOnAxis(ap=idx[:, E:E + 1], axis=0),
                                                bounds_check=T - 1, oob_is_err=False).then_inc(m["t_xg"], 16)
                pool.wait_ge(zero_out, 32)
                for s in range(2):
                    pool.wait_ge(y_out[s], 32 * E // 2 + i * 16 * E)
                pool.wait_ge(m["dn_ps"], TT + E)
                with nc.gpsimd.If(total > 0):
                    pool.wait_ge(m["t_yout"], total * 16)
                    nc.gpsimd.tensor_tensor(tick[0:1, 8 * i + 4:8 * i + 5], zero[0:1, 0:1], zero[0:1, 0:1], ALU.add)
                for n in range(TT * K):
                    t, q = n // K, n % K
                    if n >= 6:
                        pool.wait_ge(comb_used, n - 5 + i * TT * K)
                    pool.indirect_dma_start(out=comb[n % 6], out_offset=None, in_=y_rows,
                                            in_offset=bass.IndirectOffsetOnAxis(ap=row_i[:, q * TT + t:q * TT + t + 1], axis=0))\
                        .then_inc(comb_in[n % 6], 16)

            pool.wait_ge(bw_in, 32)
            for n in range(2):
                pool.dma_start(y_rows[64 * E:ROWS, :].rearrange("(u p) (a d) -> p u a d", p=128, a=2)[:, :, n, :],
                               zrow[:, :].unsqueeze(1).to_broadcast([128, E // 2 + XMAX, 512])).then_inc(zero_out, 16)
            moe(0)
            for c in range(DC):
                for q in range(1, SIDE_TAPS):
                    n = c * SIDE_TAPS + q
                    pool.wait_ge(side_mul, n + 1)
                    if q == 1:
                        if c >= 2:
                            pool.wait_ge(cv_rdy, c - 1)
                        before = tap_prod[(n - 1) % 4]
                    else:
                        pool.wait_ge(side_add, n - c - 1)
                        before = side[c % 2]
                    nc.gpsimd.tensor_tensor(side[c % 2], before, tap_prod[n % 4], ALU.add).then_inc(side_add, 1)
            moe(1)

        @block.scalar
        def _(a):
            A = nc.scalar.activation
            a.wait_ge(cst_in, 32)
            a.wait_ge(dve_cst, 1)
            A(cs[:, :, 0:2], v("c").rearrange("p (c w) -> p c w", w=2), ACT.Silu).then_inc(cs_rdy, 1)

            def mod_row(n):
                a.wait_ge(modrow_ps, n + 1)
                A(mrow[n % 12], bank(ROW_BANK[n]), ACT.Copy).then_inc(modrow_sb, 1)

            def square(j, c):
                src, dst, w, sc, sh, fn = JOBS[j]
                n = 8 * j + c
                if n >= 2:
                    a.wait_ge(sq_used, n - 1)
                A(sq[:, n % 2, 0:w], src(c), ACT.Square).then_inc(sq_rdy, 1)

            def norm_sum(j, squared=False, wait=lambda c: None):
                src, dst, w, sc, sh, fn = JOBS[j]
                for c in [] if squared else range(DC):
                    wait(c)
                    square(j, c)
                a.wait_ge(sq_used, 8 * (j + 1))
                if j:
                    a.wait_ge(nrm_mul, 8 * j)
                A(rs[:, 0:w], bank(NB)[:, 0:w], ACT.Sqrt, bias=eps[:, 0:1]).then_inc(std_rdy, 1)

            def norm_apply(j):
                src, dst, w, sc, sh, fn = JOBS[j]
                for c in range(DC):
                    a.wait_ge(nrm_mul, 8 * j + c + 1)
                    A(dst(c), dst(c), fn, bias=sh(c), scale=sc(c)).then_inc(nrm_out, 1)

            def norm(j, squared=False, wait=lambda c: None):
                norm_sum(j, squared, wait)
                norm_apply(j)

            def moe(i):
                m = M[i]
                a.wait_ge(logit_ps, i + 1)
                A(scoreT, bank(0)[0:E, :], ACT.Sigmoid).then_inc(scoreT_rdy, 1)
                for t in range(TT):
                    a.wait_ge(hrow_ps, t + 1 + i * TT)
                    if t >= 2:
                        a.wait_ge(hd_out[t % 2], 16 + 32 * i)
                    A(yb[t % 2].rearrange("p (c q) -> p q c", c=DC),
                      bank(1 if t % 2 == 0 else 4, 2).rearrange("p (q c) -> p q c", c=DC), ACT.Copy).then_inc(hrow_sb, 1)
                    a.wait_ge(hrow_sb, t + 1 + i * TT)
                    a.dma_start(h_rows[i][t * 128:(t + 1) * 128, :], yb[t % 2]).then_inc(hd_out[t % 2], 16)

                def silu(w, b, par, big=True):
                    a.wait_ge(m["up_ps"], w + 1)
                    if b:
                        a.wait_ge(m["act_rdy"], w - 1)
                    if big:
                        A(gate[par], bank(6)[:, 0:F], ACT.Silu).then_inc(m["gate_rdy"], 1)
                    else:
                        A(gate[par][64:128], bank(6)[0:64, 0:F], ACT.Silu).then_inc(m["gate_rdy"], 1)

                def either(u, emit):
                    flag = nc.scalar.value_load(big_i[0:1, ds(u, 1)], min_val=0, max_val=1)
                    with nc.scalar.If(flag > 0):
                        emit(True)
                    with nc.scalar.Else():
                        emit(False)

                def store(u, wait_n, par, big):
                    a.wait_ge(m["dn_ps"], u + (TT + 1))
                    if not (isinstance(wait_n, int) and wait_n == 0):
                        a.wait_ge(y_out[par], wait_n + i * 16 * E)
                    if big:
                        A(yb[par], bank(4, 2), ACT.Copy).then_inc(m["y_ev"], 1)
                    else:
                        A(yb[par][:, 0:512], bank(4), ACT.Copy).then_inc(m["y_ev"], 1)
                    a.wait_ge(m["y_ev"], u + (TT + 1))
                    p = 128 if big else 64
                    rows = y_rows[0:p * E, :].rearrange("(p e) d -> p e d", e=E)
                    for half in range(2):
                        src = yb[par][:, half * 512:(half + 1) * 512] if big else yb[par][64 * half:64 * half + 64, 0:512]
                        a.dma_start(rows[:, ds(u, 1), half * 512:(half + 1) * 512].rearrange("p e d -> p (e d)"), src)\
                         .then_inc(y_out[par], 16)

                for w in range(TT):
                    silu(w, w >= 2, w % 2)
                    if w == 1:
                        a.wait_ge(m["act_rdy"], 2)
                    if w:
                        a.wait_ge(m["dn_ps"], w)
                        A(acc[:, w - 1, :], bank(4, 2), ACT.Copy).then_inc(m["y_ev"], 1)
                for s in range(2):
                    a.wait_ge(hd_out[s], 32 + 32 * i)
                a.wait_ge(unit_rdy, i + 1)
                a.wait_ge(zero_out, 32)
                a.wait_ge(m["dn_ps"], TT)
                A(acc[:, TT - 1, :], bank(4, 2), ACT.Copy).then_inc(m["y_ev"], 1)
                either(0, lambda big: silu(TT, 1, 0, big))
                for u in range(1, 5):
                    either(u, lambda big: silu(TT + u, 1, u % 2, big))
                    either(u - 1, lambda big: store(u - 1, 32 * ((u - 1) // 2), (u - 1) % 2, big))
                with nc.scalar.Fori(1, E // 4 - 1) as g:
                    for r in range(4):
                        either(g * 4 + (1 + r), lambda big: silu(g * 4 + (TT + 1 + r), 1, (1 + r) % 2, big))
                        either(g * 4 + r, lambda big: store(g * 4 + r, g * 64 + 32 * (r // 2), r % 2, big))
                for u in range(E - 3, E):
                    either(u, lambda big: silu(TT + u, 1, u % 2, big))
                    either(u - 1, lambda big: store(u - 1, 32 * ((u - 1) // 2), (u - 1) % 2, big))
                either(E - 1, lambda big: store(E - 1, 32 * ((E - 1) // 2), 1, big))
                a.sem_inc(m["t_yev"], 1)
                a.wait_ge(unit_rdy, i + 1)
                total = nc.scalar.value_load(unit_i[0:1, XMAX:XMAX + 1], min_val=0, max_val=XMAX)
                with nc.scalar.If(total > 0):
                    a.wait_ge(y_out[0], 32 * E // 2 + i * 16 * E)
                    with nc.scalar.Fori(0, total) as j:
                        a.wait_ge(m["t_up"], j + 1)
                        A(gate[0], bank(6)[:, 0:F], ACT.Silu).then_inc(m["t_gate"], 1)
                        a.wait_ge(m["t_dn"], j + 2)
                        A(yb[0], bank(4, 2), ACT.Copy).then_inc(m["t_yev"], 1)
                        a.wait_ge(m["t_yev"], j + 2)
                        a.dma_start(y_rows[128 * E:ROWS, :].rearrange("(u p) d -> p u d", p=128)[:, ds(j, 1), :]
                                    .rearrange("p u d -> p (u d)"), yb[0]).then_inc(m["t_yout"], 16)
                        a.wait_ge(m["t_yout"], j * 16 + 16)
                        A(tick[0:1, i:i + 1], zero[0:1, 0:1], ACT.Copy).then_inc(m["t_tick"], 1)

            a.wait_ge(x_in, 32)
            norm_sum(J_CTX)
            norm_sum(J_X)
            for n in range(4):
                mod_row(n)
            a.wait_ge(mod_rdy, 1)
            norm_apply(J_CTX)
            norm_apply(J_X)
            for s, g in enumerate(LSQ):
                kind, c0, w, blk = AG[g]
                a.wait_ge(a_ps, g + 1)
                if s >= 2:
                    a.wait_ge(lsq_used, s - 1)
                if kind == "kv":
                    A(ckv[:, blk, c0:c0 + w], bank(4 + g % 4)[:, 0:w], ACT.Copy)
                else:
                    A(qa[:, blk, :], bank(4 + g % 4), ACT.Copy)
                A(sq[:, s % 2, 0:w], bank(4 + g % 4)[:, 0:w], ACT.Square).then_inc(lsq_rdy, 1)
                for n in LATE[s]:
                    mod_row(n)
                for b, lw, gs, _, _ in LAT:
                    if g == gs[-1]:
                        a.wait_ge(lsq_used, s + 1)
                        if s >= len(gs):
                            a.wait_ge(lat_rdy, s + 1 - len(gs))
                        A(rs[:, 0:lw], bank(b)[:, 0:lw], ACT.Sqrt, bias=eps[:, 0:1], scale=D / (128.0 * len(gs))).then_inc(lstd_rdy, 1)

            def kv_out(m, part):
                n = 6 * m + part
                a.wait_ge(pj_ps, n + 1)
                if part == 0:
                    for q in range(2):
                        last = A(kT[m % 2][q][0:64, T:KEYS], bank(7)[64 * q:64 * q + 64, 0:C], ACT.Copy)
                elif part == 1:
                    for q in range(2):
                        last = A(kT[m % 2][q][0:64, 0:T], bank(6)[64 * q:64 * q + 64, :], ACT.Copy)
                elif part == 4:
                    last = A(vv[m % 2][:, 0:4, :], bank(7).rearrange("p (j f) -> p j f", j=4), ACT.Copy)
                else:
                    last = A(vv[m % 2][:, 4:6, :], bank(6)[:, 0:256].rearrange("p (j f) -> p j f", j=2), ACT.Copy)
                last.then_inc(kv_ev, 1)

            for part in (0, 1, 4, 5):
                kv_out(0, part)
            for n in range(NS):
                m, i8 = n // 8, n % 8
                a.wait_ge(nmax_rdy, n + 1)
                if n >= 2:
                    a.wait_ge(pT_ps, n - 1)
                A(P[n % 2], bank(2 * (n % 2), 2)[:, 0:KEYS], ACT.Exp, bias=smx[:, n % 4, 1:2], scale=SM_SCALE,
                  accum_out=smx[:, n % 4, 2:3]).then_inc(exp_rdy, 1)
                if m + 1 < NPAIR and i8 in (1, 2, 5, 6):
                    kv_out(m + 1, {1: 0, 2: 1, 5: 4, 6: 5}[i8])
                if i8:
                    pT_copy(a, A, n - 1, True)
                if i8 == 7:
                    pT_copy(a, A, n, True)
            for n in range(DC + 1):
                if n < DC:
                    mod_row(12 + n)
                if n:
                    a.wait_ge(wo_ev, n)
                    square(J_FFN0, n - 1)
            a.wait_ge(mod_rdy, 2)
            norm(J_FFN0, squared=True)
            for n in range(20, 24):
                mod_row(n)
            moe(0)
            a.wait_ge(mod_rdy, 3)
            norm(J_MIX1, wait=lambda c: a.wait_ge(res_ev, c + 1))

            def side_taps(c, q0, q1):
                a.wait_ge(u_rdy, c + 1)
                for q in range(q0, q1):
                    n = c * SIDE_TAPS + q
                    if n >= 4:
                        a.wait_ge(side_add, (n - 4) // SIDE_TAPS * (SIDE_TAPS - 1) + max(1, (n - 4) % SIDE_TAPS))
                    at = TAPS - SIDE_TAPS + q
                    A(tap_prod[n % 4], up[c % 2][:, at:at + T], ACT.Copy, scale=v("dww", c * TAPS + at, c * TAPS + at + 1))\
                        .then_inc(side_mul, 1)

            for c in range(DC):
                if c:
                    side_taps(c - 1, 0, SIDE_TAPS // 2)
                a.wait_ge(glu_ps, c + 1)
                if c >= 2:
                    a.wait_ge(u_rdy, c - 1)
                A(sg[c % 2], bank(2 * (c % 2) + 1), ACT.Sigmoid, bias=v("pw1b", DC + c, DC + c + 1)).then_inc(sig_rdy, 1)
                if c:
                    side_taps(c - 1, SIDE_TAPS // 2, SIDE_TAPS)
            side_taps(DC - 1, 0, SIDE_TAPS)
            a.wait_ge(cent_rdy, DC)
            norm(J_LN)
            norm(J_FFN1, wait=lambda c: a.wait_ge(pw2_ev, c + 1))
            moe(1)
            norm(J_FIN, wait=lambda c: a.wait_ge(res_ev, DC + c + 1))

        @block.tensor
        def _(pe):
            mm, tr = nc.tensor.matmul, nc.tensor.transpose
            pe.wait_ge(pool_cst, 5)
            pe.wait_ge(cs_rdy, 1)

            def mod_columns(n):
                pe.wait_ge(modrow_sb, n + 1)
                for q in range(4):
                    at = 2 * (4 * (n % 12) + q)
                    last = mm(bank(COL_BANK[n])[:, at:at + 2], mrow[n % 12][:, 128 * q:128 * q + 128], k("sel"), start=True, stop=True)
                last.then_inc(modcol_ps, 1)

            def mod_chunk(n):
                pe.wait_ge(modw_in[n % MODBUF], 16 * (n // MODBUF + 1))
                before = [j for j in range(n) if ROW_BANK[j] == ROW_BANK[n]]
                if before:
                    pe.wait_ge(modrow_sb, before[-1] + 1)
                for c in range(DC):
                    t = c % 4
                    last = mm(bank(ROW_BANK[n])[32 * t:32 * t + 32, :], cs[:, c, :], mw[n % MODBUF][:, c, :],
                              start=(c < 4), stop=(c >= 4), tile_position=(0, 32 * t), skip_group_check=True)
                last.then_inc(modrow_ps, 1)

            def mean(j, c):
                w = JOBS[j][2]
                if j and c == 0:
                    pe.wait_ge(rs_rdy, j)
                pe.wait_ge(sq_rdy, 8 * j + c + 1)
                mm(bank(NB)[:, 0:w], mean_w[:, :], sq[:, c % 2, 0:w], start=(c == 0), stop=(c == DC - 1)).then_inc(sq_used, 1)

            def norm(j):
                for c in range(DC):
                    mean(j, c)

            norm(J_CTX)
            norm(J_X)
            for n in range(4):
                mod_chunk(n)
            for n in range(4):
                mod_columns(n)
            pe.wait_ge(nrm_out, 16)
            pe.wait_ge(aw_in, 32)
            pe.wait_ge(rs_rdy, 2)

            def latent_sum(s):
                if s == 4:
                    pe.wait_ge(modrow_sb, 12)
                g = LSQ[s]
                b, w, gs, _, _ = [x for x in LAT if g in x[2]][0]
                pe.wait_ge(lsq_rdy, s + 1)
                mm(bank(b)[:, 0:w], mean_w[:, :], sq[:, s % 2, 0:w], start=(g == gs[0]),
                   stop=(g == gs[-1])).then_inc(lsq_used, 1)

            for g, (kind, c0, w, blk) in enumerate(AG):
                if g >= 4:
                    if AG[g - 4][0] == "pe":
                        pe.wait_ge(a_pe, (g - 4) // 3 + 1)
                    else:
                        pe.wait_ge(lsq_rdy, LSQ.index(g - 4) + 1)
                for c in range(DC):
                    if kind == "q":
                        lhs, M_ = wqa_sb[:, c, 128 * blk:128 * blk + 128], 128
                    elif kind == "kv":
                        lhs, M_ = wkva_sb[:, c, 128 * blk:128 * blk + 128], 128
                    else:
                        lhs, M_ = wkva_sb[:, c, KVL:KVW], 2 * ROPE
                    last = mm(bank(4 + g % 4)[0:M_, 0:w], lhs, hA[:, c, c0:c0 + w], start=(c == 0), stop=(c == DC - 1))
                last.then_inc(a_ps, 1)
                for n in LATE[LSQ.index(g)] if g in LSQ else []:
                    mod_chunk(n)
                if g >= 1 and g - 1 in LSQ:
                    latent_sum(LSQ.index(g - 1))
            latent_sum(len(LSQ) - 1)

            def project(m, part):
                if part == 0 and m:
                    pe.wait_ge(kv_ev, 4 * m - 1)
                elif part == 1 and m:
                    pe.wait_ge(kv_ev, 4 * m)
                    pe.wait_ge(o_ev, m - 1)
                elif part == 2:
                    pe.wait_ge(kv_ev, 4 * m + 1)
                elif part == 3:
                    pe.wait_ge(kv_ev, 4 * m + 2)
                elif part == 4:
                    pe.wait_ge(q_ev, 2 * m + 1)
                elif part == 5:
                    pe.wait_ge(q_ev, 2 * m + 2)
                if part < 2:
                    b, w, c0 = ((7, C, T), (6, T, 0))[part]
                    for c in range(2):
                        last = mm(bank(b)[:, 0:w], wkvb_sb[:, c, 2 * m, :], ckv[:, c, c0:c0 + w],
                                  start=(c == 0), stop=(c == 1))
                elif part < 4:
                    for c in range(4):
                        last = mm(bank(7 if part == 2 else 6), wqb_sb[:, c, 2 * m + part - 2, :], qa[:, c, :],
                                  start=(c == 0), stop=(c == 3))
                else:
                    for j in (range(4) if part == 4 else range(4, 6)):
                        for c in range(2):
                            last = mm(bank(7 if part == 4 else 6)[:, (j % 4) * 128:(j % 4) * 128 + 128],
                                      ckv[:, c, j * 128:(j + 1) * 128], wkvb_sb[:, c, 2 * m + 1, :],
                                      start=(c == 0), stop=(c == 1))
                last.then_inc(pj_ps, 1)

            def scores(n):
                m, q, t = n // 8, (n // TT) % 2, n % TT
                pe.wait_ge(kv_ev, 4 * m + 2)
                pe.wait_ge(q_ev, 2 * m + 1 + q)
                if n == 1:
                    pe.wait_ge(mod_rdy, 2)
                if n >= 2:
                    pe.wait_ge(exp_rdy, n - 1)
                for c0, w in ((0, 512), (512, 256)):
                    last = mm(bank(2 * (n % 2), 2)[:, c0:c0 + w], qT[m % 2][q][0:96, t * 128:(t + 1) * 128],
                              kT[m % 2][q][0:96, c0:c0 + w], start=True, stop=True)
                last.then_inc(s_ps, 1)

            def turn(n):
                pe.wait_ge(p_rdy, n + 1)
                if n:
                    pe.wait_ge(pT_act, n)
                    pe.wait_ge(pT_dve, n)
                for j in range(6):
                    last = tr(bank(4, 2)[:, j * 128:(j + 1) * 128], P[n % 2][:, j * 128:(j + 1) * 128], ident)
                last.then_inc(pT_ps, 1)

            for n in range(4, 12):
                mod_columns(n)
            pe.wait_ge(lat_rdy, 4)
            pe.wait_ge(bw_in, 32)
            for part in range(6):
                if part == 2:
                    pe.wait_ge(lat_rdy, 8)
                project(0, part)
            scores(0)
            for n in range(NS):
                m, i8 = n // 8, n % 8
                if n + 1 < NS and (n == 0 or i8 != 0):
                    scores(n + 1)
                if m + 1 < NPAIR and i8 < 6:
                    project(m + 1, i8)
                turn(n)
                if i8 == 7:
                    if n + 2 < NS:
                        scores(n + 2)
                    pe.wait_ge(pT_act, n + 1)
                    pe.wait_ge(pT_dve, n + 1)
                    pe.wait_ge(kv_ev, 4 * min(m + 2, NPAIR))
                    for j in range(6):
                        for q in range(2):
                            last = mm(bank(6)[64 * q:64 * q + 64, :], vv[m % 2][:, j, 64 * q:64 * q + 64], pT[:, q, j, :],
                                      start=(j == 0), stop=(j == 5), tile_position=(0, 64 * q), skip_group_check=True)
                    last.then_inc(o_ps, 1)
            pe.wait_ge(o_ev, NPAIR)
            pe.wait_ge(wo_in, 16)
            for n in range(DC):
                mod_chunk(12 + n)
                if n >= 2:
                    pe.wait_ge(wo_ev, n - 1)
                for c in range(DC):
                    last = mm(bank(n % 2), wo_sb[:, c, n * 128:(n + 1) * 128], oT[:, c, :], start=(c == 0), stop=(c == DC - 1))
                last.then_inc(wo_ps, 1)
                if n:
                    mean(J_FFN0, n - 1)

            def moe(i):
                m = M[i]
                def up_mm(lhs, s):
                    for c in range(DC):
                        last = mm(bank(6), lhs(c), w13(s)[:, :, c, :], start=(c == 0), stop=(c == DC - 1))
                    return last

                def up_small(lhs, s):
                    for c in range(DC):
                        for q in range(2):
                            last = mm(bank(6)[64 * q:64 * q + 64, 0:F], lhs(c)[:, 0:64], w13(s)[:, q, c, :], start=(c == 0),
                                      stop=(c == DC - 1), tile_position=(0, 64 * q), skip_group_check=True)
                    return last

                def down_small(par, s):
                    for kk in range(2):
                        for q in range(2):
                            last = mm(bank(4)[64 * q:64 * q + 64, :], actT[par][:, kk, 0:64], w2(s)[:, kk, q * 512:(q + 1) * 512],
                                      start=(kk == 0), stop=(kk == 1), tile_position=(0, 64 * q), skip_group_check=True)
                    return last

                def either(u, emit):
                    flag = nc.tensor.value_load(big_i[0:1, ds(u, 1)], min_val=0, max_val=1)
                    with nc.tensor.If(flag > 0):
                        emit(True)
                    with nc.tensor.Else():
                        emit(False)

                def down_mm(par, s):
                    for half in range(2):
                        for kk in range(2):
                            last = mm(bank(4 + half), actT[par][:, kk, :], w2(s)[:, kk, half * 512:(half + 1) * 512],
                                      start=(kk == 0), stop=(kk == 1))
                    return last

                def act_tr(par):
                    for kk in range(2):
                        last = tr(bank(7)[:, kk * 128:(kk + 1) * 128], act[par][:, kk * 128:(kk + 1) * 128], ident)
                    return last

                def rows_tr(par):
                    for c in range(DC):
                        last = tr(bank(1, 2)[:, c * 128:(c + 1) * 128], xg[par][:, c * 128:(c + 1) * 128], ident)
                    return last

                def up(w, lhs, s, big=True):
                    pe.wait_ge(m["act_rdy"], w)
                    (up_mm if big else up_small)(lhs, s).then_inc(m["up_ps"], 1)

                def down(w, par, s, big=True):
                    pe.wait_ge(m["actT_ev"], w + 1)
                    pe.wait_ge(m["y_ev"], w)
                    (down_mm if big else down_small)(par, s).then_inc(m["dn_ps"], 1)

                def turn_act(w, par):
                    pe.wait_ge(m["act_rdy"], w + 1)
                    pe.wait_ge(m["actT_ev"], w)
                    act_tr(par).then_inc(m["actT_ps"], 1)

                def turn_rows(u, n_in, par):
                    pe.wait_ge(xg_in[par], n_in + i * 8 * E)
                    pe.wait_ge(xgT_ev, u + i * E)
                    rows_tr(par).then_inc(xgT_ps, 1)

                pe.wait_ge(rw_in, 32 * (i + 1))
                for c in range(DC):
                    last = mm(bank(0)[0:E, :], rw_sb[:, c, :], hM[:, c, :], start=(c == 0), stop=(c == DC - 1))
                last.then_inc(logit_ps, 1)
                for t in range(TT):
                    if t == 0:
                        pe.wait_ge(scoreT_rdy, i + 1)
                    last = tr(bank(3)[:, t * E:(t + 1) * E], scoreT[:, t * 128:(t + 1) * 128], ident[0:E, 0:E])
                last.then_inc(score_ps, 1)
                for t in range(TT):
                    if t >= 2:
                        pe.wait_ge(hrow_sb, t - 1 + i * TT)
                    for c in range(DC):
                        last = tr(bank(1 if t % 2 == 0 else 4, 2)[:, c * 128:(c + 1) * 128], hM[:, c, t * 128:(t + 1) * 128], ident)
                    last.then_inc(hrow_ps, 1)
                if i == 0:
                    for n in range(20, 24):
                        mod_columns(n)
                pe.wait_ge(sh_in, 48 * (i + 1))
                up(0, lambda c: hM[:, c, 0:128], RING - 1)
                pe.wait_ge(chosen_rdy, i + 1)
                for t in range(TT):
                    for s in range(t + 1):
                        last = mm(bank(3)[:, t * E:(t + 1) * E], upper_b[:, :] if s == t else ones_b[:, :],
                                  chosen_b[:, s * E:(s + 1) * E], start=(s == 0), stop=(s == t))
                last.then_inc(pos_ps, 1)
                for t in range(TT):
                    last = mm(bank(0)[0:E, 0:1], chosen_b[:, t * E:(t + 1) * E], ones_b[:, 0:1], start=(t == 0), stop=(t == TT - 1))
                for t in range(TT):
                    last = mm(bank(0)[0:1, 256:256 + E], ones_b[:, 0:1], chosen_b[:, t * E:(t + 1) * E], start=(t == 0), stop=(t == TT - 1))
                last.then_inc(cnt_ps, 1)
                if i == 0:
                    pe.wait_ge(mod_rdy, 3)
                turn_act(0, 0)
                pe.wait_ge(nbx_rdy, i + 1)
                mm(bank(0)[0:E, 8:9], upto_b[:, :], extra_b[:, 0:1], start=True, stop=True)
                mm(bank(3)[:, TT * E:(TT + 1) * E], extra_b[:, :], upper_b[0:E, 0:E], start=True, stop=True).then_inc(end_ps, 1)
                pe.wait_ge(passed_rdy, i + 1)
                mm(bank(0)[0:1, 16:16 + XMAX], ones_b[0:E, 0:1], passed_b[:, :], start=True, stop=True)
                mm(bank(0)[0:1, 128:129], extra_b[:, 0:1], ones_b[0:E, 0:1], start=True, stop=True).then_inc(unit_ps, 1)

                pe.wait_ge(hrow_sb, TT + i * TT)
                for w in range(1, TT):
                    up(w, lambda c, w=w: hM[:, c, w * 128:(w + 1) * 128], RING - 1)
                    down(w - 1, (w - 1) % 2, RING - 1)
                    turn_act(w, w % 2)
                down(TT - 1, 1, RING - 1)
                pe.wait_ge(unit_rdy, i + 1)
                pe.sem_inc(m["t_dn"], 1)
                pe.sem_inc(m["t_xgT_ps"], 1)
                turn_rows(0, 16, 0)
                pe.wait_ge(xgT_ev, 1 + i * E)
                pe.wait_ge(m["w_in"][0], 48)
                either(0, lambda big: up(TT, lambda c: xgT[0][:, c, :], 0, big))
                turn_rows(1, 16, 1)
                turn_act(TT, 0)

                def unit(u, slot, n_w, n_next, par):
                    w = u + TT
                    pe.wait_ge(xgT_ev, u + 1 + i * E)
                    pe.wait_ge(m["w_in"][slot], n_w)
                    either(u, lambda big: up(w, lambda c: xgT[par][:, c, :], slot, big))
                    if n_next is not None:
                        turn_rows(u + 1, n_next, 1 - par)
                    either(u - 1, lambda big: down(w - 1, 1 - par, (slot - 1) % RING, big))
                    turn_act(w, par)

                with nc.tensor.Fori(0, E // 4 - 1) as g:
                    for r in range(4):
                        unit(g * 4 + (1 + r), (1 + r) % 4, g * 48 + 48 * ((1 + r) // 4 + 1), g * 32 + 16 * ((2 + r) // 2 + 1), (1 + r) % 2)
                for u in range(E - 3, E):
                    unit(u, u % 4, 48 * (u // 4 + 1), 16 * ((u + 1) // 2 + 1) if u + 1 < E else None, u % 2)
                either(E - 1, lambda big: down(TT + E - 1, 1, RING - 1, big))
                total = nc.tensor.value_load(unit_i[0:1, XMAX:XMAX + 1], min_val=0, max_val=XMAX)
                with nc.tensor.If(total > 0):
                    with nc.tensor.Fori(0, total) as j:
                        pe.wait_ge(m["t_xg"], j * 16 + 16)
                        rows_tr(0).then_inc(m["t_xgT_ps"], 1)
                        pe.wait_ge(m["t_xgT_ev"], j + 1)
                        pe.wait_ge(m["t_w"], j * 48 + 48)
                        up_mm(lambda c: xgT[0][:, c, :], 0).then_inc(m["t_up"], 1)
                        pe.wait_ge(m["t_act"], j + 1)
                        act_tr(0).then_inc(m["t_actT_ps"], 1)
                        pe.wait_ge(m["t_actT_ev"], j + 1)
                        pe.wait_ge(m["t_yev"], j + 1)
                        pe.wait_ge(m["y_ev"], TT + E)
                        down_mm(0, 0).then_inc(m["t_dn"], 1)
                pe.wait_ge(comb_used, TT * K + i * TT * K)
                for c in range(DC):
                    if c >= 2:
                        pe.wait_ge(res_ev, c - 1 + i * DC)
                    for t in range(TT):
                        last = tr(bank(c % 2)[:, t * 128:(t + 1) * 128], acc[:, t, c * 128:(c + 1) * 128], ident)
                    last.then_inc(acc_ps, 1)
                    if c:
                        mean((J_MIX1, J_FIN)[i], c - 1)
                mean((J_MIX1, J_FIN)[i], DC - 1)

            mean(J_FFN0, DC - 1)
            for n in range(20, 24):
                mod_chunk(n)
            for n in range(12, 20):
                mod_columns(n)
            pe.wait_ge(nrm_out, 8 * (J_FFN0 + 1))
            moe(0)
            pe.wait_ge(nrm_out, 8 * (J_MIX1 + 1))
            pe.wait_ge(pw_in, 16)

            for c in range(DC):
                if c >= 2:
                    pe.wait_ge(u_rdy, c - 1)
                for half in range(2):
                    for kk in range(DC):
                        last = mm(bank(2 * (c % 2) + half), pw1_sb[:, kk, half * D + c * 128:half * D + (c + 1) * 128], hM[:, kk, :],
                                  start=(kk == 0), stop=(kk == DC - 1))
                last.then_inc(glu_ps, 1)
            for c in range(DC):
                pe.wait_ge(cv_rdy, c + 1)
                last = mm(bank(6), mean_w[:, :], conv[:, c, :], start=(c == 0), stop=(c == DC - 1))
            last.then_inc(mean_ps, 1)
            norm(J_LN)
            pe.wait_ge(nrm_out, 8 * (J_LN + 1))
            pe.wait_ge(pw2_in, 16)
            for n in range(DC):
                if n >= 2:
                    pe.wait_ge(pw2_ev, n - 1)
                for c in range(DC):
                    last = mm(bank(n % 2), pw2_sb[:, c, n * 128:(n + 1) * 128], hM[:, c, :], start=(c == 0), stop=(c == DC - 1))
                last.then_inc(pw2_ps, 1)
                if n:
                    mean(J_FFN1, n - 1)
            mean(J_FFN1, DC - 1)
            pe.wait_ge(nrm_out, 8 * (J_FFN1 + 1))
            moe(1)

        @block.vector
        def _(dve):
            V = nc.vector
            step = [0]

            def link(ins, behind=0):
                step[0] += 1
                ins.then_inc(dve_step, 1)
                dve.wait_ge(dve_step, step[0] - behind)

            V.memset(cs[:, :, :], 0.0)
            V.memset(eps[:, :], EPS)
            V.memset(zrow[:, :], 0.0)
            V.memset(zero[:, :], 0.0).then_inc(dve_cst, 1)

            def mod_out(i, columns, b, p0, p1, gains):
                dve.wait_ge(modcol_ps, columns)
                for w in range(2):
                    last = V.tensor_tensor(mod[i][:, p0:p1, :, w].rearrange("p s c -> p (s c)"),
                                           bank(b)[:, 2 * DC * p0 + w:2 * DC * p1:2],
                                           v("modb", 48 * i + DC * p0, 48 * i + DC * p1), ALU.add)
                link(last)
                for n, g in gains:
                    for w in range(2):
                        last = V.scalar_tensor_tensor(modA[i][:, n, :, w], mod[i][:, 3 * n + 1, :, w], 1.0,
                                                      v(g, DC * i, DC * i + DC), ALU.add, ALU.mult)
                last.then_inc(mod_rdy, 1)

            def norm(j):
                src, dst, w, sc, sh, fn = JOBS[j]
                dve.wait_ge(std_rdy, j + 1)
                V.reciprocal(rs[:, 0:w], rs[:, 0:w]).then_inc(rs_rdy, 1)
                dve.wait_ge(rs_rdy, j + 1)
                for c in range(DC):
                    V.tensor_tensor(dst(c), src(c), rs[:, 0:w], ALU.mult).then_inc(nrm_mul, 1)

            dve.wait_ge(cst_in, 32)
            dve.wait_ge(x_in, 32)
            norm(J_CTX)
            norm(J_X)
            mod_out(0, 4, COL_BANK[0], 0, 2, [(0, "nmix")])
            dve.wait_ge(nrm_out, 16)
            dve.wait_ge(a_ps, 3)
            for a_ in range(2):
                for b_ in range(2):
                    last = V.tensor_copy(kT[a_][b_][64:96, 0:C], bank(4 + 2)[0:ROPE, 0:C])
            last.then_inc(a_pe, 1)
            rope_x = bank(4 + 5 % 4)
            dve.wait_ge(a_ps, 6)
            turned = [kT[0][n][:, 0:T] for n in range(2)]
            V.tensor_tensor(turned[0][0:32, :], rope_x[0:32, :], k("rope")[0:32, :], ALU.mult)
            link(V.tensor_tensor(turned[1][0:32, :], rope_x[32:64, :], k("rope")[32:64, :], ALU.mult))
            for a_ in range(2):
                for b_ in range(2):
                    last = V.tensor_tensor(kT[a_][b_][64:96, C:KEYS], turned[0][0:32, :], turned[1][0:32, :], ALU.add)
            last.then_inc(a_pe, 1)
            for J, (b, w, gs, lat, gain) in enumerate(LAT):
                dve.wait_ge(lstd_rdy, J + 1)
                V.reciprocal(rs[:, 0:w], rs[:, 0:w]).then_inc(lrs_rdy, 1)
                dve.wait_ge(lrs_rdy, J + 1)
                for j in range(len(gs)):
                    V.scalar_tensor_tensor(lat(j), lat(j), v(gain, j, j + 1), rs[:, 0:w], ALU.mult, ALU.mult).then_inc(lat_rdy, 1)

            dve.wait_ge(lat_rdy, 8)

            def q_out(m, q):
                b = bank(7 if q == 0 else 6)
                dve.wait_ge(pj_ps, 6 * m + 3 + q)
                dve.wait_ge(q_ev, 2 * m + q)
                dst = qT[m % 2][q]
                V.tensor_copy(dst[0:64, :], b[0:64, :])
                V.tensor_tensor(rope_t[0][64:96, :], b[64:96, :], k("rope")[64:96, :], ALU.mult)
                V.tensor_tensor(rope_t[1][64:96, :], b[96:128, :], k("rope")[96:128, :], ALU.mult).then_inc(q_rope, 1)
                dve.wait_ge(q_rope, 2 * m + q + 1)
                V.tensor_tensor(dst[64:96, :], rope_t[0][64:96, :], rope_t[1][64:96, :], ALU.add).then_inc(q_ev, 1)

            q_out(0, 0)
            q_out(0, 1)
            mod_out(0, 12, COL_BANK[4], 2, 6, [(1, "nffn")])

            def top_score(n):
                dve.wait_ge(s_ps, n + 1)
                if n >= 4:
                    dve.wait_ge(p_rdy, n - 3)
                V.tensor_reduce(smx[:, n % 4, 0:1], bank(2 * (n % 2), 2)[:, 0:KEYS], AX.X, ALU.max).then_inc(max_rdy, 1)
                dve.wait_ge(max_rdy, n + 1)
                V.tensor_scalar(smx[:, n % 4, 1:2], smx[:, n % 4, 0:1], -SM_SCALE, None, ALU.mult).then_inc(nmax_rdy, 1)

            def divide(n):
                dve.wait_ge(exp_rdy, n + 1)
                V.reciprocal(smx[:, n % 4, 0:1], smx[:, n % 4, 2:3]).then_inc(den_rdy, 1)
                dve.wait_ge(den_rdy, n + 1)
                V.tensor_scalar(P[n % 2], P[n % 2], smx[:, n % 4, 0:1], None, ALU.mult).then_inc(p_rdy, 1)

            top_score(0)
            for n in range(NS):
                m, i8 = n // 8, n % 8
                divide(n)
                if n + 1 < NS:
                    top_score(n + 1)
                if m + 1 < NPAIR and i8 in (3, 4):
                    q_out(m + 1, i8 - 3)
                if i8 == 0 and m:
                    dve.wait_ge(o_ps, m)
                    V.tensor_copy(oT[:, m - 1, :], bank(6)).then_inc(o_ev, 1)
                pT_copy(dve, V.tensor_copy, n, False)
            dve.wait_ge(mod_rdy, 2)
            dve.wait_ge(o_ps, NPAIR)
            V.tensor_copy(oT[:, NPAIR - 1, :], bank(6)).then_inc(o_ev, 1)
            for n in range(DC):
                dve.wait_ge(wo_ps, n + 1)
                V.scalar_tensor_tensor(xT[:, n, :], bank(n % 2), mod[0][:, 2, n, 0:1], xT[:, n, :], ALU.mult, ALU.add).then_inc(wo_ev, 1)
            dve.wait_ge(wo_ev, DC)
            norm(J_FFN0)

            def moe(i):
                m = M[i]
                TE = TT * E
                te = lambda ap: ap.rearrange("p (t e) -> p t e", t=TT)

                def product(w, b, par, big=True):
                    dve.wait_ge(m["gate_rdy"], w + 1)
                    if b:
                        dve.wait_ge(m["actT_ps"], w - 1)
                    if big:
                        V.tensor_tensor(act[par], gate[par], bank(6)[:, F:2 * F], ALU.mult).then_inc(m["act_rdy"], 1)
                    else:
                        V.tensor_tensor(act[par][0:64], gate[par][64:128], bank(6)[64:128, 0:F], ALU.mult).then_inc(m["act_rdy"], 1)

                def rows_out(u, par, w):
                    dve.wait_ge(xgT_ps, u + 1 + i * E)
                    dve.wait_ge(m["up_ps"], w)
                    V.tensor_copy(xgT[par].rearrange("p c t -> p (c t)"), bank(1, 2)).then_inc(xgT_ev, 1)

                def act_out(w, b, par):
                    dve.wait_ge(m["actT_ps"], w + 1)
                    if b:
                        dve.wait_ge(m["dn_ps"], w - 1)
                    V.tensor_copy(actT[par].rearrange("p k t -> p (k t)"), bank(7)[:, 0:F]).then_inc(m["actT_ev"], 1)

                dve.wait_ge(score_ps, i + 1)
                link(V.tensor_copy(score, bank(3)[:, 0:TE]))
                dve.wait_ge(rw_in, 32 * (i + 1))
                link(V.tensor_tensor(te(select), te(score), bias_sb[:, :].unsqueeze(1).to_broadcast([128, TT, E]), ALU.add))
                for n in range(TT * G):
                    last = V.max(gtop[:, 8 * n:8 * n + 8], select[:, 8 * n:8 * n + 8])
                link(last)
                link(V.tensor_tensor(gsum, gtop[:, 0:8 * TT * G:8], gtop[:, 1:8 * TT * G:8], ALU.add))
                gs3 = gsum.rearrange("p (t g) -> p t g", t=TT)
                one = gs3.unsqueeze(3).to_broadcast([128, TT, G, G])
                other = gs3.unsqueeze(2).to_broadcast([128, TT, G, G])
                g4 = lambda ap: ap.rearrange("p (t g h) -> p t g h", t=TT, g=G)
                V.tensor_tensor(g4(cmpa), other, one, ALU.is_gt)
                link(V.tensor_tensor(g4(cmpb), other, one, ALU.is_equal))
                link(V.tensor_tensor(cmpb.rearrange("p (t x) -> p t x", t=TT), cmpb.rearrange("p (t x) -> p t x", t=TT),
                                     k("before").unsqueeze(1).to_broadcast([128, TT, G * G]), ALU.mult))
                link(V.tensor_tensor(cmpa, cmpa, cmpb, ALU.add))
                link(V.tensor_reduce(rank, cmpa.rearrange("p (n h) -> p n h", h=G), AX.X, ALU.add))
                link(V.tensor_scalar(rank, rank, TOPG - 0.5, -3e38, ALU.is_gt, ALU.mult))
                link(V.tensor_tensor(select.rearrange("p (n e) -> p n e", e=G), select.rearrange("p (n e) -> p n e", e=G),
                                     rank.unsqueeze(2).to_broadcast([128, TT * G, G]), ALU.add))
                for t in range(TT):
                    last = V.max(top[:, 8 * t:8 * t + 8], select[:, t * E:(t + 1) * E])
                link(last)
                for t in range(TT):
                    last = V.max_index(topu[:, 8 * t:8 * t + 8], top[:, 8 * t:8 * t + 8], select[:, t * E:(t + 1) * E])
                link(last)
                link(V.tensor_copy(topi, topu[:, :]))
                hot4 = hot.rearrange("p (k t e) -> p k t e", k=K, t=TT)
                for q in range(K):
                    last = V.tensor_tensor(hot4[:, q], k("iota").unsqueeze(1).to_broadcast([128, TT, E]),
                                           topi[:, q:8 * TT:8].unsqueeze(2).to_broadcast([128, TT, E]), ALU.is_equal)
                link(last)
                link(V.tensor_reduce(cmpb, hot.rearrange("p (k x) -> p x k", k=K), AX.X, ALU.add))
                V.tensor_copy(chosen_b[:, :], cmpb).then_inc(chosen_rdy, 1)
                if i == 0:
                    mod_out(1, 24, COL_BANK[12], 0, 6, [(0, "nmix"), (1, "nffn")])
                product(0, 0, 0)
                hot3, prod3 = hot.rearrange("p (k x) -> p k x", k=K), prod.rearrange("p (k x) -> p k x", k=K)
                dve.wait_ge(cnt_ps, i + 1)
                for n in range(BLOCKS - 1):
                    last = V.tensor_scalar(nbx[0:E, n:n + 1], bank(0)[0:E, 0:1], 128.0 * (n + 1), None, ALU.is_gt)
                link(last)
                V.tensor_scalar(big_i[0:1, :], bank(0)[0:1, 256:256 + E], 64.5, None, ALU.is_gt)
                link(V.tensor_reduce(nbx[0:E, 3:4], nbx[0:E, 0:3], AX.X, ALU.add))
                V.tensor_copy(extra_b[:, :], nbx[0:E, 3:4].to_broadcast([E, 128])).then_inc(nbx_rdy, 1)
                dve.wait_ge(end_ps, i + 1)
                link(V.tensor_copy(nbx[0:E, 0:1], bank(0)[0:E, 8:9]))
                V.tensor_scalar(passed_b[:, :], k("iota")[0:E, 0:XMAX], nbx[0:E, 0:1], None, ALU.is_ge).then_inc(passed_rdy, 1)
                bc = lambda ap: ap.unsqueeze(1).to_broadcast([128, TT, E])
                V.scalar_tensor_tensor(te(cmpa), te(bank(3)[:, 0:TE]), float(E), bc(k("iota")), ALU.mult, ALU.add)
                link(V.tensor_scalar(xrow, bank(3)[:, TE:TE + E], 128.0, 128.0 * (E - 1), ALU.mult, ALU.add))
                V.tensor_scalar(gtop, bank(3)[:, 0:TE], 127.5, None, ALU.is_gt)
                link(V.tensor_tensor(te(select), te(bank(3)[:, 0:TE]), bc(xrow), ALU.add))
                link(V.tensor_tensor(select, select, cmpa, ALU.subtract))
                link(V.tensor_tensor(select, select, gtop, ALU.mult))
                link(V.tensor_tensor(cmpa, cmpa, select, ALU.add))
                link(V.tensor_tensor(prod3, hot3, cmpa.unsqueeze(1).to_broadcast([128, K, TE]), ALU.mult))
                link(V.tensor_reduce(gtop[:, 0:K * TT], prod.rearrange("p (n e) -> p n e", e=E), AX.X, ALU.add))
                V.tensor_copy(row_i[:, :], gtop[:, 0:K * TT]).then_inc(rows_rdy, 1)
                dve.wait_ge(unit_ps, i + 1)
                V.tensor_scalar(unit_i[0:1, 0:XMAX], bank(0)[0:1, 16:16 + XMAX], float(E - 1), None, ALU.min)
                V.tensor_copy(unit_i[0:1, XMAX:XMAX + 1], bank(0)[0:1, 128:129]).then_inc(unit_rdy, 1)

                def either(u, emit):
                    flag = nc.vector.value_load(big_i[0:1, ds(u, 1)], min_val=0, max_val=1)
                    with nc.vector.If(flag > 0):
                        emit(True)
                    with nc.vector.Else():
                        emit(False)

                act_out(0, 0, 0)
                link(V.tensor_tensor(prod3, hot3, score.unsqueeze(1).to_broadcast([128, K, TE]), ALU.mult))
                link(V.tensor_reduce(wk, prod.rearrange("p (n e) -> p n e", e=E), AX.X, ALU.add))
                link(V.tensor_reduce(wsum, wk.rearrange("p (k t) -> p t k", k=K), AX.X, ALU.add))
                link(V.reciprocal(wsum, wsum))
                link(V.scalar_tensor_tensor(wk.rearrange("p (k t) -> p k t", k=K), wk.rearrange("p (k t) -> p k t", k=K), ROUTED,
                                            wsum.unsqueeze(1).to_broadcast([128, K, TT]), ALU.mult, ALU.mult))
                dve.wait_ge(m["actT_ev"], 1)
                for w in range(1, TT):
                    product(w, w >= 2, w % 2)
                    act_out(w, w >= 2, w % 2)
                rows_out(0, 0, 0)
                either(0, lambda big: product(TT, 1, 0, big))
                rows_out(1, 1, 0)
                act_out(TT, 1, 0)
                with nc.vector.Fori(0, E // 4 - 1) as g:
                    for r in range(4):
                        w = g * 4 + (TT + 1 + r)
                        either(g * 4 + (1 + r), lambda big: product(w, 1, (1 + r) % 2, big))
                        rows_out(g * 4 + (2 + r), r % 2, g * 4 + (TT + 1 + r))
                        act_out(w, 1, (1 + r) % 2)
                for u in range(E - 3, E):
                    either(u, lambda big: product(TT + u, 1, u % 2, big))
                    if u + 1 < E:
                        rows_out(u + 1, (u + 1) % 2, TT + u)
                    act_out(TT + u, 1, u % 2)
                total = nc.vector.value_load(unit_i[0:1, XMAX:XMAX + 1], min_val=0, max_val=XMAX)
                with nc.vector.If(total > 0):
                    dve.wait_ge(m["up_ps"], TT + E - 1)
                    with nc.vector.Fori(0, total) as j:
                        dve.wait_ge(m["t_xgT_ps"], j + 2)
                        V.tensor_copy(xgT[0].rearrange("p c t -> p (c t)"), bank(1, 2)).then_inc(m["t_xgT_ev"], 1)
                        dve.wait_ge(m["t_gate"], j + 1)
                        V.tensor_tensor(act[0], gate[0], bank(6)[:, F:2 * F], ALU.mult).then_inc(m["t_act"], 1)
                        dve.wait_ge(m["t_actT_ps"], j + 1)
                        V.tensor_copy(actT[0].rearrange("p k t -> p (k t)"), bank(7)[:, 0:F]).then_inc(m["t_actT_ev"], 1)
                dve.wait_ge(m["y_ev"], TT)
                for n in range(TT * K):
                    t, q = n // K, n % K
                    dve.wait_ge(comb_in[n % 6], 16 * (n // 6 + 1 + i * TT * K // 6))
                    if n:
                        dve.wait_ge(comb_used, n + i * TT * K)
                    V.scalar_tensor_tensor(acc[:, t, :], comb[n % 6], wk[:, q * TT + t:q * TT + t + 1], acc[:, t, :],
                                           ALU.mult, ALU.add).then_inc(comb_used, 1)
                for c in range(DC):
                    dve.wait_ge(acc_ps, c + 1 + i * DC)
                    V.scalar_tensor_tensor(xT[:, c, :], bank(c % 2), mod[i][:, 5, c, 0:1], xT[:, c, :], ALU.mult, ALU.add)\
                        .then_inc(res_ev, 1)
                dve.wait_ge(res_ev, DC + i * DC)

            moe(0)
            norm(J_MIX1)
            for n in range(2):
                V.memset(up[n][:, 0:PAD], 0.0)
                V.memset(up[n][:, PAD + T:PT_], 0.0).then_inc(pad_rdy, 1)
            dve.wait_ge(pad_rdy, 2)
            def glu_out(c):
                dve.wait_ge(sig_rdy, c + 1)
                if c >= 2:
                    dve.wait_ge(side_mul, SIDE_TAPS * (c - 1))
                V.scalar_tensor_tensor(up[c % 2][:, PAD:PAD + T], bank(2 * (c % 2)), v("pw1b", c, c + 1), sg[c % 2],
                                       ALU.add, ALU.mult).then_inc(u_rdy, 1)

            glu_out(0)
            for c in range(DC):
                dve.wait_ge(u_rdy, c + 1)
                tap = lambda q: v("dww", c * TAPS + q, c * TAPS + q + 1)
                link(V.tensor_scalar(conv[:, c, :], up[c % 2][:, 0:T], tap(0), v("dwb", c, c + 1), ALU.mult, ALU.add), 1)
                link(V.tensor_scalar(tmp[c % 2], up[c % 2][:, 1:1 + T], tap(1), None, ALU.mult), 1)
                for q in range(2, TAPS - SIDE_TAPS):
                    part = (conv[:, c, :], tmp[c % 2])[q % 2]
                    link(V.scalar_tensor_tensor(part, up[c % 2][:, q:q + T], tap(q), part, ALU.mult, ALU.add),
                         1 if q < TAPS - SIDE_TAPS - 1 else 0)
                link(V.tensor_tensor(conv[:, c, :], conv[:, c, :], tmp[c % 2], ALU.add))
                if c + 1 < DC:
                    glu_out(c + 1)
                dve.wait_ge(side_add, (SIDE_TAPS - 1) * (c + 1))
                V.tensor_tensor(conv[:, c, :], conv[:, c, :], side[c % 2], ALU.add).then_inc(cv_rdy, 1)
            dve.wait_ge(mean_ps, 1)
            dve.wait_ge(cv_rdy, DC)
            for c in range(DC):
                V.tensor_tensor(conv[:, c, :], conv[:, c, :], bank(6), ALU.subtract).then_inc(cent_rdy, 1)
            dve.wait_ge(cent_rdy, DC)
            norm(J_LN)
            for c in range(DC):
                dve.wait_ge(pw2_ps, c + 1)
                link(V.tensor_scalar(tmp[c % 2], bank(c % 2), v("pw2b", c, c + 1), mod[1][:, 2, c, 0:1], ALU.add, ALU.mult))
                V.tensor_tensor(xT[:, c, :], xT[:, c, :], tmp[c % 2], ALU.add).then_inc(pw2_ev, 1)
            dve.wait_ge(pw2_ev, DC)
            norm(J_FFN1)
            moe(1)
            norm(J_FIN)


def constants():
    c = np.zeros((128, NCST), np.float32)
    p = np.arange(128)

    def put(name, a):
        lo, hi = CST[name]
        c[:a.shape[0], lo:hi] = a

    put("ident", np.eye(128))
    put("sel", (p[:, None] % 32 == np.arange(2)[None]).astype(np.float32))
    put("iota", np.tile(np.arange(E), (128, 1)))
    put("before", np.tile((np.arange(G)[None, :] < np.arange(G)[:, None]).reshape(1, -1), (128, 1)))
    put("upper", (p[:, None] < p[None, :]))
    put("upto", (np.arange(E)[:, None] <= np.arange(E)[None, :]))
    put("tok", p[:, None] + 128 * np.arange(TT)[None])
    tok = np.arange(T, dtype=np.float32)
    row, col = np.floor(tok / 64), tok % 64
    inv = (np.float32(10000.0) ** (-np.arange(0, 16, 2, dtype=np.float32) / np.float32(16))).astype(np.float32)
    ang = np.concatenate([row[:, None] * inv, row[:, None] * inv, col[:, None] * inv, col[:, None] * inv], -1).T
    sign = np.where(np.arange(ROPE) % 16 < 8, -1.0, 1.0)[:, None]
    cos, sin = np.cos(ang.astype(np.float32)), np.sin(ang.astype(np.float32)) * sign
    put("rope", np.concatenate([cos, sin, cos, sin]))
    return c


SWAP = np.arange(ROPE) ^ 8


def kernel(**inputs):
    import concourse.bacc as _bacc
    from concourse import mybir as _mybir
    from concourse.bass_utils import run_bass_kernel_spmd as _run

    a = {n: np.asarray(x) for n, x in inputs.items()}

    def cols(x):
        return x.reshape(-1, 128).T

    def feats(x):
        return np.ascontiguousarray(x.T.reshape(DC, 128, -1).transpose(1, 0, 2))

    vec = np.concatenate([
        np.stack([cols(a["c"][0]), cols(a["c_ctx"])], -1).reshape(128, -1),
        cols(a["mod_b"][0]), cols(a["mod_b"][1]), cols(a["norm_mix_w"].reshape(-1)), cols(a["norm_ffn_w"].reshape(-1)),
        cols(a["mla_q_norm"][0]), cols(a["mla_kv_norm"][0]), cols(a["conv_pw1_b"][0]), cols(a["conv_dw_b"][0]),
        cols(a["conv_norm_w"][0]), cols(a["conv_norm_b"][0]), cols(a["conv_pw2_b"][0]), cols(a["final_norm_w"]),
        a["conv_dw_w"][0].T.reshape(DC, 128, TAPS).transpose(1, 0, 2).reshape(128, -1)], axis=1)
    wq_b = a["mla_wq_b"][0].reshape(QL, H, NOPE + ROPE)
    wq_b = np.concatenate([wq_b, wq_b[:, :, NOPE + SWAP]], axis=2).reshape(QL, H * 128)
    wkv_a = a["mla_wkv_a"][0]
    wkv_a = np.concatenate([wkv_a, wkv_a[:, KVL + SWAP]], axis=1)
    wkv_b = a["mla_wkv_b"][0].reshape(KVL, H // 2, 2, 2, NOPE).transpose(0, 1, 3, 2, 4).reshape(KVL, -1)
    ins = [feats(a["x"][0]), feats(a["ctx"][0]), vec, constants(), a["mod_w"], a["mla_wq_a"][0], wq_b, wkv_a, wkv_b,
           a["mla_wo"][0], a["conv_pw1_w"][0], a["conv_pw2_w"][0], a["router_w"], a["router_bias"], a["exp_w1"], a["exp_w3"],
           a["exp_w2"], a["shared_w1"], a["shared_w3"], a["shared_w2"]]
    nc = _bacc.Bacc("TRN2", target_bir_lowering=False, num_devices=1)
    arrays, args = {}, []
    for n, x in enumerate(ins):
        x = np.ascontiguousarray(x)
        arrays[f"in_{n}"] = x
        args.append(nc.dram_tensor(f"in_{n}", x.shape, _mybir.dt.from_np(x.dtype), kind="ExternalInput").ap())
    args.append(nc.dram_tensor("out_0", (128, DC, T), _mybir.dt.float32, kind="ExternalOutput").ap())
    build(nc, *args)
    r = _run(nc, [arrays], core_ids=[0])
    y = r.results[0]["out_0"]
    return np.ascontiguousarray(y.transpose(1, 0, 2).reshape(D, T).T).reshape(1, T, D)
```
